# Optimizing a Trainium2 kernel written in Bass

```python
import jax, jax.numpy as jnp
from jax import lax
import numpy as np

D_MODEL = 1024
BATCH = 1
SEQ = 512
DEPTH = 1

CHUNK = 64
Q_BLOCK = 128
EPS = 1e-6

GLA_HEADS = 4
GLA_DK = D_MODEL // 2 // GLA_HEADS
GLA_DV = D_MODEL // GLA_HEADS
GLA_GATE_RANK = 16
GLA_GATE_TEMP = 16.0

DSA_HEADS = 8
DSA_HEAD_DIM = 128
IDX_HEADS = 8
IDX_DIM = 64
TOPK_MAX = 256

N_GROUPS = 4
EXPERTS_PER_GROUP = 8
N_EXPERTS = N_GROUPS * EXPERTS_PER_GROUP
TOP_K_EXPERTS = 2
EXPERT_HIDDEN = D_MODEL // 2

GLA_QK_W = GLA_HEADS * GLA_DK
GLA_V_W = GLA_HEADS * GLA_DV
DSA_W = DSA_HEADS * DSA_HEAD_DIM
IN_SPLITS = (GLA_QK_W, GLA_QK_W, GLA_V_W, GLA_GATE_RANK, GLA_V_W,
             DSA_W, DSA_W, DSA_W, IDX_HEADS * IDX_DIM, IDX_DIM, IDX_HEADS,
             D_MODEL, D_MODEL)
IN_WIDTH = sum(IN_SPLITS)

kernel_name = "hybrid_gla_dsa_hiermoe_block"

def rms_norm(x, g):
    xf = x.astype(jnp.float32)
    y = xf * lax.rsqrt(jnp.mean(xf * xf, axis=-1, keepdims=True) + EPS)
    return y * g.astype(jnp.float32)

def layer_norm(x, g, b):
    xf = x.astype(jnp.float32)
    mu = jnp.mean(xf, axis=-1, keepdims=True)
    var = jnp.mean(jnp.square(xf - mu), axis=-1, keepdims=True)
    return (xf - mu) * lax.rsqrt(var + EPS) * g.astype(jnp.float32) + b.astype(jnp.float32)

def split_cols(z):
    offsets = [int(o) for o in np.cumsum(IN_SPLITS)[:-1]]
    return jnp.split(z, offsets, axis=-1)

def gla_branch(q, k, v, a_lr, r, w_a2, b_a, norm_g):
    B, S, _ = q.shape
    nc = S // CHUNK
    f32 = jnp.float32
    q = q.astype(f32).reshape(B, nc, CHUNK, GLA_HEADS, GLA_DK) * (GLA_DK ** -0.5)
    k = k.astype(f32).reshape(B, nc, CHUNK, GLA_HEADS, GLA_DK)
    v = v.astype(f32).reshape(B, nc, CHUNK, GLA_HEADS, GLA_DV)
    log_a = jax.nn.log_sigmoid((a_lr @ w_a2 + b_a).astype(f32)) / GLA_GATE_TEMP
    log_a = log_a.reshape(B, nc, CHUNK, GLA_HEADS, GLA_DK)
    cum = jnp.cumsum(log_a, axis=2)
    cum_end = cum[:, :, -1:]
    k_dec = k * jnp.exp(cum_end - cum)
    chunk_decay = jnp.exp(cum_end[:, :, 0])
    xs = (jnp.moveaxis(q, 1, 0), jnp.moveaxis(k_dec, 1, 0),
          jnp.moveaxis(v, 1, 0), jnp.moveaxis(chunk_decay, 1, 0))

    def step(state, inp):
        qc, kc, vc, dc = inp
        state = dc[..., None] * state + jnp.einsum('bchk,bchv->bhkv', kc, vc)
        out = jnp.einsum('bchk,bhkv->bchv', qc, state)
        return state, out

    s0 = jnp.zeros((B, GLA_HEADS, GLA_DK, GLA_DV), f32)
    _, o = lax.scan(step, s0, xs)
    o = jnp.moveaxis(o, 0, 1).reshape(B, S, GLA_HEADS, GLA_DV)
    o = rms_norm(o, norm_g)
    o = o * jax.nn.silu(r.astype(f32).reshape(B, S, GLA_HEADS, GLA_DV))
    return o.reshape(B, S, GLA_V_W)

def dsa_branch(q, k, v, qi, ki, wi, q_norm_g, k_norm_g, ln_g, ln_b):
    B, S, _ = q.shape
    f32 = jnp.float32
    topk = min(TOPK_MAX, S // 4)
    nb = S // Q_BLOCK
    q = rms_norm(q.reshape(B, S, DSA_HEADS, DSA_HEAD_DIM), q_norm_g)
    k = rms_norm(k.reshape(B, S, DSA_HEADS, DSA_HEAD_DIM), k_norm_g)
    v = v.astype(f32).reshape(B, S, DSA_HEADS, DSA_HEAD_DIM)
    qi = qi.astype(f32).reshape(B, S, IDX_HEADS, IDX_DIM)
    ki = layer_norm(ki, ln_g, ln_b)
    wi = wi.astype(f32) * (IDX_HEADS ** -0.5)
    key_chunk = jnp.arange(S) // CHUNK
    gather = jax.vmap(lambda arr, ids: arr[ids])

    def block(i):
        start = i * Q_BLOCK
        qb = lax.dynamic_slice_in_dim(q, start, Q_BLOCK, axis=1)
        qib = lax.dynamic_slice_in_dim(qi, start, Q_BLOCK, axis=1)
        wib = lax.dynamic_slice_in_dim(wi, start, Q_BLOCK, axis=1)
        q_chunk = (start + jnp.arange(Q_BLOCK)) // CHUNK
        admissible = key_chunk[None, :] <= q_chunk[:, None]
        idx_logits = jnp.einsum('bqhd,bsd->bqhs', qib, ki) * (IDX_DIM ** -0.5)
        score = jnp.einsum('bqh,bqhs->bqs', wib, jax.nn.relu(idx_logits))
        score = jnp.where(admissible[None], score, -jnp.inf)
        top_val, top_idx = lax.top_k(score, topk)
        valid = jnp.isfinite(top_val)
        k_sel = gather(k, top_idx)
        v_sel = gather(v, top_idx)
        logits = jnp.einsum('bqhd,bqkhd->bqhk', qb, k_sel) * (DSA_HEAD_DIM ** -0.5)
        logits = jnp.where(valid[:, :, None, :], logits, -jnp.inf)
        p = jax.nn.softmax(logits, axis=-1)
        return jnp.einsum('bqhk,bqkhd->bqhd', p, v_sel)

    o = lax.map(block, jnp.arange(nb))
    return jnp.moveaxis(o, 0, 1).reshape(B, S, DSA_W)

def hier_moe(h, w_rg, b_rg, w_re, b_re, w_gate, w_up, w_down):
    B, S, D = h.shape
    f32 = jnp.float32
    t = h.reshape(B * S, D)
    g_prob = jax.nn.softmax((t @ w_rg + b_rg).astype(f32), axis=-1)
    g_idx = jnp.argmax(g_prob, axis=-1)
    g_w = jnp.take_along_axis(g_prob, g_idx[:, None], axis=1)
    e_logits = (t @ w_re + b_re).astype(f32).reshape(B * S, N_GROUPS, EXPERTS_PER_GROUP)
    e_logits = jnp.take_along_axis(e_logits, g_idx[:, None, None], axis=1)[:, 0]
    e_prob = jax.nn.softmax(e_logits, axis=-1)
    top_p, top_e = lax.top_k(e_prob, TOP_K_EXPERTS)
    top_w = g_w * top_p / jnp.sum(top_p, axis=-1, keepdims=True)
    expert_ids = g_idx[:, None] * EXPERTS_PER_GROUP + top_e
    gates = jnp.einsum('tk,tke->te', top_w,
                       jax.nn.one_hot(expert_ids, N_EXPERTS, dtype=f32))
    y = jnp.zeros((B * S, D), f32)
    for e in range(N_EXPERTS):
        hid = jax.nn.silu(t @ w_gate[e]) * (t @ w_up[e])
        y = y + gates[:, e:e + 1] * (hid @ w_down[e]).astype(f32)
    return y.reshape(B, S, D)

def setup_inputs(seed: int = 0) -> dict:
    key = jax.random.key(seed)
    ks = jax.random.split(key, 24)
    f32 = jnp.float32
    L, D, F = DEPTH, D_MODEL, EXPERT_HIDDEN

    def nrm(k, shape, scale):
        return jax.random.normal(k, shape, f32) * scale

    return {
        "x": nrm(ks[0], (BATCH, SEQ, D), 1.0),
        "norm1_g": 1.0 + nrm(ks[1], (L, D), 0.05),
        "w_in": nrm(ks[2], (L, D, IN_WIDTH), D ** -0.5),
        "gla_w_a2": nrm(ks[3], (L, GLA_GATE_RANK, GLA_QK_W), GLA_GATE_RANK ** -0.5),
        "gla_b_a": nrm(ks[4], (L, GLA_QK_W), 0.02),
        "gla_norm_g": 1.0 + nrm(ks[5], (L, GLA_DV), 0.05),
        "dsa_q_norm_g": 1.0 + nrm(ks[6], (L, DSA_HEAD_DIM), 0.05),
        "dsa_k_norm_g": 1.0 + nrm(ks[7], (L, DSA_HEAD_DIM), 0.05),
        "idx_k_ln_g": 1.0 + nrm(ks[8], (L, IDX_DIM), 0.05),
        "idx_k_ln_b": nrm(ks[9], (L, IDX_DIM), 0.02),
        "w_branch_gla": nrm(ks[10], (L, GLA_V_W, D), GLA_V_W ** -0.5),
        "w_branch_dsa": nrm(ks[11], (L, DSA_W, D), DSA_W ** -0.5),
        "w_out": nrm(ks[12], (L, D, D), D ** -0.5),
        "norm2_g": 1.0 + nrm(ks[13], (L, D), 0.05),
        "w_router_group": nrm(ks[14], (L, D, N_GROUPS), D ** -0.5),
        "b_router_group": nrm(ks[15], (L, N_GROUPS), 0.01),
        "w_router_expert": nrm(ks[16], (L, D, N_EXPERTS), D ** -0.5),
        "b_router_expert": nrm(ks[17], (L, N_EXPERTS), 0.01),
        "w_exp_gate": nrm(ks[18], (L, N_EXPERTS, D, F), D ** -0.5),
        "w_exp_up": nrm(ks[19], (L, N_EXPERTS, D, F), D ** -0.5),
        "w_exp_down": nrm(ks[20], (L, N_EXPERTS, F, D), F ** -0.5),
    }

def reference(x, norm1_g, w_in, gla_w_a2, gla_b_a, gla_norm_g, dsa_q_norm_g, dsa_k_norm_g,
              idx_k_ln_g, idx_k_ln_b, w_branch_gla, w_branch_dsa, w_out, norm2_g,
              w_router_group, b_router_group, w_router_expert, b_router_expert,
              w_exp_gate, w_exp_up, w_exp_down):
    dt = x.dtype
    for l in range(DEPTH):
        h = rms_norm(x, norm1_g[l]).astype(dt)
        z = h @ w_in[l]
        (gq, gk, gv, ga, gr, dq, dk, dv, iq, ik, iw, gate_a, gate_b) = split_cols(z)
        o_gla = gla_branch(gq, gk, gv, ga, gr, gla_w_a2[l], gla_b_a[l], gla_norm_g[l]).astype(dt)
        o_dsa = dsa_branch(dq, dk, dv, iq, ik, iw, dsa_q_norm_g[l], dsa_k_norm_g[l],
                           idx_k_ln_g[l], idx_k_ln_b[l]).astype(dt)
        mix = (jax.nn.sigmoid(gate_a) * (o_gla @ w_branch_gla[l])
               + jax.nn.sigmoid(gate_b) * (o_dsa @ w_branch_dsa[l]))
        x = x + mix @ w_out[l]
        h2 = rms_norm(x, norm2_g[l]).astype(dt)
        x = x + hier_moe(h2, w_router_group[l], b_router_group[l], w_router_expert[l],
                         b_router_expert[l], w_exp_gate[l], w_exp_up[l], w_exp_down[l]).astype(dt)
    return x


_drawn_inputs = setup_inputs


def setup_inputs(seed=0):
    import zlib

    import numpy as np

    out = dict(_drawn_inputs(seed))
    spreads = {}
    factors = {'gla_b_a': 5.175,
     'dsa_q_norm_g': 3.841,
     'dsa_k_norm_g': 3.947,
     'idx_k_ln_b': 3.817,
     'b_router_group': 31.508,
     'b_router_expert': 5.509}
    for name, (base, spread) in spreads.items():
        noise = np.random.default_rng([zlib.crc32(name.encode()), seed]).standard_normal(out[name].shape)
        drawn = base * np.exp(spread * noise) if base else spread * noise
        out[name] = __import__('jax').numpy.asarray(drawn.astype(out[name].dtype))
    for name, factor in factors.items():
        out[name] = (out[name] * factor).astype(out[name].dtype)
    return out
```

```python
from contextlib import ExitStack

import numpy as np

import concourse.bass as bass
from concourse import mybir

ALU = mybir.AluOpType
ACT = mybir.ActivationFunctionType
F32 = mybir.dt.float32
BF16 = mybir.dt.bfloat16
I32 = mybir.dt.int32
U32 = mybir.dt.uint32
AX = mybir.AxisListType.X

P = 128
CHUNK = 64
EPS = 1e-6
GATE_TEMP = 16.0
TOPK_MAX = 256
TOP_E = 2
SLOTS = 64
NEG = -1.0e30
TAKEN = -3.0e38
PIECE = 4096
QK_STEPS = 8 * (2 * 3 + 1)


class Steps:

    def __init__(self, eng, sem, base=0):
        self.eng, self.sem, self.base, self.n = eng, sem, base, 0

    def did(self, instruction):
        instruction.then_inc(self.sem, 1)
        self.n += 1
        return self.n

    def settle(self, n=None):
        self.eng.wait_ge(self.sem, self.base + (self.n if n is None else n))


def encoder_block(nc, x, norm1_g, w_in, gla_w_a2, gla_b_a, gla_norm_g, dsa_q_norm_g, dsa_k_norm_g,
                  idx_k_ln_g, idx_k_ln_b, w_branch_gla, w_branch_dsa, w_out, norm2_g,
                  w_router_group, b_router_group, w_router_expert, b_router_expert,
                  w_exp_gate, w_exp_up, w_exp_down, out):
    _, S, D = x.shape
    RANK = gla_w_a2.shape[1]
    DK = D // 2 // 4
    DV = gla_norm_g.shape[1]
    GH = D // DV
    HD = dsa_q_norm_g.shape[1]
    H = D // HD
    ID = idx_k_ln_g.shape[1]
    G = w_router_group.shape[2]
    NE = w_router_expert.shape[2]
    EPG = NE // G
    F = w_exp_gate.shape[3]
    IH = (w_in.shape[2] - (2 * GH * DK + 2 * D + RANK + 3 * D + ID + 2 * D)) // (ID + 1)
    TOPK = min(TOPK_MAX, S // 4)
    T = S // P
    K = D // P
    NCH = S // CHUNK
    BLK = 512
    HALF = F // 2
    assert (S, D, F, BLK, HD, DK, TOPK) == (512, 1024, 512, 512, P, P, P) and IH == 8 and ID == 64

    widths = [GH * DK, GH * DK, D, RANK, D, D, D, D, IH * ID, ID, IH, D, D]
    offs = [int(v) for v in np.cumsum([0] + widths)]
    O_GQ, O_GK, O_GV, O_GA, O_GR, O_DQ, O_DK, O_DV, O_IQ, O_IK, O_IW, O_SA, O_SB = offs[:13]
    assert O_DK == O_DQ + D and O_SB == O_SA + D

    PAIRS = S * TOP_E
    MORE = (PAIRS - 1) // SLOTS
    ROWS = (NE + MORE) * SLOTS
    FIRST_MORE = NE * SLOTS
    MAX_TILES = S // SLOTS

    xd = x[0].rearrange("(t p) d -> p t d", p=P)
    outd = out[0].rearrange("(t p) d -> p t d", p=P)
    wind = w_in[0].rearrange("(k p) n -> p k n", p=P)
    pad_ = w_branch_gla[0].rearrange("(k p) n -> p k n", p=P)
    pbd_ = w_branch_dsa[0].rearrange("(k p) n -> p k n", p=P)
    woutd = w_out[0].rearrange("(k p) n -> p k n", p=P)
    h2_rows = nc.dram_tensor("h2_rows", (S, D), F32).ap()
    y_rows = nc.dram_tensor("y_rows", (ROWS, D), F32).ap()
    row_token = nc.dram_tensor("row_token", (ROWS, 1), I32).ap()
    wgd = w_exp_gate[0].rearrange("e (k p) f -> e p k f", p=P)
    wud = w_exp_up[0].rearrange("e (k p) f -> e p k f", p=P)
    wdd = w_exp_down[0].rearrange("e (k p) d -> e p k d", p=P)

    with ExitStack() as ctx:
        def sem(name):
            return ctx.enter_context(nc.semaphore(name))

        def sb(name, shape, dt=F32):
            return ctx.enter_context(nc.sbuf_tensor(name, shape, dt))

        arena = sb("arena", [P, 12 * PIECE])
        bank = [ctx.enter_context(nc.psum_tensor(f"bank{i}", [P, 512], F32)) for i in range(8)]

        def piece(i, n=1, words=None, off=0):
            return arena[:, i * PIECE + off:i * PIECE + off + (words or n * PIECE - off)]

        hT = piece(0).rearrange("p (k t) -> p k t", k=K)
        ring = [piece(1), piece(2)]
        qk = piece(3, 2).rearrange("p (h t) -> p h t", h=2 * H)
        vals = piece(5, 3).rearrange("p (v t d) -> p v t d", v=3, t=T)
        dv, gv, gr = vals[:, 0], vals[:, 1], vals[:, 2]
        gqT = piece(8, words=2048).rearrange("p (h t) -> p h t", h=GH)
        gk = piece(8, words=2048, off=2048).rearrange("p (t n) -> p t n", t=T)
        gates = arena[:, 6 * PIECE:10 * PIECE].rearrange("p (s q j t) -> p s q j t", s=2, q=2, j=K)[:, :, 0]
        mixT = piece(3).rearrange("p (k t) -> p k t", k=K)
        x_sb = piece(9).rearrange("p (t d) -> p t d", t=T)
        AT = piece(9).rearrange("p (k t) -> p k t", k=K)
        h2T = piece(9).rearrange("p (k t) -> p k t", k=K)
        xn = piece(10).rearrange("p (t d) -> p t d", t=T)
        qiT = piece(10).rearrange("p (h t) -> p h t", h=IH)
        BT = piece(10).rearrange("p (k t) -> p k t", k=K)
        x2 = piece(10).rearrange("p (t d) -> p t d", t=T)
        M2 = 11 * PIECE

        def m2(off, words):
            return arena[:, M2 + off:M2 + off + words]
        SMALL = ID + 32 + IH
        wsm = m2(0, K * SMALL).rearrange("p (k n) -> p k n", k=K)
        ki_raw, ki_cen, ki_sq = m2(832, 512), m2(1344, 512), m2(1856, 512)
        kiT = m2(2368, 512)
        relu = [m2(2880, 512), m2(3392, 512)]
        wiT = m2(3392, 512)
        sq = [m2(0, 512), m2(512, 512)]
        rms = [m2(1024, 512), m2(1536, 512)]
        state = [piece(10, words=1024, off=1024 * i).rearrange("p (h v) -> p h v", h=GH) for i in range(2)]
        g_abs, g_min, g_log, g_kd = [piece(10, words=512, off=2048 + 512 * i) for i in range(4)]
        oscr = [m2(DV * i, DV) for i in range(GH)]
        wa2, gnorm = m2(2048, GH * DK), m2(2048 + GH * DK, DV)
        prob = [m2(512 * i, 512) for i in range(3)]
        probT = [m2(1536 + 512 * i, 512) for i in range(3)]
        zrow = m2(3072, D)
        mtmp = [m2(512 * i, 512) for i in range(2)]
        h2s = [m2(1024 * i, 1024) for i in range(2)]
        g2b = m2(2048, 1024)
        lgT = m2(3072, 512)
        le = m2(0, T * NE).rearrange("p (t e) -> p t e", t=T)
        pen = m2(128, T * NE).rearrange("p (t e) -> p t e", t=T)
        oh = m2(256, TOP_E * T * NE).rearrange("p (k t e) -> p k t e", k=TOP_E, t=T)
        cnt, more, xinc, mbase = [m2(1024 + NE * i, NE) for i in range(4)]
        own = m2(512, MORE * NE).rearrange("p (m e) -> p m e", m=MORE)
        slot_pieces = [(0, 6, 8), (4, 5, 7), (1, 2, 3)]
        wgu, wdn = [], []
        for a, b, c in slot_pieces:
            both = arena[:, a * PIECE:(b + 1) * PIECE]
            wgu.append((piece(a).rearrange("p (k f) -> p k f", k=K), piece(b).rearrange("p (k f) -> p k f", k=K),
                        both.rearrange("p (q w) -> p q w", w=PIECE)[:, ::(b - a), :].rearrange(
                            "p q (k f) -> p q k f", k=K)))
            wdn.append(piece(c).rearrange("p (k d) -> p k d", k=F // P))
        xg = [arena[:, 9 * PIECE + 1024 * i:9 * PIECE + 1024 * (i + 1)] for i in range(3)]
        hTe = [m2(512 * i, 512).rearrange("p (k s) -> p k s", k=K) for i in range(3)]
        silu_g, hid = m2(1536, 256), m2(1792, 256)
        hidT = m2(2048, 256).rearrange("p (c h s) -> p c h s", c=2, h=2)
        y_sb = [m2(2304 + 512 * i, 512) for i in range(3)]
        yg = [arena[:, 1024 * i:1024 * (i + 1)] for i in range(TOP_E * T)]

        ident = sb("ident", [P, P])
        mean_m = sb("mean_m", [P, P])
        mean_i = sb("mean_i", [ID, ID])
        suffix = sb("suffix", [P, P])
        chunk_of = sb("chunk_of", [P, 2])
        before = sb("before", [P, P], BF16)
        ones_b = sb("ones_b", [P, P], BF16)
        one = sb("one", [P, 1])
        eps = sb("eps", [P, 1])
        zero_i = sb("zero_i", [P, ROWS // SLOTS], I32)
        bias0 = sb("bias0", [P, P])
        bias = [bias0] + [sb(f"bias{i}", [P, (i + 1) * P]) for i in range(1, T)]
        gaT = sb("gaT", [32, S])
        g1c = sb("g1c", [P, K])
        gqk = sb("gqk", [P, 2])
        lngb = sb("lngb", [ID, 2])
        wi = sb("wi", [P, T, IH])
        ms = sb("ms", [P, T])
        rs = sb("rs", [P, T])
        mx8 = sb("mx8", [P, T, 8])
        decay = sb("decay", [P, GH, NCH])
        oms = sb("oms", [P, T, GH])
        ors = sb("ors", [P, T, GH])
        orr = sb("orr", [P, GH])
        nmx = sb("nmx", [P, T * H])
        mxl = sb("mxl", [P, T * H])
        psm = sb("psm", [P, T * H])
        prc = sb("prc", [P, T * H])
        brt = sb("brt", [G + NE, 1])
        wr = sb("wr", [P, K, G + NE])
        tokid = sb("tokid", [P, T], I32)
        eio = sb("eio", [P, NE])
        gio = sb("gio", [P, NE])
        tio = sb("tio", [P, MORE])
        lg = sb("lg", [P, T, 8])
        tg = sb("tg", [P, T, G])
        v8 = sb("v8", [P, T, 8])
        i8 = sb("i8", [P, T, 8], U32)
        gid = sb("gid", [P, T])
        gw = sb("gw", [P, T])
        eid = sb("eid", [P, TOP_E, T])
        wt = sb("wt", [P, TOP_E, T])
        mask_b = sb("mask_b", [P, T, NE], BF16)
        rk = sb("rk", [P, TOP_E, T])
        rtmp = sb("rtmp", [P, TOP_E, T])
        isov = sb("isov", [P, TOP_E, T])
        rowf = sb("rowf", [P, TOP_E, T])
        tabf = sb("tabf", [P, TOP_E, T])
        row_i = sb("row_i", [P, TOP_E, T], I32)
        tab_i = sb("tab_i", [P, TOP_E, T], I32)
        ownf = sb("ownf", [P, MORE + 1])
        own_i = sb("own_i", [P, MORE + 1], I32)
        idx_all = sb("idx_all", [SLOTS, NE], I32)
        idx_more = sb("idx_more", [SLOTS, 1], I32)

        names = """consts_done small_loaded wsm_zeroed ms_ready xn_ready xT_ready hT_by_dve hT_by_act
            acc_ready small_ready ki_evicted small_evicted ki_mean_ready ki_cen_ready ki_sq_ready ki_var_ready
            kiT_ready wi_ps wi_ready qiT_ready idx_logit_ready relu_ready relu_used
            qk_sq_ready qk_ms_ready qk_rms_ready qk_ready bias_ready
            gv_ready a_ready a_abs a_exp la_ready suf_ready kd_ready kdec_ready ind_ready decay_ready kv_ready
            state_ready o_ready oms_ready o_normed oT_ready AT_ready
            logit_ready lmax_ready prob_ready probn_ready pT_ready pT_evicted av_done BT_ready
            gates_ready f_free f_ready mix_ready x_again x_out_ready x2_ready h2_ms h2_ready h2_stored h2T_ps h2T_ready
            lgT_ps lgT_ready lg_ps gexp_in gexp_out eexp_in eexp_out maskb_ready rank_ready tab_ready
            table_zero scattered idx_loaded own_ready
            wring_free xg_T he_ready gu_ready silu_ready hid_ready hidT_ps hidT_ready y_ready
            m_w m_idx m_xg m_T m_he m_gu m_silu m_hid m_hT m_hTs m_y m_st
            wr_loaded rows_zeroed oln_ready rs_ready ki_std_ready ors_ready h2_rs gla_loaded g2_loaded out_ready out_stored dve_s act_s pool_s dve_qk""".split()
        s = {n: sem(n) for n in names}
        acc_free = [sem(f"acc_free{i}") for i in range(2)]
        x_loaded = [sem(f"x_loaded{i}") for i in range(T)]
        wring = [sem(f"wring_loaded{i}") for i in range(2)]
        wgu_loaded = [sem(f"wgu_loaded{i}") for i in range(3)]
        wdn_loaded = [sem(f"wdn_loaded{i}") for i in range(3)]
        xg_loaded = [sem(f"xg_loaded{i}") for i in range(3)]
        y_stored = [sem(f"y_stored{i}") for i in range(3)]
        yg_loaded = [sem(f"yg_loaded{i}") for i in range(TOP_E * T)]
        h2s_stored = [sem(f"h2s_stored{i}") for i in range(2)]

        B_IQ, B_Q, B_GQ, B_GK, B_DV, B_GV, B_GR, B_SA, B_PA, B_OUT = 0, 1, 5, 6, 7, 9, 11, 13, 17, 21
        N_IQ, N_Q, N_GQ, N_GK, N_DV, N_GV, N_GR, N_SA = [4 * b for b in
                                                         (B_IQ, B_Q, B_GQ, B_GK, B_DV, B_GV, B_GR, B_SA)]

        E3 = NE - NE % 3
        assert NE % 3 == 2
        UNITS = H * T
        SMALL_DMAS = 11

        block = ctx.enter_context(nc.Block())

        @block.sync
        def _(sp):
            def load_block(m, src):
                sp.dma_start(ring[m % 2].rearrange("p (k n) -> p k n", k=K), src).then_inc(wring[m % 2], 16)

            def load_win(m, off, more_=0):
                if m >= 2:
                    sp.wait_ge(s["acc_ready"], more_ * 4 + 4 * (m - 1))
                load_block(m, wind[:, :, bass.ds(off, BLK)])

            load_win(B_IQ, O_IQ)
            for i in range(4):
                load_win(B_Q + i, O_DQ + BLK * i)
            load_win(B_GQ, O_GQ)
            load_win(B_GK, O_GK)
            for j, off in enumerate((O_DV, O_GV, O_GR)):
                for i in range(2):
                    load_win(B_DV + 2 * j + i, off + BLK * i)
            with sp.Fori(0, 2) as g:
                for i in range(2):
                    load_win(B_SA + i, g * (2 * BLK) + (O_SA + BLK * i), g * 2)
            for i in range(2):
                if i == 0:
                    sp.wait_ge(s["acc_ready"], 4 * (B_PA - 1))
                else:
                    sp.wait_ge(s["f_ready"], 4)
                load_block(B_PA + 2 * i, pad_[:, :, BLK * i:BLK * (i + 1)])
                if i == 0:
                    sp.wait_ge(s["acc_ready"], 4 * B_PA)
                load_block(B_PA + 2 * i + 1, pbd_[:, :, BLK * i:BLK * (i + 1)])
            sp.wait_ge(s["f_ready"], K)
            for i in range(2):
                load_block(B_OUT + i, woutd[:, :, BLK * i:BLK * (i + 1)])
            sp.dma_start(x2, xd).then_inc(s["x_again"], 16)

            def expert(dram, e):
                return dram[bass.ds(e, 1)].rearrange("e p k f -> p (e k) f")

            def load_up(e, sl):
                sp.dma_start(wgu[sl][0], expert(wgd, e)).then_inc(wgu_loaded[sl], 16)
                sp.dma_start(wgu[sl][1], expert(wud, e)).then_inc(wgu_loaded[sl], 16)

            def load_down(e, sl):
                sp.dma_start(wdn[sl], expert(wdd, e)).then_inc(wdn_loaded[sl], 16)

            sp.wait_ge(s["mix_ready"], K)
            for e in range(2):
                load_up(e, e)
                load_down(e, e)
            sp.wait_ge(s["x_out_ready"], 2 * T)
            load_up(2, 2)
            load_down(2, 2)
            with sp.Fori(3, E3, 3) as e:
                for sl in range(3):
                    sp.wait_ge(s["gu_ready"], e + (sl - 2))
                    load_up(e + sl, sl)
                    sp.wait_ge(s["y_ready"], e + (sl - 2))
                    load_down(e + sl, sl)
            for sl in range(2):
                sp.wait_ge(s["gu_ready"], E3 + sl - 2)
                load_up(E3 + sl, sl)
                sp.wait_ge(s["y_ready"], E3 + sl - 2)
                load_down(E3 + sl, sl)
            sp.wait_ge(s["own_ready"], 1)
            n_more = sp.value_load(own_i[0:1, MORE:MORE + 1], min_val=0, max_val=MORE)
            with sp.If(n_more > 0):
                sp.wait_ge(s["y_ready"], NE)
                with sp.Fori(0, n_more) as t:
                    e = sp.value_load(own_i[0:1, bass.ds(t, 1)], min_val=0, max_val=NE - 1)
                    sp.wait_ge(s["m_y"], t + 1)
                    sp.dma_start(wgu[2][0], expert(wgd, e)).then_inc(s["m_w"], 16)
                    sp.dma_start(wgu[2][1], expert(wud, e)).then_inc(s["m_w"], 16)
                    sp.dma_start(wdn[2], expert(wdd, e)).then_inc(s["m_w"], 16)

        @block.tensor
        def _(pe):
            mm, tr = nc.tensor.matmul, nc.tensor.transpose

            def arrived(m, more_=0):
                pe.wait_ge(wring[m % 2], more_ + 16 * (m // 2 + 1))

            def blk(m):
                return ring[m % 2].rearrange("p (k n) -> p k n", k=K)

            def acc_tile(n, lhs, rhs, more_=0):
                if n >= 2:
                    pe.wait_ge(acc_free[n % 2], more_ + n // 2)
                for k in range(K):
                    last = mm(bank[n % 2][:, :], lhs(k), rhs(k), start=(k == 0), stop=(k == K - 1))
                last.then_inc(s["acc_ready"], 1)

            def feature_tile(m, c, n, more_=0):
                acc_tile(n, lambda k: blk(m)[:, k, c * P:(c + 1) * P], lambda k: hT[:, k, :], more_)

            pe.wait_ge(s["consts_done"], 1)
            pe.wait_ge(s["xn_ready"], T)
            for k in range(K):
                if k >= 4:
                    pe.wait_ge(s["hT_by_dve" if k % 2 == 0 else "hT_by_act"], (k - 4) // 2 + 1)
                for t in range(T):
                    last = tr(bank[2 + k % 4][:, t * P:(t + 1) * P], xn[:, t, k * P:(k + 1) * P], ident[:, :])
                last.then_inc(s["xT_ready"], 1)
            pe.wait_ge(s["hT_by_dve"], K // 2)
            pe.wait_ge(s["hT_by_act"], K // 2)

            pe.wait_ge(s["small_loaded"], 16 * SMALL_DMAS)
            for k in range(K):
                last = mm(bank[6][0:SMALL, :], wsm[:, k, :], hT[:, k, :], start=(k == 0), stop=(k == K - 1))
            last.then_inc(s["small_ready"], 1)
            arrived(B_IQ)
            for c in range(4):
                feature_tile(B_IQ, c, N_IQ + c)
                if c == 0:
                    pe.wait_ge(s["ki_evicted"], 1)
                    mm(bank[7][0:ID, :], mean_i[:, :], ki_raw[0:ID, :], start=True, stop=True)\
                        .then_inc(s["ki_mean_ready"], 1)
                if c == 1:
                    pe.wait_ge(s["small_evicted"], 1)
                    pe.wait_ge(s["ki_sq_ready"], 1)
                    mm(bank[6][0:ID, :], mean_i[:, :], ki_sq[0:ID, :], start=True, stop=True)\
                        .then_inc(s["ki_var_ready"], 1)
            pe.wait_ge(s["ki_cen_ready"], 1)
            for t in range(T):
                last = tr(bank[7][:, t * IH:(t + 1) * IH], wiT[0:IH, t * P:(t + 1) * P], ident[0:IH, 0:IH])
            last.then_inc(s["wi_ps"], 1)
            for i in range(2):
                pe.wait_ge(acc_free[i], (N_IQ + 4) // 2)
            pe.wait_ge(s["kiT_ready"], 1)
            u = 0
            for i in range(1, T):
                n = (i + 1) * P
                for h in range(IH):
                    if u >= 4:
                        pe.wait_ge(s["relu_ready"], u - 3)
                    mm(bank[2 + u % 4][:, 0:n], qiT[0:ID, h, i * P:(i + 1) * P], kiT[0:ID, 0:n],
                       start=True, stop=True).then_inc(s["idx_logit_ready"], 1)
                    u += 1

            with pe.Fori(0, 2) as g:
                def mean_square(j):
                    pe.wait_ge(s["qk_sq_ready"], g * 8 + (j + 1))
                    if j >= 2:
                        pe.wait_ge(s["qk_rms_ready"], g * 8 + (j - 1))
                    mm(bank[6 + j % 2][:, :], mean_m[:, :], sq[j % 2], start=True, stop=True)\
                        .then_inc(s["qk_ms_ready"], 1)
                for j in range(8):
                    if j % 4 == 0:
                        arrived(B_Q + j // 4, g * 16)
                    feature_tile(B_Q + j // 4, j % 4, N_Q + j, g * 4)
                    if j > 0:
                        mean_square(j - 1)
                mean_square(7)

            def token_block(m, n0):
                arrived(m)
                for t in range(T):
                    acc_tile(n0 + t, lambda k: hT[:, k, t * P:(t + 1) * P], lambda k: blk(m)[:, k, :])

            arrived(B_GQ)
            for c in range(4):
                feature_tile(B_GQ, c, N_GQ + c)
            token_block(B_GK, N_GK)
            for j in range(6):
                token_block(B_DV + j, N_DV + 4 * j)

            for i in range(2):
                pe.wait_ge(acc_free[i], N_SA // 2)
            pe.wait_ge(s["gla_loaded"], 48)
            pe.wait_ge(s["small_evicted"], 1)
            mm(bank[2][:, :], gaT[0:RANK + 1, 0:P], wa2[0:RANK + 1, :], start=True, stop=True)\
                .then_inc(s["a_ready"], 1)
            for t in range(T):
                pe.wait_ge(s["la_ready"], t + 1)
                mm(bank[3][:, :], suffix[:, :], g_log, start=True, stop=True).then_inc(s["suf_ready"], 1)
                if t >= 1:
                    pe.wait_ge(s["decay_ready"], t)
                for h in range(GH):
                    last = mm(bank[4][:, 2 * h:2 * h + 2], g_log[:, h * DK:(h + 1) * DK], chunk_of[:, :],
                              start=True, stop=True)
                last.then_inc(s["ind_ready"], 1)
                if t + 1 < T:
                    mm(bank[2][:, :], gaT[0:RANK + 1, (t + 1) * P:(t + 2) * P], wa2[0:RANK + 1, :],
                       start=True, stop=True).then_inc(s["a_ready"], 1)
                pe.wait_ge(s["kdec_ready"], t + 1)
                for c in range(2):
                    ch = 2 * t + c
                    rows = slice(c * CHUNK, (c + 1) * CHUNK)
                    if ch >= 1:
                        pe.wait_ge(s["state_ready"], ch)
                    for h in range(GH):
                        last = mm(bank[5 + h // 2][:, (h % 2) * DV:(h % 2 + 1) * DV],
                                  gk[rows, t, h * DK:(h + 1) * DK], gv[rows, t, h * DV:(h + 1) * DV],
                                  start=True, stop=True)
                    last.then_inc(s["kv_ready"], 1)
                    pe.wait_ge(s["state_ready"], ch + 1)
                    if c == 0 and t >= 1:
                        pe.wait_ge(s["o_normed"], t)
                    for h in range(GH):
                        last = mm(bank[h // 2][rows, (h % 2) * DV:(h % 2 + 1) * DV],
                                  gqT[:, h, ch * CHUNK:(ch + 1) * CHUNK], state[c][:, h, :],
                                  start=True, stop=True)
                    last.then_inc(s["o_ready"], 1)
                pe.wait_ge(s["o_normed"], t + 1)
                for hf in range(2):
                    if t or hf:
                        pe.wait_ge(s["AT_ready"], 2 * t + hf)
                    for k in range(4):
                        last = tr(bank[7][:, k * P:(k + 1) * P], gr[:, t, (4 * hf + k) * P:(4 * hf + k + 1) * P],
                                  ident[:, :])
                    last.then_inc(s["oT_ready"], 1)

            def logits(u):
                h, i = divmod(u, T)
                n = (i + 1) * P
                if u >= 2:
                    pe.wait_ge(s["lmax_ready"], u - 1)
                mm(bank[2 + u % 2][:, 0:n], qk[:, h, i * P:(i + 1) * P], qk[:, H + h, 0:n],
                   start=True, stop=True).then_inc(s["logit_ready"], 1)

            def prob_transposes(u):
                pe.wait_ge(s["probn_ready"], u + 1)
                if u >= 2:
                    pe.wait_ge(s["pT_evicted"], u - 1)
                for j in range(u % T + 1):
                    last = tr(bank[4 + u % 2][:, j * P:(j + 1) * P], prob[u % 3][:, j * P:(j + 1) * P], ident[:, :])
                last.then_inc(s["pT_ready"], 1)

            def attend(u):
                h, i = divmod(u, T)
                pe.wait_ge(s["pT_evicted"], u + 1)
                if i == 0 and h >= 2:
                    pe.wait_ge(s["BT_ready"], h - 1)
                for j in range(i + 1):
                    last = mm(bank[6 + h % 2][:, i * P:(i + 1) * P], dv[:, j, h * HD:(h + 1) * HD],
                              probT[u % 3][:, j * P:(j + 1) * P], start=(j == 0), stop=(j == i))
                last.then_inc(s["av_done"], 1)

            pe.wait_ge(s["qk_ready"], 1 + 2 * H)
            pe.wait_ge(s["AT_ready"], 2 * T)
            logits(0)
            for u in range(UNITS + 2):
                if u < UNITS and u % 2 == 0:
                    n = u // 2
                    if n % 4 == 0:
                        arrived(B_SA + n // 4)
                    feature_tile(B_SA + n // 4, n % 4, N_SA + n)
                if u + 1 < UNITS:
                    logits(u + 1)
                if 1 <= u <= UNITS:
                    prob_transposes(u - 1)
                if u >= 2:
                    attend(u - 2)

            pe.wait_ge(s["BT_ready"], H)
            with pe.Fori(0, 2) as g:
                arrived(B_PA, g * 16)
                arrived(B_PA + 1, g * 16)
                for j in range(4):
                    pe.wait_ge(s["f_free"], g * 4 + (j + 1))
                    b0 = 2 * (j % 2)
                    for b, m, src in ((b0, B_PA, AT), (b0 + 1, B_PA + 1, BT)):
                        for k in range(K):
                            last = mm(bank[b][:, :], blk(m)[:, k, j * P:(j + 1) * P], src[:, k, :],
                                      start=(k == 0), stop=(k == K - 1))
                    last.then_inc(s["f_ready"], 1)

            def h2_transposes(t):
                pe.wait_ge(s["h2_ready"], t + 1)
                for hf in range(2):
                    if t >= 1:
                        pe.wait_ge(s["h2T_ready"], 2 * (t - 1) + hf + 1)
                    for k in range(4):
                        last = tr(bank[hf][:, k * P:(k + 1) * P], h2s[t % 2][:, (4 * hf + k) * P:(4 * hf + k + 1) * P],
                                  ident[:, :])
                    last.then_inc(s["h2T_ps"], 1)

            pe.wait_ge(s["mix_ready"], K)
            arrived(B_OUT)
            arrived(B_OUT + 1)
            for t in range(T):
                for hf in range(2):
                    if t >= 2:
                        pe.wait_ge(s["x2_ready"], 2 * (t - 2) + hf + 1)
                    for k in range(K):
                        last = mm(bank[4 + 2 * (t % 2) + hf][:, :], mixT[:, k, t * P:(t + 1) * P],
                                  blk(B_OUT + hf)[:, k, :], start=(k == 0), stop=(k == K - 1))
                    last.then_inc(s["x_out_ready"], 1)
                if t >= 1:
                    h2_transposes(t - 1)
            h2_transposes(T - 1)

            pe.wait_ge(s["h2T_ready"], 2 * T)
            pe.wait_ge(s["wr_loaded"], 16)
            for k in range(K):
                last = mm(bank[2][0:G + NE, :], wr[:, k, :], h2T[:, k, :], start=(k == 0), stop=(k == K - 1))
            last.then_inc(s["lgT_ps"], 1)
            pe.wait_ge(s["lgT_ready"], 1)
            for t in range(T):
                last = tr(bank[3][:, t * (G + NE):(t + 1) * (G + NE)], lgT[0:G + NE, t * P:(t + 1) * P],
                          ident[0:G + NE, 0:G + NE])
            last.then_inc(s["lg_ps"], 1)
            pe.wait_ge(s["maskb_ready"], 1)
            for t in range(T):
                for j in range(t + 1):
                    mm(bank[4][:, t * NE:(t + 1) * NE], (before if j == t else ones_b)[:, :], mask_b[:, j, :],
                       start=(j == 0), stop=(j == t))
            for j in range(T):
                last = mm(bank[5][:, 0:NE], ones_b[:, :], mask_b[:, j, :], start=(j == 0), stop=(j == T - 1))
            last.then_inc(s["rank_ready"], 1)

            def gather_transposes(b, done):
                for k in range(K):
                    last = tr(bank[4][:, k * SLOTS:(k + 1) * SLOTS], xg[b][0:SLOTS, k * P:(k + 1) * P],
                              ident[0:SLOTS, 0:SLOTS])
                last.then_inc(done, 1)

            def gate_up(sl, done):
                for k in range(K):
                    for hf in range(2):
                        last = mm(bank[0][hf * SLOTS:(hf + 1) * SLOTS, :], hTe[sl][:, k, :],
                                  wgu[sl][2][:, :, k, hf * HALF:(hf + 1) * HALF], start=(k == 0), stop=(k == K - 1))
                last.then_inc(done, 1)

            def hidden_transposes(done):
                for c in range(2):
                    last = tr(bank[5][:, c * P:(c + 1) * P], hid[:, c * P:(c + 1) * P], ident[:, :])
                last.then_inc(done, 1)

            def down(sl, done):
                for k in range(F // P):
                    for hf in range(2):
                        last = mm(bank[1][hf * SLOTS:(hf + 1) * SLOTS, :], hidT[:, k % 2, k // 2, :],
                                  wdn[sl][:, k, hf * 512:(hf + 1) * 512], start=(k == 0), stop=(k == F // P - 1))
                last.then_inc(done, 1)

            def run_expert(e, sl, up_round, has_next=True):
                pe.wait_ge(wgu_loaded[sl], up_round * 2)
                nx = (sl + 1) % 3
                if has_next:
                    pe.wait_ge(xg_loaded[nx], up_round + (16 if nx == 0 else 0))
                pe.wait_ge(s["he_ready"], e + 1)
                gate_up(sl, s["gu_ready"])
                if has_next:
                    gather_transposes(nx, s["xg_T"])
                pe.wait_ge(s["hid_ready"], e + 1)
                hidden_transposes(s["hidT_ps"])
                pe.wait_ge(s["hidT_ready"], e + 1)
                pe.wait_ge(wdn_loaded[sl], up_round)
                down(sl, s["y_ready"])

            pe.wait_ge(xg_loaded[0], 16)
            gather_transposes(0, s["xg_T"])
            with pe.Fori(0, E3 // 3) as r:
                for sl in range(3):
                    run_expert(r * 3 + sl, sl, r * 16 + 16)
            for sl in range(2):
                run_expert(E3 + sl, sl, 16 * (E3 // 3 + 1), has_next=(sl == 0))

            n_more = pe.value_load(own_i[0:1, MORE:MORE + 1], min_val=0, max_val=MORE)
            with pe.If(n_more > 0):
                with pe.Fori(0, n_more) as t:
                    pe.wait_ge(s["m_xg"], t * 16 + 16)
                    for k in range(K):
                        last = tr(bank[3 + k // 4][:, (k % 4) * P:(k % 4 + 1) * P], xg[0][:, k * P:(k + 1) * P],
                                  ident[:, :])
                    last.then_inc(s["m_T"], 1)
                    pe.wait_ge(s["m_w"], t * 48 + 48)
                    pe.wait_ge(s["m_he"], t + 1)
                    gate_up(2, s["m_gu"])
                    pe.wait_ge(s["m_hid"], t + 1)
                    hidden_transposes(s["m_hT"])
                    pe.wait_ge(s["m_hTs"], t + 1)
                    down(2, s["m_y"])

        @block.scalar
        def _(act):
            A = nc.scalar.activation
            for t in range(T):
                act.dma_start(x_sb[:, t, :], xd[:, t, :]).then_inc(x_loaded[t], 16)
            small = s["small_loaded"]
            act.wait_ge(s["wsm_zeroed"], 1)
            with nc.allow_non_contiguous_dma(reason="a few narrow columns, once"):
                act.dma_start(wsm[:, :, 0:ID], wind[:, :, O_IK:O_IK + ID]).then_inc(small, 16)
                act.dma_start(wsm[:, :, ID:ID + RANK], wind[:, :, O_GA:O_GA + RANK]).then_inc(small, 16)
                act.dma_start(wsm[:, :, ID + 32:ID + 32 + IH], wind[:, :, O_IW:O_IW + IH]).then_inc(small, 16)
                act.dma_start(g1c[:, :], norm1_g[0].rearrange("(k p) -> p k", p=P)).then_inc(small, 16)
                act.dma_start(gqk[:, 0:1], dsa_q_norm_g.rearrange("a p -> p a")).then_inc(small, 16)
                act.dma_start(gqk[:, 1:2], dsa_k_norm_g.rearrange("a p -> p a")).then_inc(small, 16)
                act.dma_start(lngb[:, 0:1], idx_k_ln_g.rearrange("a p -> p a")).then_inc(small, 16)
                act.dma_start(lngb[:, 1:2], idx_k_ln_b.rearrange("a p -> p a")).then_inc(small, 16)
                act.dma_start(brt[0:G, :], b_router_group.rearrange("a p -> p a")).then_inc(small, 16)
                act.dma_start(brt[G:G + NE, :], b_router_expert.rearrange("a p -> p a")).then_inc(small, 16)
                act.dma_start(wr[:, :, 0:G], w_router_group[0].rearrange("(k p) n -> p k n", p=P)).then_inc(small, 16)
            act.wait_ge(s["consts_done"], 1)
            for t in range(T):
                act.wait_ge(x_loaded[t], 16)
                A(xn[:, t, :], x_sb[:, t, :], ACT.Square, scale=float(D) ** -0.5,
                  accum_out=ms[:, t:t + 1]).then_inc(s["ms_ready"], 1)
                act.wait_ge(s["ms_ready"], t + 1)
                A(ms[:, t:t + 1], ms[:, t:t + 1], ACT.Sqrt, bias=eps[:, 0:1]).then_inc(s["rs_ready"], 1)
            act.wait_ge(s["small_loaded"], 16 * SMALL_DMAS)
            for k in range(1, K, 2):
                act.wait_ge(s["xT_ready"], k + 1)
                A(hT[:, k, :], bank[2 + k % 4][:, :], ACT.Copy, scale=g1c[:, k:k + 1]).then_inc(s["hT_by_act"], 1)

            act.wait_ge(s["ki_cen_ready"], 1)
            A(ki_sq[0:ID, :], ki_cen[0:ID, :], ACT.Square).then_inc(s["ki_sq_ready"], 1)
            for c in range(4):
                n = N_IQ + c
                act.wait_ge(s["acc_ready"], n + 1)
                A(qiT[0:ID, 2 * c, :], bank[n % 2][0:ID, :], ACT.Copy)
                A(qiT[0:ID, 2 * c + 1, :], bank[n % 2][ID:2 * ID, :], ACT.Copy).then_inc(acc_free[n % 2], 1)
                if c == 1:
                    act.wait_ge(s["ki_var_ready"], 1)
                    A(ki_raw[0:ID, :], bank[6][0:ID, :], ACT.Sqrt, bias=eps[0:ID, 0:1]).then_inc(s["ki_std_ready"], 1)
            u = 0
            for i in range(1, T):
                n = (i + 1) * P
                for h in range(IH):
                    act.wait_ge(s["idx_logit_ready"], u + 1)
                    if u >= 2:
                        act.wait_ge(s["relu_used"], u - 1)
                    A(relu[u % 2][:, 0:n], bank[2 + u % 4][:, 0:n], ACT.Relu).then_inc(s["relu_ready"], 1)
                    u += 1

            with act.Fori(0, 2) as g:
                def root(j):
                    act.wait_ge(s["qk_ms_ready"], g * 8 + (j + 2))
                    act.wait_ge(s["qk_ready"], g * 8 + (1 + max(j - 1, 0)))
                    A(rms[j % 2], bank[6 + j % 2][:, :], ACT.Sqrt, bias=eps[:, 0:1]).then_inc(s["qk_rms_ready"], 1)

                for j in range(8):
                    n = N_Q + j
                    act.wait_ge(s["acc_ready"], g * 8 + (n + 1))
                    act.wait_ge(s["qk_ms_ready"], g * 8 + (1 + max(j - 1, 0)))
                    A(sq[j % 2], bank[n % 2][:, :], ACT.Square).then_inc(s["qk_sq_ready"], 1)
                    if j > 0:
                        root(j - 1)
                root(7)

            for c in range(4):
                n = N_GQ + c
                act.wait_ge(s["acc_ready"], n + 1)
                A(gqT[:, c, :], bank[n % 2][:, :], ACT.Copy, scale=float(DK) ** -0.5).then_inc(acc_free[n % 2], 1)
            for t in range(T):
                n = N_GK + t
                act.wait_ge(s["acc_ready"], n + 1)
                A(gk[:, t, :], bank[n % 2][:, :], ACT.Copy).then_inc(acc_free[n % 2], 1)
            for j in range(3):
                for hf in range(2):
                    for t in range(T):
                        n = N_DV + 8 * j + 4 * hf + t
                        act.wait_ge(s["acc_ready"], n + 1)
                        A(vals[:, j, t, hf * BLK:(hf + 1) * BLK], bank[n % 2][:, :],
                          ACT.Silu if j == 2 else ACT.Copy).then_inc(acc_free[n % 2], 1)

            def gate_log():
                A(g_log, g_abs, ACT.Exp).then_inc(s["act_s"], 1)
                act_steps[0] += 1
                act.wait_ge(s["act_s"], act_steps[0])
                A(g_abs, g_log, ACT.Ln, bias=one[:, 0:1]).then_inc(s["a_exp"], 1)

            act_steps = [0]
            act.wait_ge(s["a_abs"], 1)
            gate_log()
            for t in range(T):
                act.wait_ge(s["suf_ready"], t + 1)
                A(g_kd, bank[3][:, :], ACT.Exp).then_inc(s["kd_ready"], 1)
                act.wait_ge(s["ind_ready"], t + 1)
                A(decay[:, :, 2 * t:2 * t + 2], bank[4][:, 0:2 * GH].rearrange("p (h c) -> p h c", h=GH),
                  ACT.Exp).then_inc(s["decay_ready"], 1)
                if t + 1 < T:
                    act.wait_ge(s["a_abs"], t + 2)
                    gate_log()
                act.wait_ge(s["o_ready"], 2 * t + 2)
                for h in range(GH):
                    last = A(oscr[h], bank[h // 2][:, (h % 2) * DV:(h % 2 + 1) * DV], ACT.Square,
                             scale=float(DV) ** -0.5, accum_out=oms[:, t, h:h + 1])
                last.then_inc(s["oms_ready"], 1)
                act.wait_ge(s["oms_ready"], t + 1)
                A(ors[:, t, :], oms[:, t, :], ACT.Ln, bias=eps[:, 0:1]).then_inc(s["oln_ready"], 1)
                act.wait_ge(s["oln_ready"], t + 1)
                A(ors[:, t, :], ors[:, t, :], ACT.Exp, scale=-0.5).then_inc(s["ors_ready"], 1)
                for hf in range(2):
                    act.wait_ge(s["oT_ready"], 2 * t + hf + 1)
                    A(AT[:, 4 * hf:4 * hf + 4, t * P:(t + 1) * P],
                      bank[7][:, :].rearrange("p (k t) -> p k t", k=4), ACT.Copy).then_inc(s["AT_ready"], 1)

            def gate_tile(n):
                act.wait_ge(s["acc_ready"], N_SA + n + 1)
                A(gates[:, n // K, n % K, :], bank[n % 2][:, :], ACT.Exp, scale=-1.0)\
                    .then_inc(acc_free[n % 2], 1)

            for u in range(UNITS + 2):
                if u < UNITS:
                    if u % 2 == 1:
                        gate_tile(u // 2)
                    n = (u % T + 1) * P
                    act.wait_ge(s["lmax_ready"], u + 1)
                    A(prob[u % 3][:, 0:n], prob[u % 3][:, 0:n], ACT.Exp, bias=nmx[:, u:u + 1],
                      scale=float(HD) ** -0.5, accum_out=psm[:, u:u + 1]).then_inc(s["prob_ready"], 1)
                if u >= 2:
                    v = u - 2
                    n = (v % T + 1) * P
                    act.wait_ge(s["pT_ready"], v + 1)
                    if v >= 3:
                        act.wait_ge(s["av_done"], v - 2)
                    A(probT[v % 3][:, 0:n], bank[4 + v % 2][:, 0:n], ACT.Copy).then_inc(s["pT_evicted"], 1)
                    if v % T == 0 and v >= T:
                        act.wait_ge(s["av_done"], v)
                        h = v // T - 1
                        A(BT[:, h, :], bank[6 + h % 2][:, :], ACT.Copy).then_inc(s["BT_ready"], 1)
            act.wait_ge(s["av_done"], UNITS)
            A(BT[:, H - 1, :], bank[6 + (H - 1) % 2][:, :], ACT.Copy).then_inc(s["BT_ready"], 1)

            for t in range(T):
                act.wait_ge(s["x2_ready"], 2 * t + 2)
                if t >= 2:
                    act.wait_ge(h2s_stored[t % 2], 16 * (t // 2))
                    act.wait_ge(s["h2T_ps"], 2 * (t - 2) + 2)
                A(h2s[t % 2], x2[:, t, :], ACT.Square, scale=float(D) ** -0.5,
                  accum_out=ms[:, t:t + 1]).then_inc(s["h2_ms"], 1)
                act.wait_ge(s["h2_ms"], t + 1)
                A(ms[:, t:t + 1], ms[:, t:t + 1], ACT.Sqrt, bias=eps[:, 0:1]).then_inc(s["h2_rs"], 1)
                act.wait_ge(s["h2_ready"], t + 1)
                act.dma_start(h2_rows[t * P:(t + 1) * P, :], h2s[t % 2]).then_inc(h2s_stored[t % 2], 16)
                for hf in range(2):
                    act.wait_ge(s["h2T_ps"], 2 * t + hf + 1)
                    A(h2T[:, 4 * hf:4 * hf + 4, t * P:(t + 1) * P],
                      bank[hf][:, :].rearrange("p (k t) -> p k t", k=4), ACT.Copy).then_inc(s["h2T_ready"], 1)
            act.wait_ge(s["lgT_ps"], 1)
            act.wait_ge(s["rows_zeroed"], 16)
            A(lgT[0:G + NE, :], bank[2][0:G + NE, :], ACT.Identity, bias=brt[:, 0:1]).then_inc(s["lgT_ready"], 1)
            act.wait_ge(s["gexp_in"], 1)
            A(tg[:, :, :], tg[:, :, :], ACT.Exp).then_inc(s["gexp_out"], 1)
            act.wait_ge(s["eexp_in"], 1)
            A(wt[:, 1, :], wt[:, 1, :], ACT.Exp).then_inc(s["eexp_out"], 1)

            def store_y(row, sl, done):
                for hf in range(2):
                    act.dma_start(y_rows[bass.ds(row, SLOTS), hf * 512:(hf + 1) * 512],
                                  y_sb[sl][hf * SLOTS:(hf + 1) * SLOTS, :]).then_inc(done, 16)

            def run_expert(e, sl, rounds):
                act.wait_ge(s["gu_ready"], e + 1)
                A(silu_g, bank[0][:, 0:HALF], ACT.Silu).then_inc(s["silu_ready"], 1)
                act.wait_ge(s["hidT_ps"], e + 1)
                A(hidT, bank[5][:, 0:HALF].rearrange("p (c h s) -> p c h s", c=2, h=2), ACT.Copy)\
                    .then_inc(s["hidT_ready"], 1)
                act.wait_ge(s["y_ready"], e + 1)
                act.wait_ge(y_stored[sl], rounds * 32 + 32)
                A(y_sb[sl], bank[1][:, :], ACT.Copy).then_inc(s["act_s"], 1)
                act.wait_ge(s["act_s"], e + (T + 1))
                store_y(e * SLOTS, sl, y_stored[sl])

            with act.Fori(0, E3 // 3) as r:
                for sl in range(3):
                    run_expert(r * 3 + sl, sl, r)
            for sl in range(2):
                run_expert(E3 + sl, sl, E3 // 3)

            n_more = act.value_load(own_i[0:1, MORE:MORE + 1], min_val=0, max_val=MORE)
            with act.If(n_more > 0):
                with act.Fori(0, n_more) as t:
                    act.wait_ge(s["m_gu"], t + 1)
                    A(silu_g, bank[0][:, 0:HALF], ACT.Silu).then_inc(s["m_silu"], 1)
                    act.wait_ge(s["m_hT"], t + 1)
                    A(hidT, bank[5][:, 0:HALF].rearrange("p (c h s) -> p c h s", c=2, h=2), ACT.Copy)\
                        .then_inc(s["m_hTs"], 1)
                    act.wait_ge(s["m_y"], t + 2)
                    act.wait_ge(y_stored[2], 32 * (E3 // 3 + 1))
                    act.wait_ge(s["m_st"], t * 32 + 32)
                    A(y_sb[2], bank[1][:, :], ACT.Copy).then_inc(s["act_s"], 1)
                    act.wait_ge(s["act_s"], t + (NE + T + 1))
                    store_y(t * SLOTS + FIRST_MORE, 2, s["m_st"])

            for t in range(T):
                act.wait_ge(s["out_ready"], t + 1)
                act.dma_start(outd[:, t, :], x2[:, t, :]).then_inc(s["out_stored"], 16)
            act.wait_ge(s["out_stored"], 16 * T)

        @block.vector
        def _(dve):
            V = nc.vector
            st = Steps(dve, s["dve_s"])
            for counted in (s["qk_ready"], s["qk_ms_ready"], s["dve_qk"], s["m_y"]):
                V.engine_nop().then_inc(counted, 1)
            for counted in y_stored + [s["m_st"]]:
                V.engine_nop().then_inc(counted, 32)
            dve.wait_ge(s["small_loaded"], 16 * SMALL_DMAS)
            for t in range(T):
                dve.wait_ge(s["rs_ready"], t + 1)
                st.did(V.reciprocal(rs[:, t:t + 1], ms[:, t:t + 1]))
                st.settle()
                V.tensor_scalar(xn[:, t, :], x_sb[:, t, :], rs[:, t:t + 1], None, ALU.mult).then_inc(s["xn_ready"], 1)
            for k in range(0, K, 2):
                dve.wait_ge(s["xT_ready"], k + 1)
                V.tensor_scalar(hT[:, k, :], bank[2 + k % 4][:, :], g1c[:, k:k + 1], None, ALU.mult)\
                    .then_inc(s["hT_by_dve"], 1)

            dve.wait_ge(s["small_ready"], 1)
            V.tensor_copy(ki_raw[0:ID, :], bank[6][0:ID, :]).then_inc(s["ki_evicted"], 1)
            V.tensor_copy(gaT[0:RANK, :], bank[6][ID:ID + RANK, :])
            V.tensor_scalar(wiT[0:IH, :], bank[6][ID + 32:ID + 32 + IH, :], float(ID) ** -0.5 * float(IH) ** -0.5,
                            None, ALU.mult).then_inc(s["small_evicted"], 1)
            dve.wait_ge(s["ki_evicted"], 1)
            dve.wait_ge(s["ki_mean_ready"], 1)
            V.tensor_tensor(ki_cen[0:ID, :], ki_raw[0:ID, :], bank[7][0:ID, :], ALU.subtract)\
                .then_inc(s["ki_cen_ready"], 1)
            dve.wait_ge(s["ki_std_ready"], 1)
            st.did(V.reciprocal(ki_raw[0:ID, :], ki_raw[0:ID, :]))
            st.settle()
            dve.wait_ge(s["ki_cen_ready"], 1)
            st.did(V.scalar_tensor_tensor(kiT[0:ID, :], ki_cen[0:ID, :], lngb[:, 0:1], ki_raw[0:ID, :],
                                          ALU.mult, ALU.mult))
            st.settle()
            V.tensor_scalar(kiT[0:ID, :], kiT[0:ID, :], lngb[:, 1:2], None, ALU.add).then_inc(s["kiT_ready"], 1)
            dve.wait_ge(s["wi_ps"], 1)
            V.tensor_copy(wi[:, :, :], bank[7][:, 0:T * IH].rearrange("p (t h) -> p t h", t=T))\
                .then_inc(s["wi_ready"], 1)
            dve.wait_ge(s["wi_ready"], 1)
            u = 0
            for i in range(1, T):
                n = (i + 1) * P
                for h in range(IH):
                    dve.wait_ge(s["relu_ready"], u + 1)
                    if h == 0:
                        V.tensor_scalar(bias[i][:, :], relu[u % 2][:, 0:n], wi[:, i, 0:1], None, ALU.mult)\
                            .then_inc(s["relu_used"], 1)
                    else:
                        dve.wait_ge(s["relu_used"], u)
                        V.scalar_tensor_tensor(bias[i][:, :], relu[u % 2][:, 0:n], wi[:, i, h:h + 1],
                                               bias[i][:, :], ALU.mult, ALU.add).then_inc(s["relu_used"], 1)
                    u += 1
                dve.wait_ge(s["relu_used"], u)
                st.did(V.memset(bias[i][0:CHUNK, n - CHUNK:n], NEG))
            st.settle()

            with dve.Fori(0, 2) as g:
                lp = Steps(dve, s["dve_qk"], g * QK_STEPS + 1)

                def finish_norm(j):
                    dve.wait_ge(s["qk_rms_ready"], g * 8 + (j + 1))
                    lp.settle()
                    lp.did(V.reciprocal(rms[j % 2], rms[j % 2]))
                    lp.settle()
                    tile = qk[:, bass.ds(g * H + j, 1), :].rearrange("p a t -> p (a t)")
                    V.tensor_tensor(tile, tile, rms[j % 2], ALU.mult).then_inc(s["qk_ready"], 1)

                def top_maxima():
                    for i in range(1, T):
                        lp.did(V.max(mx8[:, i, :], bias[i][:, :]))

                def take_maxima():
                    for i in range(1, T):
                        lp.did(V.match_replace(bias[i][:, :], mx8[:, i, :], bias[i][:, :], TAKEN))

                for j in range(8):
                    n = N_Q + j
                    lp.settle()
                    dve.wait_ge(s["qk_sq_ready"], g * 8 + (j + 1))
                    tile = qk[:, bass.ds(g * H + j, 1), :].rearrange("p a t -> p (a t)")
                    V.tensor_scalar(tile, bank[n % 2][:, :], gqk[:, bass.ds(g, 1)], None, ALU.mult)\
                        .then_inc(acc_free[n % 2], 1)
                    if j > 0:
                        take_maxima()
                        dve.wait_ge(acc_free[(n - 1) % 2], g * 4 + ((n - 1) // 2 + 1))
                        finish_norm(j - 1)
                    top_maxima()
                dve.wait_ge(acc_free[(N_Q + 7) % 2], g * 4 + ((N_Q + 7) // 2 + 1))
                finish_norm(7)
                take_maxima()
                assert lp.n == QK_STEPS, lp.n
            dve.wait_ge(s["dve_qk"], 1 + 2 * QK_STEPS)
            for i in range(1, T):
                V.tensor_scalar(bias[i][:, :], bias[i][:, :], TAKEN * 0.5, NEG, ALU.is_ge, ALU.mult)\
                    .then_inc(s["bias_ready"], 1)

            dve.wait_ge(s["gla_loaded"], 48)

            def gate_pre(t):
                dve.wait_ge(s["a_ready"], t + 1)
                st.did(V.tensor_scalar(g_min, bank[2][:, :], 0.0, None, ALU.min))
                st.settle()
                V.scalar_tensor_tensor(g_abs, g_min, 2.0, bank[2][:, :], ALU.mult, ALU.subtract)\
                    .then_inc(s["a_abs"], 1)

            gate_pre(0)
            for t in range(T):
                dve.wait_ge(s["a_exp"], t + 1)
                st.settle()
                V.tensor_tensor(g_log, g_min, g_abs, ALU.subtract).then_inc(s["la_ready"], 1)
                dve.wait_ge(s["kd_ready"], t + 1)
                V.tensor_tensor(gk[:, t, :], gk[:, t, :], g_kd, ALU.mult).then_inc(s["kdec_ready"], 1)
                if t + 1 < T:
                    dve.wait_ge(s["la_ready"], t + 1)
                    dve.wait_ge(s["ind_ready"], t + 1)
                    gate_pre(t + 1)
                for h in range(GH):
                    st.did(V.tensor_tensor(gr[:, t, h * DV:(h + 1) * DV], gr[:, t, h * DV:(h + 1) * DV], gnorm[:, :],
                                           ALU.mult))
                for c in range(2):
                    ch = 2 * t + c
                    dve.wait_ge(s["kv_ready"], ch + 1)
                    dve.wait_ge(s["decay_ready"], t + 1)
                    if ch >= 1:
                        dve.wait_ge(s["state_ready"], ch)
                    if ch >= 2:
                        dve.wait_ge(s["o_ready"], ch - 1)
                    for h in range(GH):
                        kv = bank[5 + h // 2][:, (h % 2) * DV:(h % 2 + 1) * DV]
                        if ch == 0:
                            last = V.tensor_copy(state[c][:, h, :], kv)
                        else:
                            last = V.scalar_tensor_tensor(state[c][:, h, :], state[1 - c][:, h, :],
                                                          decay[:, h, ch:ch + 1], kv, ALU.mult, ALU.add)
                    last.then_inc(s["state_ready"], 1)
                dve.wait_ge(s["oms_ready"], t + 1)
                dve.wait_ge(s["ors_ready"], t + 1)
                st.did(V.tensor_scalar(oms[:, t, :], oms[:, t, :], EPS, -0.5, ALU.add, ALU.mult))
                st.did(V.tensor_tensor(orr[:, :], ors[:, t, :], ors[:, t, :], ALU.mult))
                st.settle()
                st.did(V.tensor_tensor(oms[:, t, :], oms[:, t, :], orr[:, :], ALU.mult))
                st.settle()
                st.did(V.scalar_tensor_tensor(ors[:, t, :], oms[:, t, :], 1.5, ors[:, t, :], ALU.add, ALU.mult))
                st.settle()
                for h in range(GH):
                    last = V.scalar_tensor_tensor(gr[:, t, h * DV:(h + 1) * DV],
                                                  bank[h // 2][:, (h % 2) * DV:(h % 2 + 1) * DV], ors[:, t, h:h + 1],
                                                  gr[:, t, h * DV:(h + 1) * DV], ALU.mult, ALU.mult)
                last.then_inc(s["o_normed"], 1)

            dve.wait_ge(s["bias_ready"], T)
            for u in range(UNITS + 1):
                if u < UNITS:
                    i = u % T
                    n = (i + 1) * P
                    dve.wait_ge(s["logit_ready"], u + 1)
                    if u >= 3:
                        dve.wait_ge(s["pT_ready"], u - 2)
                    st.did(V.tensor_tensor_reduce(out=prob[u % 3][:, 0:n], in0=bank[2 + u % 2][:, 0:n],
                                                  in1=bias[i][:, :], scale=1.0, scalar=2.0 * NEG, op0=ALU.add,
                                                  op1=ALU.max, accum_out=mxl[:, u:u + 1]))
                    st.settle()
                    V.tensor_scalar(nmx[:, u:u + 1], mxl[:, u:u + 1], -float(HD) ** -0.5, None, ALU.mult)\
                        .then_inc(s["lmax_ready"], 1)
                if u >= 1:
                    v = u - 1
                    n = (v % T + 1) * P
                    dve.wait_ge(s["prob_ready"], v + 1)
                    st.did(V.reciprocal(prc[:, v:v + 1], psm[:, v:v + 1]))
                    st.settle()
                    V.tensor_scalar(prob[v % 3][:, 0:n], prob[v % 3][:, 0:n], prc[:, v:v + 1], None, ALU.mult)\
                        .then_inc(s["probn_ready"], 1)

            def sigmoid(f):
                for g in range(2):
                    st.did(V.tensor_scalar(gates[:, g, f, :], gates[:, g, f, :], 1.0, None, ALU.add))
                    st.settle()
                    st.did(V.reciprocal(gates[:, g, f, :], gates[:, g, f, :]))

            for i in range(2):
                dve.wait_ge(acc_free[i], (N_SA + 4 * 4) // 2)
                dve.wait_ge(s["av_done"], UNITS)
                V.engine_nop().then_inc(s["f_free"], 1)
            sigmoid(0)
            for f in range(K):
                b0 = 2 * (f % 2)
                dve.wait_ge(s["f_ready"], f + 1)
                st.settle()
                st.did(V.tensor_tensor(mixT[:, f, :], bank[b0][:, :], gates[:, 0, f, :], ALU.mult))
                V.tensor_tensor(mtmp[f % 2], bank[b0 + 1][:, :], gates[:, 1, f, :], ALU.mult)\
                    .then_inc(s["f_free"], 1)
                st.settle()
                dve.wait_ge(s["f_free"], f + 3)
                V.tensor_tensor(mixT[:, f, :], mixT[:, f, :], mtmp[f % 2], ALU.add).then_inc(s["mix_ready"], 1)
                if f + 1 < K:
                    sigmoid(f + 1)

            dve.wait_ge(s["x_again"], 16)
            dve.wait_ge(s["g2_loaded"], 16)
            for t in range(T):
                for hf in range(2):
                    dve.wait_ge(s["x_out_ready"], 2 * t + hf + 1)
                    V.tensor_tensor(x2[:, t, hf * BLK:(hf + 1) * BLK], bank[4 + 2 * (t % 2) + hf][:, :],
                                    x2[:, t, hf * BLK:(hf + 1) * BLK], ALU.add).then_inc(s["x2_ready"], 1)
                dve.wait_ge(s["h2_rs"], t + 1)
                st.did(V.reciprocal(rs[:, t:t + 1], ms[:, t:t + 1]))
                st.settle()
                dve.wait_ge(s["x2_ready"], 2 * t + 2)
                V.scalar_tensor_tensor(h2s[t % 2], x2[:, t, :], rs[:, t:t + 1], g2b, ALU.mult, ALU.mult)\
                    .then_inc(s["h2_ready"], 1)

            dve.wait_ge(s["lg_ps"], 1)
            for i in range(2):
                dve.wait_ge(h2s_stored[i], 16 * (T // 2))
            lps = bank[3][:, 0:T * (G + NE)].rearrange("p (t n) -> p t n", t=T)
            st.did(V.memset(lg[:, :, :], NEG))
            st.settle()
            st.did(V.tensor_copy(lg[:, :, 0:G], lps[:, :, 0:G]))
            st.did(V.tensor_copy(le[:, :, :], lps[:, :, G:G + NE]))
            st.settle()
            for t in range(T):
                st.did(V.max(v8[:, t, :], lg[:, t, :]))
            st.settle()
            for t in range(T):
                st.did(V.max_index(i8[:, t, :], v8[:, t, :], lg[:, t, :]))
            V.tensor_tensor(tg[:, :, :], lg[:, :, 0:G], v8[:, :, 0:1].to_broadcast([P, T, G]), ALU.subtract)\
                .then_inc(s["gexp_in"], 1)
            st.settle()
            st.did(V.tensor_copy(gid[:, :], i8[:, :, 0]))
            st.settle()
            for t in range(T):
                st.did(V.tensor_scalar(pen[:, t, :], gio[:, :], gid[:, t:t + 1], NEG, ALU.not_equal, ALU.mult))
            st.settle()
            st.did(V.tensor_tensor(le[:, :, :], le[:, :, :], pen[:, :, :], ALU.add))
            st.settle()
            dve.wait_ge(s["gexp_in"], 1)
            for t in range(T):
                st.did(V.max(v8[:, t, :], le[:, t, :]))
            st.settle()
            for t in range(T):
                st.did(V.max_index(i8[:, t, :], v8[:, t, :], le[:, t, :]))
            V.tensor_tensor(wt[:, 1, :], v8[:, :, 1], v8[:, :, 0], ALU.subtract).then_inc(s["eexp_in"], 1)
            st.settle()
            for k in range(TOP_E):
                st.did(V.tensor_copy(eid[:, k, :], i8[:, :, k]))
            st.settle()
            for k in range(TOP_E):
                for t in range(T):
                    st.did(V.tensor_scalar(oh[:, k, t, :], eio[:, :], eid[:, k, t:t + 1], None, ALU.is_equal))
            st.settle()
            V.tensor_tensor(mask_b[:, :, :], oh[:, 0], oh[:, 1], ALU.add).then_inc(s["maskb_ready"], 1)
            dve.wait_ge(s["gexp_out"], 1)
            st.did(V.reduce_sum(gw[:, :], tg[:, :, :], AX))
            dve.wait_ge(s["eexp_out"], 1)
            st.did(V.tensor_scalar(wt[:, 0, :], wt[:, 1, :], 1.0, None, ALU.add))
            st.settle()
            st.did(V.tensor_tensor(gw[:, :], gw[:, :], wt[:, 0, :], ALU.mult))
            st.settle()
            st.did(V.reciprocal(wt[:, 0, :], gw[:, :]))
            st.settle()
            st.did(V.tensor_tensor(wt[:, 1, :], wt[:, 1, :], wt[:, 0, :], ALU.mult))
            dve.wait_ge(s["rank_ready"], 1)
            st.did(V.tensor_copy(cnt[:, :], bank[5][:, 0:NE]))
            st.settle()
            st.did(V.tensor_scalar(more[:, :], cnt[:, :], float(SLOTS), None, ALU.is_gt))
            for m in range(2, MAX_TILES):
                st.settle()
                st.did(V.scalar_tensor_tensor(more[:, :], cnt[:, :], float(SLOTS * m), more[:, :], ALU.is_gt, ALU.add))
            st.did(V.memset(mbase[:, :], 1.0))
            st.settle()
            st.did(V.tensor_tensor_scan(xinc[:, :], mbase[:, :], more[:, :], 0.0, ALU.mult, ALU.add))
            st.settle()
            st.did(V.tensor_tensor(more[:, :], xinc[:, :], more[:, :], ALU.subtract))
            st.settle()
            st.did(V.tensor_scalar(mbase[:, :], more[:, :], float(SLOTS), float(FIRST_MORE - SLOTS), ALU.mult, ALU.add))
            rank = bank[4][:, 0:T * NE].rearrange("p (t e) -> p t e", t=T)
            for k in range(TOP_E):
                st.did(V.tensor_tensor(pen[:, :, :], oh[:, k], rank, ALU.mult))
                st.settle()
                st.did(V.reduce_sum(rk[:, k, :], pen[:, :, :], AX))
                st.settle()
                st.did(V.tensor_tensor(pen[:, :, :], oh[:, k], mbase[:, :].unsqueeze(1).to_broadcast([P, T, NE]),
                                       ALU.mult))
                st.settle()
                st.did(V.reduce_sum(rtmp[:, k, :], pen[:, :, :], AX))
                st.settle()
            st.did(V.tensor_scalar(isov[:, :, :], rk[:, :, :], float(SLOTS), None, ALU.is_ge))
            st.did(V.scalar_tensor_tensor(rowf[:, :, :], eid[:, :, :], float(SLOTS), rk[:, :, :], ALU.mult, ALU.add))
            st.did(V.scalar_tensor_tensor(tabf[:, :, :], rk[:, :, :], float(NE), eid[:, :, :], ALU.mult, ALU.add))
            st.did(V.tensor_tensor(rtmp[:, :, :], rtmp[:, :, :], rk[:, :, :], ALU.add))
            st.settle()
            for dst, src in ((row_i, rowf), (tab_i, tabf)):
                st.did(V.tensor_tensor(oh[:, :, :, 0], rtmp[:, :, :], src[:, :, :], ALU.subtract))
                st.settle()
                st.did(V.tensor_tensor(oh[:, :, :, 0], oh[:, :, :, 0], isov[:, :, :], ALU.mult))
                st.settle()
                st.did(V.tensor_tensor(src[:, :, :], src[:, :, :], oh[:, :, :, 0], ALU.add))
                st.settle()
                last = V.tensor_copy(dst[:, :, :], src[:, :, :])
                if dst is tab_i:
                    last.then_inc(s["tab_ready"], 1)
                else:
                    st.did(last)
            st.did(V.tensor_tensor(own[:, :, :], xinc[:, :].unsqueeze(1).to_broadcast([P, MORE, NE]),
                                   tio[:, :].unsqueeze(2).to_broadcast([P, MORE, NE]), ALU.is_le))
            st.settle()
            st.did(V.reduce_sum(ownf[:, 0:MORE], own[:, :, :], AX))
            st.did(V.tensor_copy(ownf[:, MORE:MORE + 1], xinc[:, NE - 1:NE]))
            st.settle()
            st.did(V.tensor_scalar(ownf[:, 0:MORE], ownf[:, 0:MORE], float(NE - 1), None, ALU.min))
            st.settle()
            V.tensor_copy(own_i[:, :], ownf[:, :]).then_inc(s["own_ready"], 1)

            def evict_gathered(sl, done):
                V.tensor_copy(hTe[sl], bank[4][:, :].rearrange("p (k s) -> p k s", k=K)).then_inc(done, 1)

            def run_expert(e, sl, has_next=True):
                dve.wait_ge(s["silu_ready"], e + 1)
                V.tensor_tensor(hid, silu_g, bank[0][:, HALF:F], ALU.mult).then_inc(s["hid_ready"], 1)
                if has_next:
                    dve.wait_ge(s["xg_T"], e + 2)
                    evict_gathered((sl + 1) % 3, s["he_ready"])

            dve.wait_ge(s["xg_T"], 1)
            evict_gathered(0, s["he_ready"])
            with dve.Fori(0, E3 // 3) as r:
                for sl in range(3):
                    run_expert(r * 3 + sl, sl)
            for sl in range(2):
                run_expert(E3 + sl, sl, has_next=(sl == 0))
            dve.wait_ge(s["own_ready"], 1)
            n_more = dve.value_load(own_i[0:1, MORE:MORE + 1], min_val=0, max_val=MORE)
            with dve.If(n_more > 0):
                with dve.Fori(0, n_more) as t:
                    dve.wait_ge(s["m_T"], t + 1)
                    for hf in range(2):
                        last = V.tensor_copy(hTe[2][:, 4 * hf:4 * hf + 4, :],
                                             bank[3 + hf][:, :].rearrange("p (k s) -> p k s", k=4)[:, :, 0:SLOTS])
                    last.then_inc(s["m_he"], 1)
                    dve.wait_ge(s["m_silu"], t + 1)
                    V.tensor_tensor(hid, silu_g, bank[0][:, HALF:F], ALU.mult).then_inc(s["m_hid"], 1)

            for t in range(T):
                for k in range(TOP_E):
                    dve.wait_ge(yg_loaded[TOP_E * t + k], 16)
                    last = V.scalar_tensor_tensor(x2[:, t, :], yg[TOP_E * t + k], wt[:, k, t:t + 1], x2[:, t, :],
                                                  ALU.mult, ALU.add)
                    if k < TOP_E - 1:
                        st.did(last)
                        st.settle()
                last.then_inc(s["out_ready"], 1)

        @block.gpsimd
        def _(pool):
            Q = nc.gpsimd
            st = Steps(pool, s["pool_s"])

            def step(instruction):
                st.did(instruction)
                st.settle()

            step(Q.memset(gaT[:, :], 1.0))
            Q.memset(wsm[:, :, :], 0.0).then_inc(s["wsm_zeroed"], 1)
            pool.wait_ge(s["wsm_zeroed"], 1)
            def ones_where(tile, value, *selects):
                step(Q.memset(tile, value))
                for base, cm, pattern in selects:
                    step(Q.affine_select(out=tile, in_=tile, compare_op=ALU.is_ge, fill=0.0, base=base,
                                           pattern=pattern, channel_multiplier=cm))

            ones_where(ident[:, :], 1.0, (0, 1, [[-1, P]]), (0, -1, [[1, P]]))
            ones_where(mean_m[:, :], 1.0 / HD)
            ones_where(mean_i[:, :], 1.0 / ID)
            ones_where(one[:, :], 1.0)
            ones_where(eps[:, :], EPS)
            ones_where(ones_b[:, :], 1.0)
            ones_where(before[:, :], 1.0, (-1, -1, [[1, P]]))
            inv = 1.0 / GATE_TEMP
            ones_where(suffix[:, :], inv, (-1, 1, [[-1, P]]))
            step(Q.memset(suffix[CHUNK:P, 0:CHUNK], 0.0))
            ones_where(chunk_of[:, 0:1], inv, (CHUNK - 1, -1, [[0, 1]]))
            ones_where(chunk_of[:, 1:2], inv, (-CHUNK, 1, [[0, 1]]))
            step(Q.memset(zero_i[:, :], 0))
            step(Q.memset(bias0[:, :], 0.0))
            Q.memset(bias0[0:CHUNK, CHUNK:P], NEG).then_inc(s["bias_ready"], 1)
            step(Q.iota(tokid[:, :], pattern=[[P, T]], base=0, channel_multiplier=1))
            step(Q.iota(eio[:, :], pattern=[[1, NE]], base=0, channel_multiplier=0,
                          allow_small_or_imprecise_dtypes=True))
            step(Q.iota(gio[:, :].rearrange("p (g e) -> p g e", g=G), pattern=[[1, G], [0, EPG]], base=0,
                          channel_multiplier=0, allow_small_or_imprecise_dtypes=True))
            step(Q.iota(tio[:, :], pattern=[[1, MORE]], base=0, channel_multiplier=0,
                          allow_small_or_imprecise_dtypes=True))
            pool.engine_nop().then_inc(s["consts_done"], 1)
            tab = row_token.rearrange("(p n) a -> p (n a)", p=SLOTS)
            pool.dma_start(tab, zero_i[0:SLOTS, :]).then_inc(s["table_zero"], 16)
            with nc.allow_non_contiguous_dma(reason="the routers' columns"):
                pool.dma_start(wr[:, :, G:G + NE], w_router_expert[0].rearrange("(k p) n -> p k n", p=P))\
                    .then_inc(s["wr_loaded"], 16)
            pool.wait_ge(s["relu_used"], (T - 1) * IH)
            pool.dma_start(wa2[0:RANK, :], gla_w_a2[0]).then_inc(s["gla_loaded"], 16)
            pool.dma_start(wa2[RANK:RANK + 1, :], gla_b_a).then_inc(s["gla_loaded"], 16)
            pool.dma_start(gnorm[:, :], gla_norm_g[0].partition_broadcast(P)).then_inc(s["gla_loaded"], 16)
            step(Q.memset(zrow, 0.0))
            zp = (ROWS - FIRST_MORE) // 8
            pool.dma_start(y_rows[FIRST_MORE:ROWS].rearrange("(p r) d -> p r d", r=8),
                           zrow[0:zp].unsqueeze(1).to_broadcast([zp, 8, D])).then_inc(s["rows_zeroed"], 16)
            pool.wait_ge(s["mix_ready"], K)
            pool.wait_ge(s["rows_zeroed"], 16)
            pool.dma_start(g2b, norm2_g[0].partition_broadcast(P)).then_inc(s["g2_loaded"], 16)

            pool.wait_ge(s["table_zero"], 16)
            pool.wait_ge(s["tab_ready"], 1)
            for k in range(TOP_E):
                for t in range(T):
                    pool.indirect_dma_start(
                        out=row_token, out_offset=bass.IndirectOffsetOnAxis(ap=tab_i[:, k, t:t + 1], axis=0),
                        in_=tokid[:, t:t + 1], in_offset=None, bounds_check=ROWS - 1, oob_is_err=False)\
                        .then_inc(s["scattered"], 16)
            pool.wait_ge(s["scattered"], 16 * TOP_E * T)
            pool.dma_start(idx_all[:, :], row_token[0:FIRST_MORE].rearrange("(r e) a -> r (e a)", e=NE))\
                .then_inc(s["idx_loaded"], 16)
            pool.wait_ge(s["idx_loaded"], 16)
            for i in range(2):
                pool.wait_ge(h2s_stored[i], 16 * (T // 2))

            def gather(sl, tokens, done):
                pool.indirect_dma_start(
                    out=xg[sl][0:SLOTS, :], out_offset=None, in_=h2_rows,
                    in_offset=bass.IndirectOffsetOnAxis(ap=tokens, axis=0),
                    bounds_check=S - 1, oob_is_err=False).then_inc(done, 16)

            pool.wait_ge(s["lgT_ready"], 1)
            for e in range(NE):
                if e >= 3:
                    pool.wait_ge(s["xg_T"], e - 2)
                gather(e % 3, idx_all[:, e:e + 1], xg_loaded[e % 3])
            pool.wait_ge(s["own_ready"], 1)
            n_more = pool.value_load(own_i[0:1, MORE:MORE + 1], min_val=0, max_val=MORE)
            with pool.If(n_more > 0):
                pool.wait_ge(s["xg_T"], NE)
            for t in range(MORE):
                with pool.If(n_more > t):
                    if t >= 1:
                        pool.wait_ge(s["m_T"], t)
                    pool.dma_start(idx_more[:, :], row_token[FIRST_MORE + t * SLOTS:FIRST_MORE + (t + 1) * SLOTS, :])\
                        .then_inc(s["m_idx"], 16)
                    pool.wait_ge(s["m_idx"], 16 * (t + 1))
                    gather(0, idx_more[:, :], s["m_xg"])
            with pool.If(n_more > 0):
                pool.wait_ge(s["m_st"], n_more * 32 + 32)
            for sl in range(3):
                pool.wait_ge(y_stored[sl], 32 * (1 + E3 // 3 + (1 if sl < NE % 3 else 0)))
            for t in range(T):
                for k in range(TOP_E):
                    pool.indirect_dma_start(
                        out=yg[TOP_E * t + k], out_offset=None, in_=y_rows,
                        in_offset=bass.IndirectOffsetOnAxis(ap=row_i[:, k, t:t + 1], axis=0),
                        bounds_check=ROWS - 1, oob_is_err=False).then_inc(yg_loaded[TOP_E * t + k], 16)


_NAMES = ['x', 'norm1_g', 'w_in', 'gla_w_a2', 'gla_b_a', 'gla_norm_g', 'dsa_q_norm_g', 'dsa_k_norm_g',
          'idx_k_ln_g', 'idx_k_ln_b', 'w_branch_gla', 'w_branch_dsa', 'w_out', 'norm2_g',
          'w_router_group', 'b_router_group', 'w_router_expert', 'b_router_expert',
          'w_exp_gate', 'w_exp_up', 'w_exp_down']


def kernel(**inputs):
    import concourse.bacc as bacc
    from concourse.bass_utils import run_bass_kernel_spmd

    nc = bacc.Bacc("TRN2", target_bir_lowering=False, num_devices=1)
    arrays, args = {}, []
    for name in _NAMES:
        a = np.ascontiguousarray(inputs[name])
        arrays[name + "_in"] = a
        args.append(nc.dram_tensor(name + "_in", a.shape, mybir.dt.from_np(a.dtype), kind="ExternalInput").ap())
    shape = arrays["x_in"].shape
    args.append(nc.dram_tensor("out_rows", shape, F32, kind="ExternalOutput").ap())
    encoder_block(nc, *args)
    r = run_bass_kernel_spmd(nc, [arrays], core_ids=[0])
    return r.results[0]["out_rows"]
```

```python
from contextlib import ExitStack

import numpy as np

import concourse.bass as bass
from concourse import mybir

ALU = mybir.AluOpType
ACT = mybir.ActivationFunctionType
F32 = mybir.dt.float32
F32R = mybir.dt.float32r
BF16 = mybir.dt.bfloat16
I32 = mybir.dt.int32
U32 = mybir.dt.uint32
AX = mybir.AxisListType.X

P = 128
CHUNK = 64
EPS = 1e-6
GATE_TEMP = 16.0
TOPK_MAX = 256
TOP_E = 2
SLOTS = 64
NEG = -1.0e30
TAKEN = -3.0e38
PIECE = 4096


class Steps:

    def __init__(self, eng, sem, base=0):
        self.eng, self.sem, self.base, self.n = eng, sem, base, 0

    def did(self, instruction):
        instruction.then_inc(self.sem, 1)
        self.n += 1
        return self.n

    def settle(self, n=None):
        self.eng.wait_ge(self.sem, self.base + (self.n if n is None else n))


def encoder_block(nc, x, norm1_g, w_in, gla_w_a2, gla_b_a, gla_norm_g, dsa_q_norm_g, dsa_k_norm_g,
                  idx_k_ln_g, idx_k_ln_b, w_branch_gla, w_branch_dsa, w_out, norm2_g,
                  w_router_group, b_router_group, w_router_expert, b_router_expert,
                  w_exp_gate, w_exp_up, w_exp_down, out):
    _, S, D = x.shape
    RANK = gla_w_a2.shape[1]
    DK = D // 2 // 4
    DV = gla_norm_g.shape[1]
    GH = D // DV
    HD = dsa_q_norm_g.shape[1]
    H = D // HD
    ID = idx_k_ln_g.shape[1]
    G = w_router_group.shape[2]
    NE = w_router_expert.shape[2]
    EPG = NE // G
    F = w_exp_gate.shape[3]
    IH = (w_in.shape[2] - (2 * GH * DK + 2 * D + RANK + 3 * D + ID + 2 * D)) // (ID + 1)
    TOPK = min(TOPK_MAX, S // 4)
    T = S // P
    K = D // P
    NCH = S // CHUNK
    BLK = 512
    HALF = F // 2
    assert (S, D, F, BLK, HD, DK, TOPK) == (512, 1024, 512, 512, P, P, P) and IH == 8 and ID == 64

    widths = [GH * DK, GH * DK, D, RANK, D, D, D, D, IH * ID, ID, IH, D, D]
    offs = [int(v) for v in np.cumsum([0] + widths)]
    O_GQ, O_GK, O_GV, O_GA, O_GR, O_DQ, O_DK, O_DV, O_IQ, O_IK, O_IW, O_SA, O_SB = offs[:13]
    assert O_DK == O_DQ + D and O_SB == O_SA + D

    PAIRS = S * TOP_E
    MORE = (PAIRS - 1) // SLOTS
    ROWS = (NE + MORE) * SLOTS
    FIRST_MORE = NE * SLOTS
    MAX_TILES = S // SLOTS

    xd = x[0].rearrange("(t p) d -> p t d", p=P)
    outd = out[0].rearrange("(t p) d -> p t d", p=P)
    wind = w_in[0].rearrange("(k p) n -> p k n", p=P)
    pad_ = w_branch_gla[0].rearrange("(k p) n -> p k n", p=P)
    pbd_ = w_branch_dsa[0].rearrange("(k p) n -> p k n", p=P)
    woutd = w_out[0].rearrange("(k p) n -> p k n", p=P)
    h2_rows = nc.dram_tensor("h2_rows", (S, D), F32).ap()
    y_rows = nc.dram_tensor("y_rows", (ROWS, D), F32).ap()
    row_token = nc.dram_tensor("row_token", (ROWS, 1), I32).ap()
    wgd = w_exp_gate[0].rearrange("e (k p) f -> e p k f", p=P)
    wud = w_exp_up[0].rearrange("e (k p) f -> e p k f", p=P)
    wdd = w_exp_down[0].rearrange("e (k p) d -> e p k d", p=P)

    with ExitStack() as ctx:
        def sem(name):
            return ctx.enter_context(nc.semaphore(name))

        def sb(name, shape, dt=F32):
            return ctx.enter_context(nc.sbuf_tensor(name, shape, dt))

        arena_at = (nc.sbuf_base + 31) // 32 * 32
        arena = sb("arena", [P, 11 * PIECE])
        work = sb("work", [P, PIECE])
        as_f32r = {i: nc.alloc_sbuf_tensor_at(f"piece{i}_r", [P, PIECE], F32R, offset=arena_at + 4 * PIECE * i)
                   for i in (0, 1, 2, 7, 9, 10, 11)}
        bank = [ctx.enter_context(nc.psum_tensor(f"bank{i}", [P, 512], F32)) for i in range(8)]

        def piece(i, n=1, words=None, off=0):
            return arena[:, i * PIECE + off:i * PIECE + off + (words or n * PIECE - off)]

        def piece_r(i, words=PIECE, off=0):
            return as_f32r[i][:, off:off + words]

        hT_hi, hT_lo = [piece_r(i).rearrange("p (k t) -> p k t", k=K) for i in (0, 7)]
        w_raw = [piece(1, words=2048, off=2048 * i).rearrange("p (k n) -> p k n", k=K) for i in range(2)]
        w_lo = [piece_r(1, words=2048, off=2048 * i).rearrange("p (k n) -> p k n", k=K)
                for i in range(2)]
        w_hi = [piece_r(2, words=2048, off=2048 * i).rearrange("p (k n) -> p k n", k=K)
                for i in range(2)]
        qk = piece(3, 2).rearrange("p (h t) -> p h t", h=2 * H)
        gr, gv = [piece(i).rearrange("p (t d) -> p t d", t=T) for i in (5, 6)]
        dv = piece(6).rearrange("p (t d) -> p t d", t=T)
        gqT = piece(8, words=2048).rearrange("p (h t) -> p h t", h=GH)
        gk = piece(8, words=2048, off=2048).rearrange("p (t n) -> p t n", t=T)
        gates = [piece(i).rearrange("p (j t) -> p j t", j=K) for i in (5, 8)]
        wout_sb = [piece(i).rearrange("p (k n) -> p k n", k=K) for i in (4, 6)]
        mixT = piece(3).rearrange("p (k t) -> p k t", k=K)
        x_sb = piece(9).rearrange("p (t d) -> p t d", t=T)
        AT, BT = [piece(i).rearrange("p (k t) -> p k t", k=K) for i in (9, 10)]
        AT_lo, BT_lo = [piece_r(i).rearrange("p (k t) -> p k t", k=K) for i in (9, 10)]
        AT_hi, BT_hi = [piece_r(i).rearrange("p (k t) -> p k t", k=K) for i in (0, 7)]
        h2T = piece(9).rearrange("p (k t) -> p k t", k=K)
        xn = piece(10).rearrange("p (t d) -> p t d", t=T)
        qiT = piece(10).rearrange("p (h t) -> p h t", h=IH)
        x2 = piece(10).rearrange("p (t d) -> p t d", t=T)
        def m2(off, words):
            return work[:, off:off + words]
        SMALL = ID + 32 + IH
        wsm = m2(0, K * SMALL).rearrange("p (k n) -> p k n", k=K)
        wsm_lo = piece_r(11, K * SMALL).rearrange("p (k n) -> p k n", k=K)
        wsm_hi = piece_r(11, K * SMALL, K * SMALL).rearrange("p (k n) -> p k n", k=K)
        ki_raw, ki_cen, ki_sq = m2(832, 512), m2(1344, 512), m2(1856, 512)
        kiT = m2(2368, 512)
        relu = [m2(2880, 512), m2(832, 512)]
        wiT = m2(2880, 512)
        g_abs, g_min, g_log, g_kd = [piece(9, words=512, off=512 * i) for i in range(4)]
        wa2 = piece(9, words=GH * DK, off=2048)
        sq = [m2(0, 512), m2(512, 512)]
        rms = [m2(1024, 512), m2(1536, 512)]
        state = [piece(10, words=1024, off=1024 * i).rearrange("p (h v) -> p h v", h=GH) for i in range(2)]
        oscr = [m2(2816 + DV * i, DV) for i in range(GH)]
        gnorm = m2(3840, DV)
        prob = [m2(512 * i, 512) for i in range(3)]
        probT = [m2(1536 + 512 * i, 512) for i in range(3)]
        zrow = m2(3072, D)
        mtmp = [m2(512 * i, 512) for i in range(2)]
        h2s = [m2(1024 * i, 1024) for i in range(2)]
        g2b = m2(2048, 1024)
        lgT = m2(3072, 512)
        le = m2(0, T * NE).rearrange("p (t e) -> p t e", t=T)
        pen = m2(128, T * NE).rearrange("p (t e) -> p t e", t=T)
        oh = m2(256, TOP_E * T * NE).rearrange("p (k t e) -> p k t e", k=TOP_E, t=T)
        cnt, more, xinc, mbase = [m2(1024 + NE * i, NE) for i in range(4)]
        own = m2(512, MORE * NE).rearrange("p (m e) -> p m e", m=MORE)
        slot_pieces = [(0, 5, 8), (1, 7, 6), (2, 3, 4)]
        wgu, wdn = [], []
        for a, b, c in slot_pieces:
            both = arena[:, a * PIECE:(b + 1) * PIECE]
            wgu.append((piece(a).rearrange("p (k f) -> p k f", k=K), piece(b).rearrange("p (k f) -> p k f", k=K),
                        both.rearrange("p (q w) -> p q w", w=PIECE)[:, ::(b - a), :].rearrange(
                            "p q (k f) -> p q k f", k=K)))
            wdn.append(piece(c).rearrange("p (k d) -> p k d", k=F // P))
        xg = [arena[:, 9 * PIECE + 1024 * i:9 * PIECE + 1024 * (i + 1)] for i in range(3)]
        hTe = [m2(512 * i, 512).rearrange("p (k s) -> p k s", k=K) for i in range(3)]
        silu_g, hid = m2(1536, 256), m2(1792, 256)
        hidT = m2(2048, 256).rearrange("p (c h s) -> p c h s", c=2, h=2)
        y_sb = [m2(2304 + 512 * i, 512) for i in range(3)]
        yg = [arena[:, 1024 * i:1024 * (i + 1)] for i in range(TOP_E * T)]

        ident = sb("ident", [P, P])
        mean_m = sb("mean_m", [P, P])
        mean_i = sb("mean_i", [ID, ID])
        suffix = sb("suffix", [P, P])
        chunk_of = sb("chunk_of", [P, 2])
        before = sb("before", [P, P], BF16)
        ones_b = sb("ones_b", [P, P], BF16)
        one = sb("one", [P, 1])
        eps = sb("eps", [P, 1])
        zero_i = sb("zero_i", [P, ROWS // SLOTS], I32)
        bias0 = sb("bias0", [P, P])
        bias = [bias0] + [sb(f"bias{i}", [P, (i + 1) * P]) for i in range(1, T)]
        gaT = sb("gaT", [32, S])
        g1c = sb("g1c", [P, K])
        gqk = sb("gqk", [P, 2])
        lngb = sb("lngb", [ID, 2])
        wi = sb("wi", [P, T, IH])
        ms = sb("ms", [P, T])
        rs = sb("rs", [P, T])
        mx8 = sb("mx8", [P, T, 8])
        decay = sb("decay", [P, GH, NCH])
        oms = sb("oms", [P, T, GH])
        ors = sb("ors", [P, T, GH])
        orr = sb("orr", [P, GH])
        nmx = sb("nmx", [P, T * H])
        mxl = sb("mxl", [P, T * H])
        psm = sb("psm", [P, T * H])
        prc = sb("prc", [P, T * H])
        brt = sb("brt", [G + NE, 1])
        wr = sb("wr", [P, K, G + NE])
        tokid = sb("tokid", [P, T], I32)
        eio = sb("eio", [P, NE])
        gio = sb("gio", [P, NE])
        tio = sb("tio", [P, MORE])
        lg = sb("lg", [P, T, 8])
        tg = sb("tg", [P, T, G])
        v8 = sb("v8", [P, T, 8])
        i8 = sb("i8", [P, T, 8], U32)
        gid = sb("gid", [P, T])
        gw = sb("gw", [P, T])
        eid = sb("eid", [P, TOP_E, T])
        wt = sb("wt", [P, TOP_E, T])
        mask_b = sb("mask_b", [P, T, NE], BF16)
        rk = sb("rk", [P, TOP_E, T])
        rtmp = sb("rtmp", [P, TOP_E, T])
        isov = sb("isov", [P, TOP_E, T])
        rowf = sb("rowf", [P, TOP_E, T])
        tabf = sb("tabf", [P, TOP_E, T])
        row_i = sb("row_i", [P, TOP_E, T], I32)
        tab_i = sb("tab_i", [P, TOP_E, T], I32)
        ownf = sb("ownf", [P, MORE + 1])
        own_i = sb("own_i", [P, MORE + 1], I32)
        idx_all = sb("idx_all", [SLOTS, NE], I32)
        idx_more = sb("idx_more", [SLOTS, 1], I32)

        names = """consts_done small_loaded wsm_zeroed ms_ready xn_ready xT_ready hT_hi_ready hT_lo_ready wsm_hi_ready wsm_lo_ready whi_ready wlo_ready AT_hi_ready AT_lo_ready BT_hi_ready BT_lo_ready wout_loaded
            acc_ready small_ready ki_evicted small_evicted ki_mean_ready ki_cen_ready ki_sq_ready ki_var_ready
            kiT_ready wi_ps wi_ready qiT_ready idx_logit_ready relu_ready relu_used
            qk_sq_ready qk_ms_ready qk_rms_ready qk_ready bias_ready
            gv_ready a_ready a_abs a_exp la_ready suf_ready kd_ready kdec_ready ind_ready decay_ready kv_ready
            state_ready o_ready oms_ready o_normed oT_ready AT_ready
            logit_ready lmax_ready prob_ready probn_ready pT_ready pT_evicted av_done BT_ready
            gates_ready f_free f_ready mix_ready x_again x_out_ready x2_ready h2_ms h2_ready h2_stored h2T_ps h2T_ready
            lgT_ps lgT_ready lg_ps gexp_in gexp_out eexp_in eexp_out maskb_ready rank_ready tab_ready
            table_zero scattered idx_loaded own_ready
            wring_free xg_T he_ready gu_ready silu_ready hid_ready hidT_ps hidT_ready y_ready
            m_w m_idx m_xg m_T m_he m_gu m_silu m_hid m_hT m_hTs m_y m_st
            wr_loaded rows_zeroed oln_ready rs_ready ki_std_ready ors_ready h2_rs gla_loaded g2_loaded out_ready out_stored dve_s act_s pool_s""".split()
        s = {n: sem(n) for n in names}
        acc_free = [sem(f"acc_free{i}") for i in range(2)]
        x_loaded = [sem(f"x_loaded{i}") for i in range(T)]
        w_loaded = [sem(f"w_loaded{i}") for i in range(4)]
        wgu_loaded = [sem(f"wgu_loaded{i}") for i in range(3)]
        wdn_loaded = [sem(f"wdn_loaded{i}") for i in range(3)]
        xg_loaded = [sem(f"xg_loaded{i}") for i in range(3)]
        y_stored = [sem(f"y_stored{i}") for i in range(3)]
        yg_loaded = [sem(f"yg_loaded{i}") for i in range(TOP_E * T)]
        h2s_stored = [sem(f"h2s_stored{i}") for i in range(2)]

        B_IQ, B_GQ, B_GK, B_GV, B_GR, B_Q, B_DV, B_SA, B_END = 0, 1, 2, 3, 5, 7, 11, 13, 17
        TOKEN_BLOCKS = (B_GK, B_GV, B_GV + 1, B_GR, B_GR + 1, B_DV, B_DV + 1)
        N_IQ, N_GQ, N_GK, N_GV, N_GR, N_Q, N_DV, N_SA, N_END = [
            4 * b for b in (B_IQ, B_GQ, B_GK, B_GV, B_GR, B_Q, B_DV, B_SA, B_END)]
        Q_P = N_END
        Q_END = Q_P + 2 * K

        def quarter(ring, q):
            return ring[q // 2 % 2][:, :, q % 2 * P:(q % 2 + 1) * P]

        def freed_by(q):
            return q // 2 * 2 + 2 if q // 4 in TOKEN_BLOCKS else q + 1

        E3 = NE - NE % 3
        assert NE % 3 == 2
        UNITS = H * T
        SMALL_DMAS = 11

        def gate_tiles(u):
            return [n for n in range(2 * K) if n * 3 // 2 == u]


        block = ctx.enter_context(nc.Block())

        @block.sync
        def _(sp):
            def load_quarter(q, src):
                sp.dma_start(quarter(w_raw, q), src).then_inc(w_loaded[q % 4], 16)

            for b, off in zip(range(B_END), (O_IQ, O_GQ, O_GK, O_GV, O_GV + BLK, O_GR, O_GR + BLK,
                                             O_DQ, O_DQ + BLK, O_DK, O_DK + BLK, O_DV, O_DV + BLK,
                                             O_SA, O_SA + BLK, O_SB, O_SB + BLK)):
                for q in range(4 * b, 4 * b + 4):
                    if q >= 4:
                        sp.wait_ge(s["acc_ready"], freed_by(q - 4))
                    load_quarter(q, wind[:, :, off + q % 4 * P:off + (q % 4 + 1) * P])
            for f in range(2):
                for i, src in enumerate((pad_, pbd_)):
                    sp.wait_ge(s["acc_ready"], freed_by(Q_P + 2 * f + i - 4))
                    load_quarter(Q_P + 2 * f + i, src[:, :, f * P:(f + 1) * P])
            sp.wait_ge(s["logit_ready"], UNITS)
            sp.dma_start(wout_sb[0], woutd[:, :, 0:BLK]).then_inc(s["wout_loaded"], 16)
            sp.wait_ge(s["av_done"], UNITS)
            sp.dma_start(wout_sb[1], woutd[:, :, BLK:D]).then_inc(s["wout_loaded"], 16)
            with sp.Fori(0, K // 2 - 1) as g:
                for j in range(2):
                    sp.wait_ge(s["f_ready"], g * 2 + (j + 1))
                    for i, src in enumerate((pad_, pbd_)):
                        load_quarter(Q_P + 2 * j + i, src[:, :, bass.ds(g * (2 * P) + (j + 2) * P, P)])
            sp.wait_ge(s["f_ready"], K)
            sp.dma_start(x2, xd).then_inc(s["x_again"], 16)

            def expert(dram, e):
                return dram[bass.ds(e, 1)].rearrange("e p k f -> p (e k) f")

            def load_up(e, sl):
                sp.dma_start(wgu[sl][0], expert(wgd, e)).then_inc(wgu_loaded[sl], 16)
                sp.dma_start(wgu[sl][1], expert(wud, e)).then_inc(wgu_loaded[sl], 16)

            def load_down(e, sl):
                sp.dma_start(wdn[sl], expert(wdd, e)).then_inc(wdn_loaded[sl], 16)

            sp.wait_ge(s["mix_ready"], K)
            load_up(0, 0)
            load_down(0, 0)
            load_up(1, 1)
            sp.wait_ge(s["x_out_ready"], 2 * T)
            load_down(1, 1)
            load_up(2, 2)
            load_down(2, 2)
            with sp.Fori(3, E3, 3) as e:
                for sl in range(3):
                    sp.wait_ge(s["gu_ready"], e + (sl - 2))
                    load_up(e + sl, sl)
                    sp.wait_ge(s["y_ready"], e + (sl - 2))
                    load_down(e + sl, sl)
            for sl in range(2):
                sp.wait_ge(s["gu_ready"], E3 + sl - 2)
                load_up(E3 + sl, sl)
                sp.wait_ge(s["y_ready"], E3 + sl - 2)
                load_down(E3 + sl, sl)
            sp.wait_ge(s["own_ready"], 1)
            n_more = sp.value_load(own_i[0:1, MORE:MORE + 1], min_val=0, max_val=MORE)
            with sp.If(n_more > 0):
                sp.wait_ge(s["y_ready"], NE)
                with sp.Fori(0, n_more) as t:
                    e = sp.value_load(own_i[0:1, bass.ds(t, 1)], min_val=0, max_val=NE - 1)
                    sp.wait_ge(s["m_y"], t + 1)
                    sp.dma_start(wgu[2][0], expert(wgd, e)).then_inc(s["m_w"], 16)
                    sp.dma_start(wgu[2][1], expert(wud, e)).then_inc(s["m_w"], 16)
                    sp.dma_start(wdn[2], expert(wdd, e)).then_inc(s["m_w"], 16)

        @block.tensor
        def _(pe):
            mm, tr = nc.tensor.matmul, nc.tensor.transpose

            def begin(n):
                if n >= 2:
                    pe.wait_ge(acc_free[n % 2], n // 2)

            def feature_tile(n):
                begin(n)
                pe.wait_ge(s["whi_ready"], n + 1)
                hi, lo = quarter(w_hi, n), quarter(w_lo, n)
                for w, h in ((hi, hT_hi), (hi, hT_lo), (lo, hT_hi)):
                    if w is lo:
                        pe.wait_ge(s["wlo_ready"], n + 1)
                    for k in range(K):
                        last = mm(bank[n % 2][:, :], w[:, k, :], h[:, k, :],
                                  start=(w is hi and h is hT_hi and k == 0), stop=(w is lo and k == K - 1))
                last.then_inc(s["acc_ready"], 1)

            def token_tile(n):
                begin(n)
                q = n // 2 * 2
                pe.wait_ge(s["whi_ready"], q + 2)
                hi, lo = w_hi[q // 2 % 2], w_lo[q // 2 % 2]
                for i in range(2):
                    t = 2 * (n % 2) + i
                    for h, w in ((hT_hi, hi), (hT_lo, hi), (hT_hi, lo)):
                        if w is lo:
                            pe.wait_ge(s["wlo_ready"], q + 2)
                        for k in range(K):
                            last = mm(bank[n % 2][:, i * 2 * P:(i + 1) * 2 * P], h[:, k, t * P:(t + 1) * P], w[:, k, :],
                                      start=(w is hi and h is hT_hi and k == 0), stop=(w is lo and k == K - 1))
                last.then_inc(s["acc_ready"], 1)

            pe.wait_ge(s["consts_done"], 1)
            pe.wait_ge(s["xn_ready"], T)
            for k in range(K):
                if k >= 4:
                    pe.wait_ge(s["hT_lo_ready"], k - 3)
                for t in range(T):
                    last = tr(bank[2 + k % 4][:, t * P:(t + 1) * P], xn[:, t, k * P:(k + 1) * P], ident[:, :])
                last.then_inc(s["xT_ready"], 1)

            pe.wait_ge(s["hT_hi_ready"], K)
            pe.wait_ge(s["wsm_lo_ready"], 1)
            for w, h in ((wsm_hi, hT_hi), (wsm_lo, hT_hi), (wsm_hi, hT_lo)):
                if h is hT_lo:
                    pe.wait_ge(s["hT_lo_ready"], K)
                for k in range(K):
                    last = mm(bank[6][0:SMALL, :], w[:, k, :], h[:, k, :],
                              start=(w is wsm_hi and h is hT_hi and k == 0), stop=(h is hT_lo and k == K - 1))
            last.then_inc(s["small_ready"], 1)
            for c in range(4):
                feature_tile(N_IQ + c)
                if c == 0:
                    pe.wait_ge(s["ki_evicted"], 1)
                    mm(bank[7][0:ID, :], mean_i[:, :], ki_raw[0:ID, :], start=True, stop=True)\
                        .then_inc(s["ki_mean_ready"], 1)
                if c == 1:
                    pe.wait_ge(s["small_evicted"], 1)
                    pe.wait_ge(s["ki_sq_ready"], 1)
                    mm(bank[6][0:ID, :], mean_i[:, :], ki_sq[0:ID, :], start=True, stop=True)\
                        .then_inc(s["ki_var_ready"], 1)
                if c == 2:
                    pe.wait_ge(s["ki_cen_ready"], 1)
                    for t in range(T):
                        last = tr(bank[7][:, t * IH:(t + 1) * IH], wiT[0:IH, t * P:(t + 1) * P], ident[0:IH, 0:IH])
                    last.then_inc(s["wi_ps"], 1)

            def index_logits(u):
                i, h = u // IH + 1, u % IH
                n = (i + 1) * P
                if u >= 4:
                    pe.wait_ge(s["relu_ready"], u - 3)
                mm(bank[2 + u % 4][:, 0:n], qiT[0:ID, h, i * P:(i + 1) * P], kiT[0:ID, 0:n],
                   start=True, stop=True).then_inc(s["idx_logit_ready"], 1)

            for n in range(N_GQ, N_GV):
                (feature_tile if n < N_GK else token_tile)(n)
                if n == N_GQ:
                    for i in range(2):
                        pe.wait_ge(acc_free[i], (N_IQ + 4) // 2)
                    pe.wait_ge(s["kiT_ready"], 1)
                for u in range(3 * (n - N_GQ), 3 * (n - N_GQ) + 3):
                    index_logits(u)

            def gate_product(t):
                mm(bank[2][:, :], gaT[0:RANK + 1, t * P:(t + 1) * P], wa2[0:RANK + 1, :], start=True, stop=True)\
                    .then_inc(s["a_ready"], 1)

            for n in range(N_GV, N_GR):
                token_tile(n)
                t = n - N_GV - 1
                if t == -1:
                    pe.wait_ge(s["relu_ready"], (T - 1) * IH)
                    pe.wait_ge(s["gla_loaded"], 48)
                    pe.wait_ge(s["small_evicted"], 1)
                    gate_product(0)
                elif t < T:
                    pe.wait_ge(s["la_ready"], t + 1)
                    if t >= 1:
                        pe.wait_ge(s["kd_ready"], t)
                    mm(bank[3][:, :], suffix[:, :], g_log, start=True, stop=True).then_inc(s["suf_ready"], 1)
                    if t >= 1:
                        pe.wait_ge(s["decay_ready"], t)
                    for h in range(GH):
                        last = mm(bank[4][:, 2 * h:2 * h + 2], g_log[:, h * DK:(h + 1) * DK], chunk_of[:, :],
                                  start=True, stop=True)
                    last.then_inc(s["ind_ready"], 1)
                    if t + 1 < T:
                        gate_product(t + 1)
            for n in range(N_GR, N_Q):
                token_tile(n)

            def mean_square(j):
                pe.wait_ge(s["qk_sq_ready"], j + 1)
                if j >= 1:
                    pe.wait_ge(s["qk_rms_ready"], j)
                mm(bank[2][:, :], mean_m[:, :], sq[j % 2], start=True, stop=True).then_inc(s["qk_ms_ready"], 1)

            def chunk_kv(ch):
                t, rows = ch // 2, slice(ch % 2 * CHUNK, (ch % 2 + 1) * CHUNK)
                pe.wait_ge(s["kdec_ready"], t + 1)
                if ch == 0:
                    for i in range(2):
                        pe.wait_ge(acc_free[i], (N_DV - 4 * 4) // 2)
                if ch >= 1:
                    pe.wait_ge(s["state_ready"], ch)
                for h in range(GH):
                    last = mm(bank[5 + h // 2][:, (h % 2) * DV:(h % 2 + 1) * DV],
                              gk[rows, t, h * DK:(h + 1) * DK], gv[rows, t, h * DV:(h + 1) * DV],
                              start=True, stop=True)
                last.then_inc(s["kv_ready"], 1)

            def chunk_out(ch):
                t, rows = ch // 2, slice(ch % 2 * CHUNK, (ch % 2 + 1) * CHUNK)
                pe.wait_ge(s["state_ready"], ch + 1)
                if ch % 2 == 0 and t >= 1:
                    pe.wait_ge(s["o_normed"], t)
                for h in range(GH):
                    last = mm(bank[3 + h // 2][rows, (h % 2) * DV:(h % 2 + 1) * DV],
                              gqT[:, h, ch * CHUNK:(ch + 1) * CHUNK], state[ch % 2][:, h, :],
                              start=True, stop=True)
                last.then_inc(s["o_ready"], 1)

            def out_transposes(t, hf):
                pe.wait_ge(s["o_normed"], t + 1)
                if t or hf:
                    pe.wait_ge(s["AT_ready"], 2 * t + hf)
                for k in range(4):
                    last = tr(bank[7][:, k * P:(k + 1) * P], gr[:, t, (4 * hf + k) * P:(4 * hf + k + 1) * P],
                              ident[:, :])
                last.then_inc(s["oT_ready"], 1)

            for j in range(2 * H):
                feature_tile(N_Q + j)
                if j > 0:
                    mean_square(j - 1)
                t, r = divmod(j, 4)
                if r == 0:
                    chunk_kv(2 * t)
                if r == 1:
                    chunk_out(2 * t)
                    chunk_kv(2 * t + 1)
                if r == 2:
                    chunk_out(2 * t + 1)
                if r in (1, 2) and t >= 1:
                    out_transposes(t - 1, r - 1)

            for n in range(N_DV, N_SA):
                token_tile(n)
                if n == N_DV:
                    mean_square(2 * H - 1)
                if n in (N_DV + 1, N_DV + 2):
                    out_transposes(T - 1, n - N_DV - 1)

            def logits(u):
                h, i = divmod(u, T)
                n = (i + 1) * P
                if u >= 2:
                    pe.wait_ge(s["lmax_ready"], u - 1)
                mm(bank[2 + u % 2][:, 0:n], qk[:, h, i * P:(i + 1) * P], qk[:, H + h, 0:n],
                   start=True, stop=True).then_inc(s["logit_ready"], 1)

            def prob_transposes(u):
                pe.wait_ge(s["probn_ready"], u + 1)
                if u >= 2:
                    pe.wait_ge(s["pT_evicted"], u - 1)
                for j in range(u % T + 1):
                    last = tr(bank[4 + u % 2][:, j * P:(j + 1) * P], prob[u % 3][:, j * P:(j + 1) * P], ident[:, :])
                last.then_inc(s["pT_ready"], 1)

            def attend(u):
                h, i = divmod(u, T)
                pe.wait_ge(s["pT_evicted"], u + 1)
                if i == 0 and h >= 2:
                    pe.wait_ge(s["BT_ready"], h - 1)
                for j in range(i + 1):
                    last = mm(bank[6 + h % 2][:, i * P:(i + 1) * P], dv[:, j, h * HD:(h + 1) * HD],
                              probT[u % 3][:, j * P:(j + 1) * P], start=(j == 0), stop=(j == i))
                last.then_inc(s["av_done"], 1)

            pe.wait_ge(s["qk_ready"], 2 * H)
            pe.wait_ge(s["AT_ready"], 2 * T)
            for i in range(2):
                pe.wait_ge(acc_free[i], (N_SA - 2) // 2)
            logits(0)
            for u in range(UNITS + 2):
                for n in gate_tiles(u):
                    feature_tile(N_SA + n)
                    if n == 0:
                        for i in range(2):
                            pe.wait_ge(acc_free[i], N_SA // 2)
                if u + 1 < UNITS:
                    logits(u + 1)
                if 1 <= u <= UNITS:
                    prob_transposes(u - 1)
                if u >= 2:
                    attend(u - 2)

            with pe.Fori(0, K, 2) as f:
                for j in range(2):
                    pe.wait_ge(s["f_free"], f + (j + 1))
                    for i, (src_hi, src_lo, which) in enumerate(((AT_hi, AT_lo, "AT"), (BT_hi, BT_lo, "BT"))):
                        q = Q_P + 2 * j + i
                        pe.wait_ge(s[which + "_hi_ready"], K)
                        pe.wait_ge(s["whi_ready"], f * 2 + (q + 1))
                        hi, lo = quarter(w_hi, q), quarter(w_lo, q)
                        for w, h in ((hi, src_hi), (hi, src_lo), (lo, src_hi)):
                            if h is src_lo:
                                pe.wait_ge(s[which + "_lo_ready"], K)
                            if w is lo:
                                pe.wait_ge(s["wlo_ready"], f * 2 + (q + 1))
                            for k in range(K):
                                last = mm(bank[2 * j + i][:, :], w[:, k, :], h[:, k, :],
                                          start=(w is hi and h is src_hi and k == 0), stop=(w is lo and k == K - 1))
                    last.then_inc(s["f_ready"], 1)

            def h2_transposes(t):
                pe.wait_ge(s["h2_ready"], t + 1)
                for hf in range(2):
                    if t >= 1:
                        pe.wait_ge(s["h2T_ready"], 2 * (t - 1) + hf + 1)
                    for k in range(4):
                        last = tr(bank[hf][:, k * P:(k + 1) * P], h2s[t % 2][:, (4 * hf + k) * P:(4 * hf + k + 1) * P],
                                  ident[:, :])
                    last.then_inc(s["h2T_ps"], 1)

            pe.wait_ge(s["mix_ready"], K)
            pe.wait_ge(s["wout_loaded"], 32)
            for t in range(T):
                for hf in range(2):
                    if t >= 2:
                        pe.wait_ge(s["x2_ready"], 2 * (t - 2) + hf + 1)
                    for k in range(K):
                        last = mm(bank[4 + 2 * (t % 2) + hf][:, :], mixT[:, k, t * P:(t + 1) * P],
                                  wout_sb[hf][:, k, :], start=(k == 0), stop=(k == K - 1))
                    last.then_inc(s["x_out_ready"], 1)
                if t >= 1:
                    h2_transposes(t - 1)
            h2_transposes(T - 1)

            pe.wait_ge(s["h2T_ready"], 2 * T)
            pe.wait_ge(s["wr_loaded"], 16)
            for k in range(K):
                last = mm(bank[2][0:G + NE, :], wr[:, k, :], h2T[:, k, :], start=(k == 0), stop=(k == K - 1))
            last.then_inc(s["lgT_ps"], 1)
            pe.wait_ge(s["lgT_ready"], 1)
            for t in range(T):
                last = tr(bank[3][:, t * (G + NE):(t + 1) * (G + NE)], lgT[0:G + NE, t * P:(t + 1) * P],
                          ident[0:G + NE, 0:G + NE])
            last.then_inc(s["lg_ps"], 1)
            pe.wait_ge(s["maskb_ready"], 1)
            for t in range(T):
                for j in range(t + 1):
                    mm(bank[4][:, t * NE:(t + 1) * NE], (before if j == t else ones_b)[:, :], mask_b[:, j, :],
                       start=(j == 0), stop=(j == t))
            for j in range(T):
                last = mm(bank[5][:, 0:NE], ones_b[:, :], mask_b[:, j, :], start=(j == 0), stop=(j == T - 1))
            last.then_inc(s["rank_ready"], 1)

            def gather_transposes(b, done):
                for k in range(K):
                    last = tr(bank[4][:, k * SLOTS:(k + 1) * SLOTS], xg[b][0:SLOTS, k * P:(k + 1) * P],
                              ident[0:SLOTS, 0:SLOTS])
                last.then_inc(done, 1)

            def gate_up(sl, done):
                for k in range(K):
                    for hf in range(2):
                        last = mm(bank[0][hf * SLOTS:(hf + 1) * SLOTS, :], hTe[sl][:, k, :],
                                  wgu[sl][2][:, :, k, hf * HALF:(hf + 1) * HALF], start=(k == 0), stop=(k == K - 1))
                last.then_inc(done, 1)

            def hidden_transposes(done):
                for c in range(2):
                    last = tr(bank[5][:, c * P:(c + 1) * P], hid[:, c * P:(c + 1) * P], ident[:, :])
                last.then_inc(done, 1)

            def down(sl, done):
                for k in range(F // P):
                    for hf in range(2):
                        last = mm(bank[1][hf * SLOTS:(hf + 1) * SLOTS, :], hidT[:, k % 2, k // 2, :],
                                  wdn[sl][:, k, hf * 512:(hf + 1) * 512], start=(k == 0), stop=(k == F // P - 1))
                last.then_inc(done, 1)

            def run_expert(e, sl, up_round, has_next=True):
                pe.wait_ge(wgu_loaded[sl], up_round * 2)
                nx = (sl + 1) % 3
                if has_next:
                    pe.wait_ge(xg_loaded[nx], up_round + (16 if nx == 0 else 0))
                pe.wait_ge(s["he_ready"], e + 1)
                gate_up(sl, s["gu_ready"])
                if has_next:
                    gather_transposes(nx, s["xg_T"])
                pe.wait_ge(s["hid_ready"], e + 1)
                hidden_transposes(s["hidT_ps"])
                pe.wait_ge(s["hidT_ready"], e + 1)
                pe.wait_ge(wdn_loaded[sl], up_round)
                down(sl, s["y_ready"])

            pe.wait_ge(xg_loaded[0], 16)
            gather_transposes(0, s["xg_T"])
            with pe.Fori(0, E3 // 3) as r:
                for sl in range(3):
                    run_expert(r * 3 + sl, sl, r * 16 + 16)
            for sl in range(2):
                run_expert(E3 + sl, sl, 16 * (E3 // 3 + 1), has_next=(sl == 0))

            n_more = pe.value_load(own_i[0:1, MORE:MORE + 1], min_val=0, max_val=MORE)
            with pe.If(n_more > 0):
                with pe.Fori(0, n_more) as t:
                    pe.wait_ge(s["m_xg"], t * 16 + 16)
                    for k in range(K):
                        last = tr(bank[3 + k // 4][:, (k % 4) * P:(k % 4 + 1) * P], xg[0][:, k * P:(k + 1) * P],
                                  ident[:, :])
                    last.then_inc(s["m_T"], 1)
                    pe.wait_ge(s["m_w"], t * 48 + 48)
                    pe.wait_ge(s["m_he"], t + 1)
                    gate_up(2, s["m_gu"])
                    pe.wait_ge(s["m_hid"], t + 1)
                    hidden_transposes(s["m_hT"])
                    pe.wait_ge(s["m_hTs"], t + 1)
                    down(2, s["m_y"])

        @block.scalar
        def _(act):
            A = nc.scalar.activation
            for t in range(T):
                act.dma_start(x_sb[:, t, :], xd[:, t, :]).then_inc(x_loaded[t], 16)
            small = s["small_loaded"]
            act.wait_ge(s["wsm_zeroed"], 1)
            with nc.allow_non_contiguous_dma(reason="a few narrow columns, once"):
                act.dma_start(wsm[:, :, 0:ID], wind[:, :, O_IK:O_IK + ID]).then_inc(small, 16)
                act.dma_start(wsm[:, :, ID:ID + RANK], wind[:, :, O_GA:O_GA + RANK]).then_inc(small, 16)
                act.dma_start(wsm[:, :, ID + 32:ID + 32 + IH], wind[:, :, O_IW:O_IW + IH]).then_inc(small, 16)
                act.dma_start(g1c[:, :], norm1_g[0].rearrange("(k p) -> p k", p=P)).then_inc(small, 16)
                act.dma_start(gqk[:, 0:1], dsa_q_norm_g.rearrange("a p -> p a")).then_inc(small, 16)
                act.dma_start(gqk[:, 1:2], dsa_k_norm_g.rearrange("a p -> p a")).then_inc(small, 16)
                act.dma_start(lngb[:, 0:1], idx_k_ln_g.rearrange("a p -> p a")).then_inc(small, 16)
                act.dma_start(lngb[:, 1:2], idx_k_ln_b.rearrange("a p -> p a")).then_inc(small, 16)
                act.dma_start(brt[0:G, :], b_router_group.rearrange("a p -> p a")).then_inc(small, 16)
                act.dma_start(brt[G:G + NE, :], b_router_expert.rearrange("a p -> p a")).then_inc(small, 16)
                act.dma_start(wr[:, :, 0:G], w_router_group[0].rearrange("(k p) n -> p k n", p=P)).then_inc(small, 16)
            act.wait_ge(s["consts_done"], 1)
            for t in range(T):
                act.wait_ge(x_loaded[t], 16)
                A(xn[:, t, :], x_sb[:, t, :], ACT.Square, scale=float(D) ** -0.5,
                  accum_out=ms[:, t:t + 1]).then_inc(s["ms_ready"], 1)
                act.wait_ge(s["ms_ready"], t + 1)
                A(ms[:, t:t + 1], ms[:, t:t + 1], ACT.Sqrt, bias=eps[:, 0:1]).then_inc(s["rs_ready"], 1)
            act.wait_ge(s["small_loaded"], 16 * SMALL_DMAS)
            A(wsm_hi, wsm, ACT.Copy).then_inc(s["wsm_hi_ready"], 1)

            done = [0]

            def split_hi(upto):
                while done[0] <= min(upto, Q_END - 1):
                    q = done[0]
                    act.wait_ge(w_loaded[q % 4], 16 * (q // 4 + 1))
                    A(quarter(w_hi, q), quarter(w_raw, q), ACT.Copy).then_inc(s["whi_ready"], 1)
                    done[0] += 1

            def before_tile(n):
                split_hi(n + 3 if (n - 1) // 4 not in TOKEN_BLOCKS else n + 2)

            split_hi(0)
            for k in range(K):
                act.wait_ge(s["xT_ready"], k + 1)
                A(hT_hi[:, k, :], bank[2 + k % 4][:, :], ACT.Copy, scale=g1c[:, k:k + 1]).then_inc(s["hT_hi_ready"], 1)
            split_hi(2)

            for c in range(4):
                n = N_IQ + c
                before_tile(n)
                if c == 1:
                    act.wait_ge(s["ki_cen_ready"], 1)
                    A(ki_sq[0:ID, :], ki_cen[0:ID, :], ACT.Square).then_inc(s["ki_sq_ready"], 1)
                act.wait_ge(s["acc_ready"], n + 1)
                A(qiT[0:ID, 2 * c, :], bank[n % 2][0:ID, :], ACT.Copy)
                A(qiT[0:ID, 2 * c + 1, :], bank[n % 2][ID:2 * ID, :], ACT.Copy).then_inc(acc_free[n % 2], 1)
                if c == 1:
                    act.wait_ge(s["ki_var_ready"], 1)
                    A(ki_raw[0:ID, :], bank[6][0:ID, :], ACT.Sqrt, bias=eps[0:ID, 0:1]).then_inc(s["ki_std_ready"], 1)

            def evict_tokens(n, first, dst, func=ACT.Copy):
                half, c = divmod(n - first, 2)
                act.wait_ge(s["acc_ready"], n + 1)
                A(dst[:, 2 * c:2 * c + 2, half * 2 * P:(half + 1) * 2 * P],
                  bank[n % 2][:, :].rearrange("p (i n) -> p i n", i=2), func).then_inc(acc_free[n % 2], 1)

            for n in range(N_GQ, N_GV):
                before_tile(n)
                if n < N_GK:
                    act.wait_ge(s["acc_ready"], n + 1)
                    A(gqT[:, n - N_GQ, :], bank[n % 2][:, :], ACT.Copy, scale=float(DK) ** -0.5)\
                        .then_inc(acc_free[n % 2], 1)
                else:
                    evict_tokens(n, N_GK, gk)
                for u in range(3 * (n - N_GQ), 3 * (n - N_GQ) + 3):
                    w = (u // IH + 2) * P
                    act.wait_ge(s["idx_logit_ready"], u + 1)
                    if u >= 2:
                        act.wait_ge(s["relu_used"], u - 1)
                    A(relu[u % 2][:, 0:w], bank[2 + u % 4][:, 0:w], ACT.Relu).then_inc(s["relu_ready"], 1)

            def gate_log(t):
                act.wait_ge(s["a_abs"], t + 1)
                A(g_log, g_abs, ACT.Exp).then_inc(s["act_s"], 1)
                act.wait_ge(s["act_s"], t + 1)
                A(g_abs, g_log, ACT.Ln, bias=one[:, 0:1]).then_inc(s["a_exp"], 1)

            for n in range(N_GV, N_GR):
                before_tile(n)
                evict_tokens(n, N_GV, gv)
                t = n - N_GV - 1
                if t == -1:
                    gate_log(0)
                elif t < T:
                    act.wait_ge(s["suf_ready"], t + 1)
                    A(g_kd, bank[3][:, :], ACT.Exp).then_inc(s["kd_ready"], 1)
                    act.wait_ge(s["ind_ready"], t + 1)
                    A(decay[:, :, 2 * t:2 * t + 2], bank[4][:, 0:2 * GH].rearrange("p (h c) -> p h c", h=GH),
                      ACT.Exp).then_inc(s["decay_ready"], 1)
                    if t + 1 < T:
                        gate_log(t + 1)
            for n in range(N_GR, N_Q):
                before_tile(n)
                evict_tokens(n, N_GR, gr, ACT.Silu)

            def root(j):
                act.wait_ge(s["qk_ms_ready"], j + 1)
                if j >= 2:
                    act.wait_ge(s["qk_ready"], j - 1)
                A(rms[j % 2], bank[2][:, :], ACT.Sqrt, bias=eps[:, 0:1]).then_inc(s["qk_rms_ready"], 1)

            def evict_out(t, hf):
                act.wait_ge(s["oT_ready"], 2 * t + hf + 1)
                A(AT[:, 4 * hf:4 * hf + 4, t * P:(t + 1) * P],
                  bank[7][:, :].rearrange("p (k t) -> p k t", k=4), ACT.Copy).then_inc(s["AT_ready"], 1)

            for j in range(2 * H):
                n = N_Q + j
                before_tile(n)
                act.wait_ge(s["acc_ready"], n + 1)
                if j >= 2:
                    act.wait_ge(s["qk_ms_ready"], j - 1)
                A(sq[j % 2], bank[n % 2][:, :], ACT.Square).then_inc(s["qk_sq_ready"], 1)
                if j > 0:
                    root(j - 1)
                t, r = divmod(j, 4)
                if r in (1, 2) and t >= 1:
                    evict_out(t - 1, r - 1)
                if r == 2:
                    act.wait_ge(s["o_ready"], 2 * t + 2)
                    for h in range(GH):
                        last = A(oscr[h], bank[3 + h // 2][:, (h % 2) * DV:(h % 2 + 1) * DV], ACT.Square,
                                 scale=float(DV) ** -0.5, accum_out=oms[:, t, h:h + 1])
                    last.then_inc(s["oms_ready"], 1)
                    act.wait_ge(s["oms_ready"], t + 1)
                    A(ors[:, t, :], oms[:, t, :], ACT.Sqrt, bias=eps[:, 0:1]).then_inc(s["ors_ready"], 1)

            for n in range(N_DV, N_SA):
                before_tile(n)
                if n == N_DV:
                    act.wait_ge(s["kv_ready"], NCH)
                evict_tokens(n, N_DV, dv)
                if n == N_DV:
                    root(2 * H - 1)
                if n in (N_DV + 1, N_DV + 2):
                    evict_out(T - 1, n - N_DV - 1)

            def gate_tile(n):
                before_tile(N_SA + n)
                act.wait_ge(s["acc_ready"], N_SA + n + 1)
                A(gates[n // K][:, n % K, :], bank[n % 2][:, :], ACT.Exp, scale=-1.0)\
                    .then_inc(acc_free[n % 2], 1)

            def hi_of(dst, src, k, done_):
                A(dst[:, k, :], src[:, k, :], ACT.Copy).then_inc(s[done_], 1)

            first_free = max(u for u in range(UNITS) if gate_tiles(u)) + 1
            for u in range(UNITS + 2):
                if u < UNITS:
                    for n in gate_tiles(u):
                        gate_tile(n)
                    if u >= first_free:
                        act.wait_ge(s["acc_ready"], N_END)
                        split_hi(Q_P + 3)
                        if u - first_free < K:
                            hi_of(AT_hi, AT, u - first_free, "AT_hi_ready")
                    n = (u % T + 1) * P
                    act.wait_ge(s["lmax_ready"], u + 1)
                    A(prob[u % 3][:, 0:n], prob[u % 3][:, 0:n], ACT.Exp, bias=nmx[:, u:u + 1],
                      scale=float(HD) ** -0.5, accum_out=psm[:, u:u + 1]).then_inc(s["prob_ready"], 1)
                if u >= 2:
                    v = u - 2
                    n = (v % T + 1) * P
                    act.wait_ge(s["pT_ready"], v + 1)
                    if v >= 3:
                        act.wait_ge(s["av_done"], v - 2)
                    A(probT[v % 3][:, 0:n], bank[4 + v % 2][:, 0:n], ACT.Copy).then_inc(s["pT_evicted"], 1)
                    if v % T == 0 and v >= T:
                        act.wait_ge(s["av_done"], v)
                        h = v // T - 1
                        A(BT[:, h, :], bank[6 + h % 2][:, :], ACT.Copy).then_inc(s["BT_ready"], 1)
                if u >= first_free and u - first_free < H - 2:
                    act.wait_ge(s["BT_ready"], u - first_free + 1)
                    hi_of(BT_hi, BT, u - first_free, "BT_hi_ready")
            act.wait_ge(s["av_done"], UNITS)
            A(BT[:, H - 1, :], bank[6 + (H - 1) % 2][:, :], ACT.Copy).then_inc(s["BT_ready"], 1)
            act.wait_ge(s["BT_ready"], H)
            for h in range(H - 2, H):
                hi_of(BT_hi, BT, h, "BT_hi_ready")

            split_hi(Q_END - 1)

            for t in range(T):
                act.wait_ge(s["x2_ready"], 2 * t + 2)
                if t >= 2:
                    act.wait_ge(h2s_stored[t % 2], 16 * (t // 2))
                    act.wait_ge(s["h2T_ps"], 2 * (t - 2) + 2)
                A(h2s[t % 2], x2[:, t, :], ACT.Square, scale=float(D) ** -0.5,
                  accum_out=ms[:, t:t + 1]).then_inc(s["h2_ms"], 1)
                act.wait_ge(s["h2_ms"], t + 1)
                A(ms[:, t:t + 1], ms[:, t:t + 1], ACT.Sqrt, bias=eps[:, 0:1]).then_inc(s["h2_rs"], 1)
                act.wait_ge(s["h2_ready"], t + 1)
                act.dma_start(h2_rows[t * P:(t + 1) * P, :], h2s[t % 2]).then_inc(h2s_stored[t % 2], 16)
                for hf in range(2):
                    act.wait_ge(s["h2T_ps"], 2 * t + hf + 1)
                    A(h2T[:, 4 * hf:4 * hf + 4, t * P:(t + 1) * P],
                      bank[hf][:, :].rearrange("p (k t) -> p k t", k=4), ACT.Copy).then_inc(s["h2T_ready"], 1)
            act.wait_ge(s["lgT_ps"], 1)
            act.wait_ge(s["rows_zeroed"], 16)
            A(lgT[0:G + NE, :], bank[2][0:G + NE, :], ACT.Identity, bias=brt[:, 0:1]).then_inc(s["lgT_ready"], 1)
            act.wait_ge(s["gexp_in"], 1)
            A(tg[:, :, :], tg[:, :, :], ACT.Exp).then_inc(s["gexp_out"], 1)
            act.wait_ge(s["eexp_in"], 1)
            A(wt[:, 1, :], wt[:, 1, :], ACT.Exp).then_inc(s["eexp_out"], 1)

            def store_y(row, sl, done):
                for hf in range(2):
                    act.dma_start(y_rows[bass.ds(row, SLOTS), hf * 512:(hf + 1) * 512],
                                  y_sb[sl][hf * SLOTS:(hf + 1) * SLOTS, :]).then_inc(done, 16)

            def run_expert(e, sl, rounds):
                act.wait_ge(s["gu_ready"], e + 1)
                A(silu_g, bank[0][:, 0:HALF], ACT.Silu).then_inc(s["silu_ready"], 1)
                act.wait_ge(s["hidT_ps"], e + 1)
                A(hidT, bank[5][:, 0:HALF].rearrange("p (c h s) -> p c h s", c=2, h=2), ACT.Copy)\
                    .then_inc(s["hidT_ready"], 1)
                act.wait_ge(s["y_ready"], e + 1)
                act.wait_ge(y_stored[sl], rounds * 32 + 32)
                A(y_sb[sl], bank[1][:, :], ACT.Copy).then_inc(s["act_s"], 1)
                act.wait_ge(s["act_s"], e + (T + 1))
                store_y(e * SLOTS, sl, y_stored[sl])

            with act.Fori(0, E3 // 3) as r:
                for sl in range(3):
                    run_expert(r * 3 + sl, sl, r)
            for sl in range(2):
                run_expert(E3 + sl, sl, E3 // 3)

            n_more = act.value_load(own_i[0:1, MORE:MORE + 1], min_val=0, max_val=MORE)
            with act.If(n_more > 0):
                with act.Fori(0, n_more) as t:
                    act.wait_ge(s["m_gu"], t + 1)
                    A(silu_g, bank[0][:, 0:HALF], ACT.Silu).then_inc(s["m_silu"], 1)
                    act.wait_ge(s["m_hT"], t + 1)
                    A(hidT, bank[5][:, 0:HALF].rearrange("p (c h s) -> p c h s", c=2, h=2), ACT.Copy)\
                        .then_inc(s["m_hTs"], 1)
                    act.wait_ge(s["m_y"], t + 2)
                    act.wait_ge(y_stored[2], 32 * (E3 // 3 + 1))
                    act.wait_ge(s["m_st"], t * 32 + 32)
                    A(y_sb[2], bank[1][:, :], ACT.Copy).then_inc(s["act_s"], 1)
                    act.wait_ge(s["act_s"], t + (NE + T + 1))
                    store_y(t * SLOTS + FIRST_MORE, 2, s["m_st"])

            for t in range(T):
                act.wait_ge(s["out_ready"], t + 1)
                act.dma_start(outd[:, t, :], x2[:, t, :]).then_inc(s["out_stored"], 16)
            act.wait_ge(s["out_stored"], 16 * T)

        @block.vector
        def _(dve):
            V = nc.vector
            st = Steps(dve, s["dve_s"])
            V.engine_nop().then_inc(s["m_y"], 1)
            for counted in y_stored + [s["m_st"]]:
                V.engine_nop().then_inc(counted, 32)
            dve.wait_ge(s["small_loaded"], 16 * SMALL_DMAS)
            for t in range(T):
                dve.wait_ge(s["rs_ready"], t + 1)
                st.did(V.reciprocal(rs[:, t:t + 1], ms[:, t:t + 1]))
                st.settle()
                V.tensor_scalar(xn[:, t, :], x_sb[:, t, :], rs[:, t:t + 1], None, ALU.mult).then_inc(s["xn_ready"], 1)
            dve.wait_ge(s["wsm_hi_ready"], 1)
            V.tensor_tensor(wsm_lo, wsm, wsm_hi.bitcast(F32), ALU.subtract).then_inc(s["wsm_lo_ready"], 1)
            for k in range(K):
                dve.wait_ge(s["hT_hi_ready"], k + 1)
                V.scalar_tensor_tensor(hT_lo[:, k, :], bank[2 + k % 4][:, :], g1c[:, k:k + 1],
                                       hT_hi[:, k, :].bitcast(F32), ALU.mult, ALU.subtract)\
                    .then_inc(s["hT_lo_ready"], 1)

            dve.wait_ge(s["small_ready"], 1)
            V.tensor_copy(ki_raw[0:ID, :], bank[6][0:ID, :]).then_inc(s["ki_evicted"], 1)
            V.tensor_copy(gaT[0:RANK, :], bank[6][ID:ID + RANK, :])
            V.tensor_scalar(wiT[0:IH, :], bank[6][ID + 32:ID + 32 + IH, :], float(ID) ** -0.5 * float(IH) ** -0.5,
                            None, ALU.mult).then_inc(s["small_evicted"], 1)
            dve.wait_ge(s["ki_evicted"], 1)
            dve.wait_ge(s["ki_mean_ready"], 1)
            V.tensor_tensor(ki_cen[0:ID, :], ki_raw[0:ID, :], bank[7][0:ID, :], ALU.subtract)\
                .then_inc(s["ki_cen_ready"], 1)
            dve.wait_ge(s["ki_std_ready"], 1)
            st.did(V.reciprocal(ki_raw[0:ID, :], ki_raw[0:ID, :]))
            st.settle()
            dve.wait_ge(s["ki_cen_ready"], 1)
            st.did(V.scalar_tensor_tensor(kiT[0:ID, :], ki_cen[0:ID, :], lngb[:, 0:1], ki_raw[0:ID, :],
                                          ALU.mult, ALU.mult))
            st.settle()
            V.tensor_scalar(kiT[0:ID, :], kiT[0:ID, :], lngb[:, 1:2], None, ALU.add).then_inc(s["kiT_ready"], 1)
            dve.wait_ge(s["wi_ps"], 1)
            V.tensor_copy(wi[:, :, :], bank[7][:, 0:T * IH].rearrange("p (t h) -> p t h", t=T))\
                .then_inc(s["wi_ready"], 1)
            dve.wait_ge(s["wi_ready"], 1)
            u = 0
            for i in range(1, T):
                n = (i + 1) * P
                for h in range(IH):
                    dve.wait_ge(s["relu_ready"], u + 1)
                    if h == 0:
                        V.tensor_scalar(bias[i][:, :], relu[u % 2][:, 0:n], wi[:, i, 0:1], None, ALU.mult)\
                            .then_inc(s["relu_used"], 1)
                    else:
                        dve.wait_ge(s["relu_used"], u)
                        V.scalar_tensor_tensor(bias[i][:, :], relu[u % 2][:, 0:n], wi[:, i, h:h + 1],
                                               bias[i][:, :], ALU.mult, ALU.add).then_inc(s["relu_used"], 1)
                    u += 1
                dve.wait_ge(s["relu_used"], u)
                st.did(V.memset(bias[i][0:CHUNK, n - CHUNK:n], NEG))
            st.settle()

            ROUNDS = TOPK // 8
            rounds = [0]

            def topk_round():
                if rounds[0] < ROUNDS:
                    rounds[0] += 1
                    st.settle()
                    for i in range(1, T):
                        st.did(V.max(mx8[:, i, :], bias[i][:, :]))
                    st.settle()
                    for i in range(1, T):
                        st.did(V.match_replace(bias[i][:, :], mx8[:, i, :], bias[i][:, :], TAKEN))

            dve.wait_ge(s["gla_loaded"], 48)

            def gate_pre(t):
                dve.wait_ge(s["a_ready"], t + 1)
                st.did(V.tensor_scalar(g_min, bank[2][:, :], 0.0, None, ALU.min))
                st.settle()
                V.scalar_tensor_tensor(g_abs, g_min, 2.0, bank[2][:, :], ALU.mult, ALU.subtract)\
                    .then_inc(s["a_abs"], 1)

            gate_pre(0)
            for i in range(2):
                dve.wait_ge(acc_free[i], N_GV // 2)
            for t in range(T):
                dve.wait_ge(s["a_exp"], t + 1)
                st.settle()
                V.tensor_tensor(g_log, g_min, g_abs, ALU.subtract).then_inc(s["la_ready"], 1)
                topk_round()
                dve.wait_ge(s["kd_ready"], t + 1)
                V.tensor_tensor(gk[:, t, :], gk[:, t, :], g_kd, ALU.mult).then_inc(s["kdec_ready"], 1)
                if t + 1 < T:
                    dve.wait_ge(s["la_ready"], t + 1)
                    dve.wait_ge(s["ind_ready"], t + 1)
                    gate_pre(t + 1)
            while rounds[0] < ROUNDS:
                topk_round()
            st.settle()
            for i in range(1, T):
                V.tensor_scalar(bias[i][:, :], bias[i][:, :], TAKEN * 0.5, NEG, ALU.is_ge, ALU.mult)\
                    .then_inc(s["bias_ready"], 1)

            def finish_norm(j):
                dve.wait_ge(s["qk_rms_ready"], j + 1)
                st.did(V.reciprocal(rms[j % 2], rms[j % 2]))
                st.settle()
                V.tensor_tensor(qk[:, j, :], qk[:, j, :], rms[j % 2], ALU.mult).then_inc(s["qk_ready"], 1)

            def next_state(ch):
                t, c = divmod(ch, 2)
                dve.wait_ge(s["kv_ready"], ch + 1)
                dve.wait_ge(s["decay_ready"], t + 1)
                if ch >= 1:
                    dve.wait_ge(s["state_ready"], ch)
                if ch >= 2:
                    dve.wait_ge(s["o_ready"], ch - 1)
                for h in range(GH):
                    kv = bank[5 + h // 2][:, (h % 2) * DV:(h % 2 + 1) * DV]
                    if ch == 0:
                        last = V.tensor_copy(state[c][:, h, :], kv)
                    else:
                        last = V.scalar_tensor_tensor(state[c][:, h, :], state[1 - c][:, h, :],
                                                      decay[:, h, ch:ch + 1], kv, ALU.mult, ALU.add)
                last.then_inc(s["state_ready"], 1)

            for i in range(2):
                dve.wait_ge(acc_free[i], N_Q // 2)
            for j in range(2 * H):
                n = N_Q + j
                t, r = divmod(j, 4)
                dve.wait_ge(s["qk_sq_ready"], j + 1)
                V.tensor_scalar(qk[:, j, :], bank[n % 2][:, :], gqk[:, j // H:j // H + 1], None, ALU.mult)\
                    .then_inc(acc_free[n % 2], 1)
                if j > 0:
                    dve.wait_ge(acc_free[(n - 1) % 2], (n - 1) // 2 + 1)
                    finish_norm(j - 1)
                if r < 2:
                    next_state(2 * t + r)
                if r == 1:
                    for h in range(GH):
                        st.did(V.tensor_tensor(gr[:, t, h * DV:(h + 1) * DV], gr[:, t, h * DV:(h + 1) * DV],
                                               gnorm[:, :], ALU.mult))
                if r == 3:
                    dve.wait_ge(s["ors_ready"], t + 1)
                    st.did(V.reciprocal(ors[:, t, :], ors[:, t, :]))
                    st.settle()
                    for h in range(GH):
                        last = V.scalar_tensor_tensor(gr[:, t, h * DV:(h + 1) * DV],
                                                      bank[3 + h // 2][:, (h % 2) * DV:(h % 2 + 1) * DV],
                                                      ors[:, t, h:h + 1], gr[:, t, h * DV:(h + 1) * DV],
                                                      ALU.mult, ALU.mult)
                    last.then_inc(s["o_normed"], 1)
            dve.wait_ge(acc_free[(N_Q + 2 * H - 1) % 2], (N_Q + 2 * H - 1) // 2 + 1)
            finish_norm(2 * H - 1)

            dve.wait_ge(s["bias_ready"], T)
            for u in range(UNITS + 1):
                if u < UNITS:
                    i = u % T
                    n = (i + 1) * P
                    dve.wait_ge(s["logit_ready"], u + 1)
                    if u >= 3:
                        dve.wait_ge(s["pT_ready"], u - 2)
                    st.did(V.tensor_tensor_reduce(out=prob[u % 3][:, 0:n], in0=bank[2 + u % 2][:, 0:n],
                                                  in1=bias[i][:, :], scale=1.0, scalar=2.0 * NEG, op0=ALU.add,
                                                  op1=ALU.max, accum_out=mxl[:, u:u + 1]))
                    st.settle()
                    V.tensor_scalar(nmx[:, u:u + 1], mxl[:, u:u + 1], -float(HD) ** -0.5, None, ALU.mult)\
                        .then_inc(s["lmax_ready"], 1)
                if u >= 1:
                    v = u - 1
                    n = (v % T + 1) * P
                    dve.wait_ge(s["prob_ready"], v + 1)
                    st.did(V.reciprocal(prc[:, v:v + 1], psm[:, v:v + 1]))
                    st.settle()
                    V.tensor_scalar(prob[v % 3][:, 0:n], prob[v % 3][:, 0:n], prc[:, v:v + 1], None, ALU.mult)\
                        .then_inc(s["probn_ready"], 1)

            def sigmoid(f):
                for g in range(2):
                    st.did(V.tensor_scalar(gates[g][:, f, :], gates[g][:, f, :], 1.0, None, ALU.add))
                    st.settle()
                    st.did(V.reciprocal(gates[g][:, f, :], gates[g][:, f, :]))

            for i in range(2):
                dve.wait_ge(acc_free[i], N_END // 2)
                dve.wait_ge(s["av_done"], UNITS)
                V.engine_nop().then_inc(s["f_free"], 1)
            sigmoid(0)
            for f in range(K):
                b0 = 2 * (f % 2)
                dve.wait_ge(s["f_ready"], f + 1)
                st.settle()
                st.did(V.tensor_tensor(mixT[:, f, :], bank[b0][:, :], gates[0][:, f, :], ALU.mult))
                V.tensor_tensor(mtmp[f % 2], bank[b0 + 1][:, :], gates[1][:, f, :], ALU.mult)\
                    .then_inc(s["f_free"], 1)
                st.settle()
                dve.wait_ge(s["f_free"], f + 3)
                V.tensor_tensor(mixT[:, f, :], mixT[:, f, :], mtmp[f % 2], ALU.add).then_inc(s["mix_ready"], 1)
                if f + 1 < K:
                    sigmoid(f + 1)

            dve.wait_ge(s["x_again"], 16)
            dve.wait_ge(s["g2_loaded"], 16)
            for t in range(T):
                for hf in range(2):
                    dve.wait_ge(s["x_out_ready"], 2 * t + hf + 1)
                    V.tensor_tensor(x2[:, t, hf * BLK:(hf + 1) * BLK], bank[4 + 2 * (t % 2) + hf][:, :],
                                    x2[:, t, hf * BLK:(hf + 1) * BLK], ALU.add).then_inc(s["x2_ready"], 1)
                dve.wait_ge(s["h2_rs"], t + 1)
                st.did(V.reciprocal(rs[:, t:t + 1], ms[:, t:t + 1]))
                st.settle()
                dve.wait_ge(s["x2_ready"], 2 * t + 2)
                V.scalar_tensor_tensor(h2s[t % 2], x2[:, t, :], rs[:, t:t + 1], g2b, ALU.mult, ALU.mult)\
                    .then_inc(s["h2_ready"], 1)

            dve.wait_ge(s["lg_ps"], 1)
            for i in range(2):
                dve.wait_ge(h2s_stored[i], 16 * (T // 2))
            lps = bank[3][:, 0:T * (G + NE)].rearrange("p (t n) -> p t n", t=T)
            st.did(V.memset(lg[:, :, :], NEG))
            st.settle()
            st.did(V.tensor_copy(lg[:, :, 0:G], lps[:, :, 0:G]))
            st.did(V.tensor_copy(le[:, :, :], lps[:, :, G:G + NE]))
            st.settle()
            for t in range(T):
                st.did(V.max(v8[:, t, :], lg[:, t, :]))
            st.settle()
            for t in range(T):
                st.did(V.max_index(i8[:, t, :], v8[:, t, :], lg[:, t, :]))
            V.tensor_tensor(tg[:, :, :], lg[:, :, 0:G], v8[:, :, 0:1].to_broadcast([P, T, G]), ALU.subtract)\
                .then_inc(s["gexp_in"], 1)
            st.settle()
            st.did(V.tensor_copy(gid[:, :], i8[:, :, 0]))
            st.settle()
            for t in range(T):
                st.did(V.tensor_scalar(pen[:, t, :], gio[:, :], gid[:, t:t + 1], NEG, ALU.not_equal, ALU.mult))
            st.settle()
            st.did(V.tensor_tensor(le[:, :, :], le[:, :, :], pen[:, :, :], ALU.add))
            st.settle()
            dve.wait_ge(s["gexp_in"], 1)
            for t in range(T):
                st.did(V.max(v8[:, t, :], le[:, t, :]))
            st.settle()
            for t in range(T):
                st.did(V.max_index(i8[:, t, :], v8[:, t, :], le[:, t, :]))
            V.tensor_tensor(wt[:, 1, :], v8[:, :, 1], v8[:, :, 0], ALU.subtract).then_inc(s["eexp_in"], 1)
            st.settle()
            for k in range(TOP_E):
                st.did(V.tensor_copy(eid[:, k, :], i8[:, :, k]))
            st.settle()
            for k in range(TOP_E):
                for t in range(T):
                    st.did(V.tensor_scalar(oh[:, k, t, :], eio[:, :], eid[:, k, t:t + 1], None, ALU.is_equal))
            st.settle()
            V.tensor_tensor(mask_b[:, :, :], oh[:, 0], oh[:, 1], ALU.add).then_inc(s["maskb_ready"], 1)
            dve.wait_ge(s["gexp_out"], 1)
            st.did(V.reduce_sum(gw[:, :], tg[:, :, :], AX))
            dve.wait_ge(s["eexp_out"], 1)
            st.did(V.tensor_scalar(wt[:, 0, :], wt[:, 1, :], 1.0, None, ALU.add))
            st.settle()
            st.did(V.tensor_tensor(gw[:, :], gw[:, :], wt[:, 0, :], ALU.mult))
            st.settle()
            st.did(V.reciprocal(wt[:, 0, :], gw[:, :]))
            st.settle()
            st.did(V.tensor_tensor(wt[:, 1, :], wt[:, 1, :], wt[:, 0, :], ALU.mult))
            dve.wait_ge(s["rank_ready"], 1)
            st.did(V.tensor_copy(cnt[:, :], bank[5][:, 0:NE]))
            st.settle()
            st.did(V.tensor_scalar(more[:, :], cnt[:, :], float(SLOTS), None, ALU.is_gt))
            for m in range(2, MAX_TILES):
                st.settle()
                st.did(V.scalar_tensor_tensor(more[:, :], cnt[:, :], float(SLOTS * m), more[:, :], ALU.is_gt, ALU.add))
            st.did(V.memset(mbase[:, :], 1.0))
            st.settle()
            st.did(V.tensor_tensor_scan(xinc[:, :], mbase[:, :], more[:, :], 0.0, ALU.mult, ALU.add))
            st.settle()
            st.did(V.tensor_tensor(more[:, :], xinc[:, :], more[:, :], ALU.subtract))
            st.settle()
            st.did(V.tensor_scalar(mbase[:, :], more[:, :], float(SLOTS), float(FIRST_MORE - SLOTS), ALU.mult, ALU.add))
            rank = bank[4][:, 0:T * NE].rearrange("p (t e) -> p t e", t=T)
            for k in range(TOP_E):
                st.did(V.tensor_tensor(pen[:, :, :], oh[:, k], rank, ALU.mult))
                st.settle()
                st.did(V.reduce_sum(rk[:, k, :], pen[:, :, :], AX))
                st.settle()
                st.did(V.tensor_tensor(pen[:, :, :], oh[:, k], mbase[:, :].unsqueeze(1).to_broadcast([P, T, NE]),
                                       ALU.mult))
                st.settle()
                st.did(V.reduce_sum(rtmp[:, k, :], pen[:, :, :], AX))
                st.settle()
            st.did(V.tensor_scalar(isov[:, :, :], rk[:, :, :], float(SLOTS), None, ALU.is_ge))
            st.did(V.scalar_tensor_tensor(rowf[:, :, :], eid[:, :, :], float(SLOTS), rk[:, :, :], ALU.mult, ALU.add))
            st.did(V.scalar_tensor_tensor(tabf[:, :, :], rk[:, :, :], float(NE), eid[:, :, :], ALU.mult, ALU.add))
            st.did(V.tensor_tensor(rtmp[:, :, :], rtmp[:, :, :], rk[:, :, :], ALU.add))
            st.settle()
            for dst, src in ((row_i, rowf), (tab_i, tabf)):
                st.did(V.tensor_tensor(oh[:, :, :, 0], rtmp[:, :, :], src[:, :, :], ALU.subtract))
                st.settle()
                st.did(V.tensor_tensor(oh[:, :, :, 0], oh[:, :, :, 0], isov[:, :, :], ALU.mult))
                st.settle()
                st.did(V.tensor_tensor(src[:, :, :], src[:, :, :], oh[:, :, :, 0], ALU.add))
                st.settle()
                last = V.tensor_copy(dst[:, :, :], src[:, :, :])
                if dst is tab_i:
                    last.then_inc(s["tab_ready"], 1)
                else:
                    st.did(last)
            st.did(V.tensor_tensor(own[:, :, :], xinc[:, :].unsqueeze(1).to_broadcast([P, MORE, NE]),
                                   tio[:, :].unsqueeze(2).to_broadcast([P, MORE, NE]), ALU.is_le))
            st.settle()
            st.did(V.reduce_sum(ownf[:, 0:MORE], own[:, :, :], AX))
            st.did(V.tensor_copy(ownf[:, MORE:MORE + 1], xinc[:, NE - 1:NE]))
            st.settle()
            st.did(V.tensor_scalar(ownf[:, 0:MORE], ownf[:, 0:MORE], float(NE - 1), None, ALU.min))
            st.settle()
            V.tensor_copy(own_i[:, :], ownf[:, :]).then_inc(s["own_ready"], 1)

            def evict_gathered(sl, done):
                V.tensor_copy(hTe[sl], bank[4][:, :].rearrange("p (k s) -> p k s", k=K)).then_inc(done, 1)

            def run_expert(e, sl, has_next=True):
                dve.wait_ge(s["silu_ready"], e + 1)
                V.tensor_tensor(hid, silu_g, bank[0][:, HALF:F], ALU.mult).then_inc(s["hid_ready"], 1)
                if has_next:
                    dve.wait_ge(s["xg_T"], e + 2)
                    evict_gathered((sl + 1) % 3, s["he_ready"])

            dve.wait_ge(s["xg_T"], 1)
            evict_gathered(0, s["he_ready"])
            with dve.Fori(0, E3 // 3) as r:
                for sl in range(3):
                    run_expert(r * 3 + sl, sl)
            for sl in range(2):
                run_expert(E3 + sl, sl, has_next=(sl == 0))
            dve.wait_ge(s["own_ready"], 1)
            n_more = dve.value_load(own_i[0:1, MORE:MORE + 1], min_val=0, max_val=MORE)
            with dve.If(n_more > 0):
                with dve.Fori(0, n_more) as t:
                    dve.wait_ge(s["m_T"], t + 1)
                    for hf in range(2):
                        last = V.tensor_copy(hTe[2][:, 4 * hf:4 * hf + 4, :],
                                             bank[3 + hf][:, :].rearrange("p (k s) -> p k s", k=4)[:, :, 0:SLOTS])
                    last.then_inc(s["m_he"], 1)
                    dve.wait_ge(s["m_silu"], t + 1)
                    V.tensor_tensor(hid, silu_g, bank[0][:, HALF:F], ALU.mult).then_inc(s["m_hid"], 1)

            for t in range(T):
                for k in range(TOP_E):
                    dve.wait_ge(yg_loaded[TOP_E * t + k], 16)
                    last = V.scalar_tensor_tensor(x2[:, t, :], yg[TOP_E * t + k], wt[:, k, t:t + 1], x2[:, t, :],
                                                  ALU.mult, ALU.add)
                    if k < TOP_E - 1:
                        st.did(last)
                        st.settle()
                last.then_inc(s["out_ready"], 1)

        @block.gpsimd
        def _(pool):
            Q = nc.gpsimd
            st = Steps(pool, s["pool_s"])

            def step(instruction):
                st.did(instruction)
                st.settle()

            step(Q.memset(gaT[:, :], 1.0))
            Q.memset(wsm[:, :, :], 0.0).then_inc(s["wsm_zeroed"], 1)
            pool.wait_ge(s["wsm_zeroed"], 1)
            def ones_where(tile, value, *selects):
                step(Q.memset(tile, value))
                for base, cm, pattern in selects:
                    step(Q.affine_select(out=tile, in_=tile, compare_op=ALU.is_ge, fill=0.0, base=base,
                                           pattern=pattern, channel_multiplier=cm))

            ones_where(ident[:, :], 1.0, (0, 1, [[-1, P]]), (0, -1, [[1, P]]))
            ones_where(mean_m[:, :], 1.0 / HD)
            ones_where(mean_i[:, :], 1.0 / ID)
            ones_where(one[:, :], 1.0)
            ones_where(eps[:, :], EPS)
            ones_where(ones_b[:, :], 1.0)
            ones_where(before[:, :], 1.0, (-1, -1, [[1, P]]))
            inv = 1.0 / GATE_TEMP
            ones_where(suffix[:, :], inv, (-1, 1, [[-1, P]]))
            step(Q.memset(suffix[CHUNK:P, 0:CHUNK], 0.0))
            ones_where(chunk_of[:, 0:1], inv, (CHUNK - 1, -1, [[0, 1]]))
            ones_where(chunk_of[:, 1:2], inv, (-CHUNK, 1, [[0, 1]]))
            step(Q.memset(zero_i[:, :], 0))
            step(Q.memset(bias0[:, :], 0.0))
            Q.memset(bias0[0:CHUNK, CHUNK:P], NEG).then_inc(s["bias_ready"], 1)
            step(Q.iota(tokid[:, :], pattern=[[P, T]], base=0, channel_multiplier=1))
            step(Q.iota(eio[:, :], pattern=[[1, NE]], base=0, channel_multiplier=0,
                          allow_small_or_imprecise_dtypes=True))
            step(Q.iota(gio[:, :].rearrange("p (g e) -> p g e", g=G), pattern=[[1, G], [0, EPG]], base=0,
                          channel_multiplier=0, allow_small_or_imprecise_dtypes=True))
            step(Q.iota(tio[:, :], pattern=[[1, MORE]], base=0, channel_multiplier=0,
                          allow_small_or_imprecise_dtypes=True))
            pool.engine_nop().then_inc(s["consts_done"], 1)

            def split_lo(first, end):
                for q in range(first, end):
                    pool.wait_ge(s["whi_ready"], q + 1)
                    Q.tensor_tensor(quarter(w_lo, q), quarter(w_raw, q), quarter(w_hi, q).bitcast(F32),
                                    ALU.subtract).then_inc(s["wlo_ready"], 1)

            tab = row_token.rearrange("(p n) a -> p (n a)", p=SLOTS)
            pool.dma_start(tab, zero_i[0:SLOTS, :]).then_inc(s["table_zero"], 16)
            with nc.allow_non_contiguous_dma(reason="the routers' columns"):
                pool.dma_start(wr[:, :, G:G + NE], w_router_expert[0].rearrange("(k p) n -> p k n", p=P))\
                    .then_inc(s["wr_loaded"], 16)
            pool.wait_ge(s["xn_ready"], T)
            pool.dma_start(wa2[0:RANK, :], gla_w_a2[0]).then_inc(s["gla_loaded"], 16)
            pool.dma_start(wa2[RANK:RANK + 1, :], gla_b_a).then_inc(s["gla_loaded"], 16)
            pool.dma_start(gnorm[:, :], gla_norm_g[0].partition_broadcast(P)).then_inc(s["gla_loaded"], 16)
            split_lo(0, N_SA)
            pool.wait_ge(s["o_normed"], T)
            step(Q.memset(zrow, 0.0))
            zp = (ROWS - FIRST_MORE) // 8
            pool.dma_start(y_rows[FIRST_MORE:ROWS].rearrange("(p r) d -> p r d", r=8),
                           zrow[0:zp].unsqueeze(1).to_broadcast([zp, 8, D])).then_inc(s["rows_zeroed"], 16)
            split_lo(N_SA, Q_P + 4)
            for src, lo, hi, which in ((AT, AT_lo, AT_hi, "AT"), (BT, BT_lo, BT_hi, "BT")):
                for k in range(K):
                    pool.wait_ge(s[which + "_hi_ready"], k + 1)
                    Q.tensor_tensor(lo[:, k, :], src[:, k, :], hi[:, k, :].bitcast(F32), ALU.subtract)\
                        .then_inc(s[which + "_lo_ready"], 1)
            split_lo(Q_P + 4, Q_END)
            pool.wait_ge(s["mix_ready"], K)
            pool.wait_ge(s["rows_zeroed"], 16)
            pool.dma_start(g2b, norm2_g[0].partition_broadcast(P)).then_inc(s["g2_loaded"], 16)

            pool.wait_ge(s["table_zero"], 16)
            pool.wait_ge(s["tab_ready"], 1)
            for k in range(TOP_E):
                for t in range(T):
                    pool.indirect_dma_start(
                        out=row_token, out_offset=bass.IndirectOffsetOnAxis(ap=tab_i[:, k, t:t + 1], axis=0),
                        in_=tokid[:, t:t + 1], in_offset=None, bounds_check=ROWS - 1, oob_is_err=False)\
                        .then_inc(s["scattered"], 16)
            pool.wait_ge(s["scattered"], 16 * TOP_E * T)
            pool.dma_start(idx_all[:, :], row_token[0:FIRST_MORE].rearrange("(r e) a -> r (e a)", e=NE))\
                .then_inc(s["idx_loaded"], 16)
            pool.wait_ge(s["idx_loaded"], 16)
            for i in range(2):
                pool.wait_ge(h2s_stored[i], 16 * (T // 2))

            def gather(sl, tokens, done):
                pool.indirect_dma_start(
                    out=xg[sl][0:SLOTS, :], out_offset=None, in_=h2_rows,
                    in_offset=bass.IndirectOffsetOnAxis(ap=tokens, axis=0),
                    bounds_check=S - 1, oob_is_err=False).then_inc(done, 16)

            pool.wait_ge(s["lgT_ready"], 1)
            for e in range(NE):
                if e >= 3:
                    pool.wait_ge(s["xg_T"], e - 2)
                gather(e % 3, idx_all[:, e:e + 1], xg_loaded[e % 3])
            pool.wait_ge(s["own_ready"], 1)
            n_more = pool.value_load(own_i[0:1, MORE:MORE + 1], min_val=0, max_val=MORE)
            with pool.If(n_more > 0):
                pool.wait_ge(s["xg_T"], NE)
            for t in range(MORE):
                with pool.If(n_more > t):
                    if t >= 1:
                        pool.wait_ge(s["m_T"], t)
                    pool.dma_start(idx_more[:, :], row_token[FIRST_MORE + t * SLOTS:FIRST_MORE + (t + 1) * SLOTS, :])\
                        .then_inc(s["m_idx"], 16)
                    pool.wait_ge(s["m_idx"], 16 * (t + 1))
                    gather(0, idx_more[:, :], s["m_xg"])
            with pool.If(n_more > 0):
                pool.wait_ge(s["m_st"], n_more * 32 + 32)
            for sl in range(3):
                pool.wait_ge(y_stored[sl], 32 * (1 + E3 // 3 + (1 if sl < NE % 3 else 0)))
            for t in range(T):
                for k in range(TOP_E):
                    pool.indirect_dma_start(
                        out=yg[TOP_E * t + k], out_offset=None, in_=y_rows,
                        in_offset=bass.IndirectOffsetOnAxis(ap=row_i[:, k, t:t + 1], axis=0),
                        bounds_check=ROWS - 1, oob_is_err=False).then_inc(yg_loaded[TOP_E * t + k], 16)


_NAMES = ['x', 'norm1_g', 'w_in', 'gla_w_a2', 'gla_b_a', 'gla_norm_g', 'dsa_q_norm_g', 'dsa_k_norm_g',
          'idx_k_ln_g', 'idx_k_ln_b', 'w_branch_gla', 'w_branch_dsa', 'w_out', 'norm2_g',
          'w_router_group', 'b_router_group', 'w_router_expert', 'b_router_expert',
          'w_exp_gate', 'w_exp_up', 'w_exp_down']


def kernel(**inputs):
    import concourse.bacc as bacc
    from concourse.bass_utils import run_bass_kernel_spmd

    nc = bacc.Bacc("TRN2", target_bir_lowering=False, num_devices=1)
    arrays, args = {}, []
    for name in _NAMES:
        a = np.ascontiguousarray(inputs[name])
        arrays[name + "_in"] = a
        args.append(nc.dram_tensor(name + "_in", a.shape, mybir.dt.from_np(a.dtype), kind="ExternalInput").ap())
    shape = arrays["x_in"].shape
    args.append(nc.dram_tensor("out_rows", shape, F32, kind="ExternalOutput").ap())
    encoder_block(nc, *args)
    r = run_bass_kernel_spmd(nc, [arrays], core_ids=[0])
    return r.results[0]["out_rows"]
```

```python
from contextlib import ExitStack

import numpy as np

import concourse.bass as bass
from concourse import mybir

ALU = mybir.AluOpType
ACT = mybir.ActivationFunctionType
F32 = mybir.dt.float32
F32R = mybir.dt.float32r
BF16 = mybir.dt.bfloat16
I32 = mybir.dt.int32
U32 = mybir.dt.uint32
AX = mybir.AxisListType.X

P = 128
CHUNK = 64
EPS = 1e-6
GATE_TEMP = 16.0
TOPK_MAX = 256
TOP_E = 2
SLOTS = 48
WIDE = 64
NEG = -1.0e30
TAKEN = -3.0e38
PIECE = 4096


class Steps:

    def __init__(self, eng, sem):
        self.eng, self.sem, self.n = eng, sem, 0

    def did(self, instruction):
        instruction.then_inc(self.sem, 1)
        self.n += 1
        return self.n

    def settle(self):
        self.eng.wait_ge(self.sem, self.n)


def encoder_block(nc, x, norm1_g, w_in, gla_w_a2, gla_b_a, gla_norm_g, dsa_q_norm_g, dsa_k_norm_g,
                  idx_k_ln_g, idx_k_ln_b, w_branch_gla, w_branch_dsa, w_out, norm2_g,
                  w_router_group, b_router_group, w_router_expert, b_router_expert,
                  w_exp_gate, w_exp_up, w_exp_down, out):
    _, S, D = x.shape
    RANK = gla_w_a2.shape[1]
    DK = D // 2 // 4
    DV = gla_norm_g.shape[1]
    GH = D // DV
    HD = dsa_q_norm_g.shape[1]
    H = D // HD
    ID = idx_k_ln_g.shape[1]
    G = w_router_group.shape[2]
    NE = w_router_expert.shape[2]
    EPG = NE // G
    F = w_exp_gate.shape[3]
    IH = (w_in.shape[2] - (2 * GH * DK + 2 * D + RANK + 3 * D + ID + 2 * D)) // (ID + 1)
    TOPK = min(TOPK_MAX, S // 4)
    T = S // P
    K = D // P
    NCH = S // CHUNK
    BLK = 512
    HALF = F // 2
    assert (S, D, F, BLK, HD, DK, TOPK) == (512, 1024, 512, 512, P, P, P) and IH == 8 and ID == 64

    widths = [GH * DK, GH * DK, D, RANK, D, D, D, D, IH * ID, ID, IH, D, D]
    offs = [int(v) for v in np.cumsum([0] + widths)]
    O_GQ, O_GK, O_GV, O_GA, O_GR, O_DQ, O_DK, O_DV, O_IQ, O_IK, O_IW, O_SA, O_SB = offs[:13]
    assert O_DK == O_DQ + D and O_SB == O_SA + D

    PAIRS = S * TOP_E
    MORE = (PAIRS - 1) // SLOTS
    ROWS = (NE + MORE) * SLOTS
    FIRST_MORE = NE * SLOTS
    MAX_TILES = (S - 1) // SLOTS + 1

    xd = x[0].rearrange("(t p) d -> p t d", p=P)
    outd = out[0].rearrange("(t p) d -> p t d", p=P)
    wind = w_in[0].rearrange("(k p) n -> p k n", p=P)
    pad_ = w_branch_gla[0].rearrange("(k p) n -> p k n", p=P)
    pbd_ = w_branch_dsa[0].rearrange("(k p) n -> p k n", p=P)
    woutd = w_out[0].rearrange("(k p) n -> p k n", p=P)
    h2_rows = nc.dram_tensor("h2_rows", (S, D), F32).ap()
    y_rows = nc.dram_tensor("y_rows", (ROWS, D), F32).ap()
    row_token = nc.dram_tensor("row_token", (ROWS, 1), I32).ap()
    wgd = w_exp_gate[0].rearrange("e (k p) f -> e p k f", p=P)
    wud = w_exp_up[0].rearrange("e (k p) f -> e p k f", p=P)
    wdd = w_exp_down[0].rearrange("e (k p) d -> e p k d", p=P)

    with ExitStack() as ctx:
        def sem(name):
            return ctx.enter_context(nc.semaphore(name))

        def sb(name, shape, dt=F32):
            return ctx.enter_context(nc.sbuf_tensor(name, shape, dt))

        arena_at = (nc.sbuf_base + 31) // 32 * 32
        arena = sb("arena", [P, 11 * PIECE])
        work = sb("work", [P, PIECE])
        as_f32r = {i: nc.alloc_sbuf_tensor_at(f"piece{i}_r", [P, PIECE], F32R, offset=arena_at + 4 * PIECE * i)
                   for i in (0, 1, 2, 3, 4, 5, 6, 7, 9, 10, 11)}
        bank = [ctx.enter_context(nc.psum_tensor(f"bank{i}", [P, 512], F32)) for i in range(8)]

        def piece(i, n=1, words=None, off=0):
            return arena[:, i * PIECE + off:i * PIECE + off + (words or n * PIECE - off)]

        def piece_r(i, words=PIECE, off=0):
            return as_f32r[i][:, off:off + words]

        hT_hi, hT_lo = [piece_r(i).rearrange("p (k t) -> p k t", k=K) for i in (0, 7)]
        w_raw = [piece(1, words=2048, off=2048 * i).rearrange("p (k n) -> p k n", k=K) for i in range(2)]
        w_lo = [piece_r(1, words=2048, off=2048 * i).rearrange("p (k n) -> p k n", k=K)
                for i in range(2)]
        w_hi = [piece_r(2, words=2048, off=2048 * i).rearrange("p (k n) -> p k n", k=K)
                for i in range(2)]
        qk = piece(3, 2).rearrange("p (h t) -> p h t", h=2 * H)
        gr, gv = [piece(i).rearrange("p (t d) -> p t d", t=T) for i in (5, 6)]
        dv = piece(6).rearrange("p (t d) -> p t d", t=T)
        gqT = piece(8, words=2048).rearrange("p (h t) -> p h t", h=GH)
        gk = piece(8, words=2048, off=2048).rearrange("p (t n) -> p t n", t=T)
        gates = [piece(i).rearrange("p (j t) -> p j t", j=K) for i in (5, 8)]
        wout_sb = [piece(i).rearrange("p (k n) -> p k n", k=K) for i in (4, 6)]
        wout_lo, wout_hi = [[piece_r(i).rearrange("p (k n) -> p k n", k=K) for i in ii] for ii in ((4, 6), (0, 7))]
        mixT = gates[0]
        mix_lo, mix_hi = [piece_r(i).rearrange("p (k t) -> p k t", k=K) for i in (5, 3)]
        x_sb = piece(9).rearrange("p (t d) -> p t d", t=T)
        AT, BT = [piece(i).rearrange("p (k t) -> p k t", k=K) for i in (9, 10)]
        AT_lo, BT_lo = [piece_r(i).rearrange("p (k t) -> p k t", k=K) for i in (9, 10)]
        AT_hi, BT_hi = [piece_r(i).rearrange("p (k t) -> p k t", k=K) for i in (0, 7)]
        h2T = piece(9).rearrange("p (k t) -> p k t", k=K)
        xn = piece(10).rearrange("p (t d) -> p t d", t=T)
        qiT = piece(10).rearrange("p (h t) -> p h t", h=IH)
        x2 = piece(10).rearrange("p (t d) -> p t d", t=T)

        def m2(off, words):
            return work[:, off:off + words]
        SMALL = ID + 32 + IH
        wsm = m2(0, K * SMALL).rearrange("p (k n) -> p k n", k=K)
        wsm_lo = piece_r(11, K * SMALL).rearrange("p (k n) -> p k n", k=K)
        wsm_hi = piece_r(11, K * SMALL, K * SMALL).rearrange("p (k n) -> p k n", k=K)
        ki_raw, ki_cen, ki_sq = m2(832, 512), m2(1344, 512), m2(1856, 512)
        kiT = m2(2368, 512)
        relu = [m2(2880, 512), m2(832, 512)]
        wiT = m2(2880, 512)
        g_abs, g_min, g_log, g_kd = [piece(9, words=512, off=512 * i) for i in range(4)]
        wa2 = piece(9, words=GH * DK, off=2048)
        sq = [m2(0, 512), m2(512, 512)]
        rms = [m2(1024, 512), m2(1536, 512)]
        state = [piece(10, words=1024, off=1024 * i).rearrange("p (h v) -> p h v", h=GH) for i in range(2)]
        oscr = [m2(2816 + DV * i, DV) for i in range(GH)]
        gnorm = m2(3840, DV)
        prob = [m2(512 * i, 512) for i in range(3)]
        probT = [m2(1536 + 512 * i, 512) for i in range(3)]
        zrow = m2(3072, D)
        mtmp = [m2(512 * i, 512) for i in range(2)]
        h2s = [m2(1024 * i, 1024) for i in range(2)]
        g2b = m2(2048, 1024)
        lgT = m2(3072, 512)
        le = m2(3584, T * NE).rearrange("p (t e) -> p t e", t=T)
        oh = m2(3584 + T * NE, TOP_E * T * NE).rearrange("p (k t e) -> p k t e", k=TOP_E, t=T)
        pen = m2(3584 + 3 * T * NE, TOP_E * NE).rearrange("p (k e) -> p k e", k=TOP_E)
        own = piece(9, words=MORE * NE, off=3072).rearrange("p (m e) -> p m e", m=MORE)
        base_of = piece(9, words=T * NE, off=3072 + MORE * NE).rearrange("p (t e) -> p t e", t=T)
        cnt, more, xinc, mbase = [piece(9, words=NE, off=3072 + (MORE + T + i) * NE) for i in range(4)]
        slot_pieces = [(1, 2, 8), (0, 4, 3), (5, 6, 7)]
        wgu, wdn = [], []
        for a, b, c in slot_pieces:
            both = arena[:, a * PIECE:(b + 1) * PIECE]
            wgu.append((piece(a).rearrange("p (k f) -> p k f", k=K), piece(b).rearrange("p (k f) -> p k f", k=K),
                        both.rearrange("p (q w) -> p q w", w=PIECE)[:, ::(b - a), :].rearrange(
                            "p q (k f) -> p q k f", k=K)))
            wdn.append(piece(c).rearrange("p (k d) -> p k d", k=F // P))
        xg = [arena[:, 9 * PIECE + 1024 * i:9 * PIECE + 1024 * (i + 1)] for i in range(3)]
        hTe = [m2(512 * i, 512).rearrange("p (k s) -> p k s", k=K) for i in range(3)]
        silu_g, hid = m2(1536, 256), m2(1792, 256)
        hidT = m2(2048, 256).rearrange("p (c h s) -> p c h s", c=2, h=2)
        y_sb = [m2(2304 + 512 * i, 512) for i in range(3)]
        yg = [arena[:, 1024 * i:1024 * (i + 1)] for i in range(TOP_E * T)]

        ident = sb("ident", [P, P])
        mean_m = sb("mean_m", [P, P])
        mean_i = sb("mean_i", [ID, ID])
        suffix = sb("suffix", [P, P])
        chunk_of = sb("chunk_of", [P, 2])
        before = sb("before", [P, P], BF16)
        ones_b = sb("ones_b", [P, P], BF16)
        one = sb("one", [P, 1])
        eps = sb("eps", [P, 1])
        no_token = sb("no_token", [P, ROWS // SLOTS], I32)
        bias0 = sb("bias0", [P, P])
        bias = [bias0] + [sb(f"bias{i}", [P, (i + 1) * P]) for i in range(1, T)]
        gaT = sb("gaT", [32, S])
        g1c = sb("g1c", [P, K])
        gqk = sb("gqk", [P, 2])
        lngb = sb("lngb", [ID, 2])
        wi = sb("wi", [P, T, IH])
        ms = sb("ms", [P, T])
        rs = sb("rs", [P, T])
        mx8 = sb("mx8", [P, T, 8])
        decay = sb("decay", [P, GH, NCH])
        oms = sb("oms", [P, T, GH])
        ors = sb("ors", [P, T, GH])
        orr = sb("orr", [P, GH])
        nmx = sb("nmx", [P, T * H])
        mxl = sb("mxl", [P, T * H])
        psm = sb("psm", [P, T * H])
        prc = sb("prc", [P, T * H])
        brt = sb("brt", [G + NE, 1])
        wr = sb("wr", [P, K, G + NE])
        tokid = sb("tokid", [P, T], I32)
        eio = sb("eio", [P, NE])
        gio = sb("gio", [P, NE])
        tio = sb("tio", [P, MORE])
        lg = sb("lg", [P, T, 8])
        tg = sb("tg", [P, T, G])
        v8 = sb("v8", [P, T, 8])
        i8 = sb("i8", [P, T, 8], U32)
        gid = sb("gid", [P, T])
        gw = sb("gw", [P, T])
        eid = sb("eid", [P, TOP_E, T])
        wt = sb("wt", [P, TOP_E, T])
        mask_b = sb("mask_b", [P, T, NE], BF16)
        rk = sb("rk", [P, TOP_E, T])
        rtmp = sb("rtmp", [P, TOP_E, T])
        isov = sb("isov", [P, TOP_E, T])
        rowf = sb("rowf", [P, TOP_E, T])
        tabf = sb("tabf", [P, TOP_E, T])
        row_i = sb("row_i", [P, TOP_E, T], I32)
        tab_i = sb("tab_i", [P, TOP_E, T], I32)
        tab_more = sb("tab_more", [P, TOP_E, T], I32)
        ownf = sb("ownf", [P, MORE + 1])
        own_i = sb("own_i", [P, MORE + 1], I32)
        idx_all = sb("idx_all", [SLOTS, NE], I32)
        idx_more = sb("idx_more", [SLOTS, 1], I32)

        names = """consts_done eps_ready small_loaded wsm_zeroed ms_ready xn_ready xT_ready hT_hi_ready hT_lo_ready
            wsm_hi_ready wsm_lo_ready whi_ready wlo_ready AT_hi_ready AT_lo_ready BT_hi_ready BT_lo_ready
            wout_loaded wout_hi_ready mix_hi_ready mix_lo_ready acc_ready small_ready ki_evicted small_evicted ki_mean_ready ki_cen_ready ki_sq_ready
            ki_var_ready kiT_ready wi_ps wi_ready idx_logit_ready relu_ready relu_used qk_sq_ready qk_ms_ready
            qk_rms_ready qk_ready bias_ready a_ready a_abs a_exp la_ready suf_ready kd_ready kdec_ready
            ind_ready decay_ready kv_ready state_ready o_ready oms_ready o_normed oT_ready AT_ready logit_ready
            lmax_ready prob_ready probn_ready pT_ready pT_evicted av_done BT_ready f_free f_ready mix_ready
            x_again x_out_ready x2_ready h2_ms h2_ready h2T_ps h2T_ready lgT_ps lgT_ready lg_ps gexp_in gexp_out
            eexp_in eexp_out maskb_ready rank_ready counts_ready tab_ready rows_ready scattered_more table_zero
            scattered idx_loaded own_ready xg_T he_ready gu_ready silu_ready hid_ready hidT_ps hidT_ready
            y_ready m_w m_idx m_xg m_T m_he m_gu m_silu m_hid m_hT m_hTs m_y m_st wr_loaded rows_zeroed rs_ready
            ki_std_ready ors_ready h2_rs gla_loaded g2_loaded out_ready out_stored dve_s act_s pool_s""".split()
        s = {n: sem(n) for n in names}
        wout_lo_ready = [sem(f"wout_lo_ready{i}") for i in range(2)]
        acc_free = [sem(f"acc_free{i}") for i in range(2)]
        x_loaded = [sem(f"x_loaded{i}") for i in range(T)]
        w_loaded = [sem(f"w_loaded{i}") for i in range(4)]
        wgu_loaded = [sem(f"wgu_loaded{i}") for i in range(3)]
        wdn_loaded = [sem(f"wdn_loaded{i}") for i in range(3)]
        xg_loaded = [sem(f"xg_loaded{i}") for i in range(3)]
        y_stored = [sem(f"y_stored{i}") for i in range(3)]
        yg_loaded = [sem(f"yg_loaded{i}") for i in range(T)]
        h2s_stored = [sem(f"h2s_stored{i}") for i in range(2)]

        B_IQ, B_GQ, B_GK, B_GV, B_GR, B_Q, B_DV, B_SA, B_END = 0, 1, 2, 3, 5, 7, 11, 13, 17
        TOKEN_BLOCKS = (B_GK, B_GV, B_GV + 1, B_GR, B_GR + 1, B_DV, B_DV + 1)
        N_IQ, N_GQ, N_GK, N_GV, N_GR, N_Q, N_DV, N_SA, N_END = [
            4 * b for b in (B_IQ, B_GQ, B_GK, B_GV, B_GR, B_Q, B_DV, B_SA, B_END)]
        Q_P = N_END
        Q_END = Q_P + 2 * K

        def quarter(ring, q):
            return ring[q // 2 % 2][:, :, q % 2 * P:(q % 2 + 1) * P]

        def freed_by(q):
            return q // 2 * 2 + 2 if q // 4 in TOKEN_BLOCKS else q + 1

        E3 = NE - NE % 3
        assert NE % 3 == 2
        UNITS = H * T
        SMALL_DMAS = 11

        GATE_PASSES = 3 * 2 * K

        def gate_tiles(u):
            return [p // 3 for p in (2 * u, 2 * u + 1) if p < GATE_PASSES and p % 3 == 2]


        block = ctx.enter_context(nc.Block())

        @block.sync
        def _(sp):
            def load_quarter(q, src):
                sp.dma_start(quarter(w_raw, q), src).then_inc(w_loaded[q % 4], 16)

            for t in range(T):
                sp.dma_start(x_sb[:, t, :], xd[:, t, :]).then_inc(x_loaded[t], 16)
            load_quarter(0, wind[:, :, O_IQ:O_IQ + P])
            small = s["small_loaded"]
            sp.wait_ge(s["wsm_zeroed"], 1)
            with nc.allow_non_contiguous_dma(reason="a few narrow columns, once"):
                sp.dma_start(wsm[:, :, 0:ID], wind[:, :, O_IK:O_IK + ID]).then_inc(small, 16)
                sp.dma_start(wsm[:, :, ID:ID + RANK], wind[:, :, O_GA:O_GA + RANK]).then_inc(small, 16)
                sp.dma_start(wsm[:, :, ID + 32:ID + 32 + IH], wind[:, :, O_IW:O_IW + IH]).then_inc(small, 16)
                sp.dma_start(g1c[:, :], norm1_g[0].rearrange("(k p) -> p k", p=P)).then_inc(small, 16)
                sp.dma_start(gqk[:, 0:1], dsa_q_norm_g.rearrange("a p -> p a")).then_inc(small, 16)
                sp.dma_start(gqk[:, 1:2], dsa_k_norm_g.rearrange("a p -> p a")).then_inc(small, 16)
                sp.dma_start(lngb[:, 0:1], idx_k_ln_g.rearrange("a p -> p a")).then_inc(small, 16)
                sp.dma_start(lngb[:, 1:2], idx_k_ln_b.rearrange("a p -> p a")).then_inc(small, 16)
                sp.dma_start(brt[0:G, :], b_router_group.rearrange("a p -> p a")).then_inc(small, 16)
                sp.dma_start(brt[G:G + NE, :], b_router_expert.rearrange("a p -> p a")).then_inc(small, 16)
                sp.dma_start(wr[:, :, 0:G], w_router_group[0].rearrange("(k p) n -> p k n", p=P)).then_inc(small, 16)

            for b, off in zip(range(B_END), (O_IQ, O_GQ, O_GK, O_GV, O_GV + BLK, O_GR, O_GR + BLK,
                                             O_DQ, O_DQ + BLK, O_DK, O_DK + BLK, O_DV, O_DV + BLK,
                                             O_SA, O_SA + BLK, O_SB, O_SB + BLK)):
                for q in range(max(4 * b, 1), 4 * b + 4):
                    if q >= 4:
                        sp.wait_ge(s["acc_ready"], freed_by(q - 4))
                    load_quarter(q, wind[:, :, off + q % 4 * P:off + (q % 4 + 1) * P])
            for f in range(2):
                for i, src in enumerate((pad_, pbd_)):
                    sp.wait_ge(s["acc_ready"], freed_by(Q_P + 2 * f + i - 4))
                    load_quarter(Q_P + 2 * f + i, src[:, :, f * P:(f + 1) * P])
            sp.wait_ge(s["logit_ready"], UNITS)
            sp.dma_start(wout_sb[0], woutd[:, :, 0:BLK]).then_inc(s["wout_loaded"], 16)
            sp.wait_ge(s["av_done"], UNITS)
            sp.dma_start(wout_sb[1], woutd[:, :, BLK:D]).then_inc(s["wout_loaded"], 16)
            with sp.Fori(0, K // 2 - 1) as g:
                for j in range(2):
                    sp.wait_ge(s["f_ready"], g * 2 + (j + 1))
                    for i, src in enumerate((pad_, pbd_)):
                        load_quarter(Q_P + 2 * j + i, src[:, :, bass.ds(g * (2 * P) + (j + 2) * P, P)])
            sp.wait_ge(s["f_ready"], K)
            sp.dma_start(x2, xd).then_inc(s["x_again"], 16)

            def expert(dram, e):
                return dram[bass.ds(e, 1)].rearrange("e p k f -> p (e k) f")

            def load_up(e, sl):
                sp.dma_start(wgu[sl][0], expert(wgd, e)).then_inc(wgu_loaded[sl], 16)
                sp.dma_start(wgu[sl][1], expert(wud, e)).then_inc(wgu_loaded[sl], 16)

            def load_down(e, sl):
                sp.dma_start(wdn[sl], expert(wdd, e)).then_inc(wdn_loaded[sl], 16)

            sp.wait_ge(s["mix_ready"], K)
            load_up(0, 0)
            load_down(0, 0)
            sp.wait_ge(s["x_out_ready"], T)
            load_up(1, 1)
            sp.wait_ge(s["x_out_ready"], 2 * T)
            load_down(1, 1)
            load_up(2, 2)
            sp.wait_ge(xg_loaded[0], 16)
            load_down(2, 2)
            with sp.Fori(3, E3, 3) as e:
                for sl in range(3):
                    sp.wait_ge(s["gu_ready"], e + (sl - 2))
                    load_up(e + sl, sl)
                    sp.wait_ge(s["y_ready"], e + (sl - 2))
                    load_down(e + sl, sl)
            for sl in range(2):
                sp.wait_ge(s["gu_ready"], E3 + sl - 2)
                load_up(E3 + sl, sl)
                sp.wait_ge(s["y_ready"], E3 + sl - 2)
                load_down(E3 + sl, sl)
            sp.wait_ge(s["own_ready"], 1)
            n_more = sp.value_load(own_i[0:1, MORE:MORE + 1], min_val=0, max_val=MORE)
            with sp.If(n_more > 0):
                sp.wait_ge(s["y_ready"], NE)
                with sp.Fori(0, n_more) as t:
                    e = sp.value_load(own_i[0:1, bass.ds(t, 1)], min_val=0, max_val=NE - 1)
                    sp.wait_ge(s["m_y"], t + 1)
                    sp.dma_start(wgu[2][0], expert(wgd, e)).then_inc(s["m_w"], 16)
                    sp.dma_start(wgu[2][1], expert(wud, e)).then_inc(s["m_w"], 16)
                    sp.dma_start(wdn[2], expert(wdd, e)).then_inc(s["m_w"], 16)

        @block.tensor
        def _(pe):
            mm, tr = nc.tensor.matmul, nc.tensor.transpose

            def begin(n):
                if n >= 2:
                    pe.wait_ge(acc_free[n % 2], n // 2)

            def feature_pass(n, i):
                if i == 0:
                    begin(n)
                    pe.wait_ge(s["whi_ready"], n + 1)
                if i == 2:
                    pe.wait_ge(s["wlo_ready"], n + 1)
                w, h = quarter(w_lo if i == 2 else w_hi, n), hT_lo if i == 1 else hT_hi
                for k in range(K):
                    last = mm(bank[n % 2][:, :], w[:, k, :], h[:, k, :],
                              start=(i == 0 and k == 0), stop=(i == 2 and k == K - 1))
                if i == 2:
                    last.then_inc(s["acc_ready"], 1)

            def feature_tile(n):
                for i in range(3):
                    feature_pass(n, i)

            def token_tile(n):
                begin(n)
                q = n // 2 * 2
                pe.wait_ge(s["whi_ready"], q + 2)
                hi, lo = w_hi[q // 2 % 2], w_lo[q // 2 % 2]
                for i in range(2):
                    t = 2 * (n % 2) + i
                    for h, w in ((hT_hi, hi), (hT_lo, hi), (hT_hi, lo)):
                        if w is lo:
                            pe.wait_ge(s["wlo_ready"], q + 2)
                        for k in range(K):
                            last = mm(bank[n % 2][:, i * 2 * P:(i + 1) * 2 * P], h[:, k, t * P:(t + 1) * P], w[:, k, :],
                                      start=(w is hi and h is hT_hi and k == 0), stop=(w is lo and k == K - 1))
                last.then_inc(s["acc_ready"], 1)

            pe.wait_ge(s["consts_done"], 1)
            pe.wait_ge(s["xn_ready"], T)
            for k in range(K):
                if k >= 4:
                    pe.wait_ge(s["hT_lo_ready"], k - 3)
                for t in range(T):
                    last = tr(bank[2 + k % 4][:, t * P:(t + 1) * P], xn[:, t, k * P:(k + 1) * P], ident[:, :])
                last.then_inc(s["xT_ready"], 1)

            pe.wait_ge(s["hT_hi_ready"], K)
            pe.wait_ge(s["wsm_lo_ready"], 1)
            for w, h in ((wsm_hi, hT_hi), (wsm_lo, hT_hi), (wsm_hi, hT_lo)):
                if h is hT_lo:
                    pe.wait_ge(s["hT_lo_ready"], K)
                for k in range(K):
                    last = mm(bank[6][0:SMALL, :], w[:, k, :], h[:, k, :],
                              start=(w is wsm_hi and h is hT_hi and k == 0), stop=(h is hT_lo and k == K - 1))
            last.then_inc(s["small_ready"], 1)
            for c in range(4):
                feature_tile(N_IQ + c)
                if c == 0:
                    pe.wait_ge(s["ki_evicted"], 1)
                    mm(bank[7][0:ID, :], mean_i[:, :], ki_raw[0:ID, :], start=True, stop=True)\
                        .then_inc(s["ki_mean_ready"], 1)
                if c == 1:
                    pe.wait_ge(s["small_evicted"], 1)
                    pe.wait_ge(s["ki_sq_ready"], 1)
                    mm(bank[6][0:ID, :], mean_i[:, :], ki_sq[0:ID, :], start=True, stop=True)\
                        .then_inc(s["ki_var_ready"], 1)
                if c == 2:
                    pe.wait_ge(s["ki_cen_ready"], 1)
                    for t in range(T):
                        last = tr(bank[7][:, t * IH:(t + 1) * IH], wiT[0:IH, t * P:(t + 1) * P], ident[0:IH, 0:IH])
                    last.then_inc(s["wi_ps"], 1)

            def index_logits(u):
                i, h = u // IH + 1, u % IH
                n = (i + 1) * P
                if u >= 4:
                    pe.wait_ge(s["relu_ready"], u - 3)
                mm(bank[2 + u % 4][:, 0:n], qiT[0:ID, h, i * P:(i + 1) * P], kiT[0:ID, 0:n],
                   start=True, stop=True).then_inc(s["idx_logit_ready"], 1)

            for n in range(N_GQ, N_GV):
                (feature_tile if n < N_GK else token_tile)(n)
                if n == N_GQ:
                    for i in range(2):
                        pe.wait_ge(acc_free[i], (N_IQ + 4) // 2)
                    pe.wait_ge(s["kiT_ready"], 1)
                for u in range(3 * (n - N_GQ), 3 * (n - N_GQ) + 3):
                    index_logits(u)

            def gate_product(t):
                mm(bank[2][:, :], gaT[0:RANK + 1, t * P:(t + 1) * P], wa2[0:RANK + 1, :], start=True, stop=True)\
                    .then_inc(s["a_ready"], 1)

            for n in range(N_GV, N_GR):
                token_tile(n)
                t = n - N_GV - 1
                if t == -1:
                    pe.wait_ge(s["relu_ready"], (T - 1) * IH)
                    pe.wait_ge(s["gla_loaded"], 48)
                    pe.wait_ge(s["small_evicted"], 1)
                    gate_product(0)
                elif t < T:
                    pe.wait_ge(s["la_ready"], t + 1)
                    if t >= 1:
                        pe.wait_ge(s["kd_ready"], t)
                    mm(bank[3][:, :], suffix[:, :], g_log, start=True, stop=True).then_inc(s["suf_ready"], 1)
                    if t >= 1:
                        pe.wait_ge(s["decay_ready"], t)
                    for h in range(GH):
                        last = mm(bank[4][:, 2 * h:2 * h + 2], g_log[:, h * DK:(h + 1) * DK], chunk_of[:, :],
                                  start=True, stop=True)
                    last.then_inc(s["ind_ready"], 1)
                    if t + 1 < T:
                        gate_product(t + 1)
            for n in range(N_GR, N_Q):
                token_tile(n)

            def mean_square(j):
                pe.wait_ge(s["qk_sq_ready"], j + 1)
                if j >= 1:
                    pe.wait_ge(s["qk_rms_ready"], j)
                mm(bank[2][:, :], mean_m[:, :], sq[j % 2], start=True, stop=True).then_inc(s["qk_ms_ready"], 1)

            def chunk_kv(ch):
                t, rows = ch // 2, slice(ch % 2 * CHUNK, (ch % 2 + 1) * CHUNK)
                pe.wait_ge(s["kdec_ready"], t + 1)
                if ch == 0:
                    for i in range(2):
                        pe.wait_ge(acc_free[i], (N_DV - 4 * 4) // 2)
                if ch >= 1:
                    pe.wait_ge(s["state_ready"], ch)
                for h in range(GH):
                    last = mm(bank[5 + h // 2][:, (h % 2) * DV:(h % 2 + 1) * DV],
                              gk[rows, t, h * DK:(h + 1) * DK], gv[rows, t, h * DV:(h + 1) * DV],
                              start=True, stop=True)
                last.then_inc(s["kv_ready"], 1)

            def chunk_out(ch):
                t, rows = ch // 2, slice(ch % 2 * CHUNK, (ch % 2 + 1) * CHUNK)
                pe.wait_ge(s["state_ready"], ch + 1)
                if ch % 2 == 0 and t >= 1:
                    pe.wait_ge(s["o_normed"], t)
                for h in range(GH):
                    last = mm(bank[3 + h // 2][rows, (h % 2) * DV:(h % 2 + 1) * DV],
                              gqT[:, h, ch * CHUNK:(ch + 1) * CHUNK], state[ch % 2][:, h, :],
                              start=True, stop=True)
                last.then_inc(s["o_ready"], 1)

            def out_transposes(t, hf):
                pe.wait_ge(s["o_normed"], t + 1)
                if t or hf:
                    pe.wait_ge(s["AT_ready"], 2 * t + hf)
                for k in range(4):
                    last = tr(bank[7][:, k * P:(k + 1) * P], gr[:, t, (4 * hf + k) * P:(4 * hf + k + 1) * P],
                              ident[:, :])
                last.then_inc(s["oT_ready"], 1)

            for j in range(2 * H):
                feature_tile(N_Q + j)
                if j > 0:
                    mean_square(j - 1)
                t, r = divmod(j, 4)
                if r == 0:
                    chunk_kv(2 * t)
                if r == 1:
                    chunk_out(2 * t)
                    chunk_kv(2 * t + 1)
                if r == 2:
                    chunk_out(2 * t + 1)
                if r in (1, 2) and t >= 1:
                    out_transposes(t - 1, r - 1)

            for n in range(N_DV, N_SA):
                token_tile(n)
                if n == N_DV:
                    mean_square(2 * H - 1)
                if n in (N_DV + 1, N_DV + 2):
                    out_transposes(T - 1, n - N_DV - 1)

            def logits(u):
                h, i = divmod(u, T)
                n = (i + 1) * P
                if u >= 2:
                    pe.wait_ge(s["lmax_ready"], u - 1)
                mm(bank[2 + u % 2][:, 0:n], qk[:, h, i * P:(i + 1) * P], qk[:, H + h, 0:n],
                   start=True, stop=True).then_inc(s["logit_ready"], 1)

            def prob_transposes(u):
                pe.wait_ge(s["probn_ready"], u + 1)
                if u >= 2:
                    pe.wait_ge(s["pT_evicted"], u - 1)
                for j in range(u % T + 1):
                    last = tr(bank[4 + u % 2][:, j * P:(j + 1) * P], prob[u % 3][:, j * P:(j + 1) * P], ident[:, :])
                last.then_inc(s["pT_ready"], 1)

            def attend(u):
                h, i = divmod(u, T)
                pe.wait_ge(s["pT_evicted"], u + 1)
                if i == 0 and h >= 2:
                    pe.wait_ge(s["BT_ready"], h - 1)
                for j in range(i + 1):
                    last = mm(bank[6 + h % 2][:, i * P:(i + 1) * P], dv[:, j, h * HD:(h + 1) * HD],
                              probT[u % 3][:, j * P:(j + 1) * P], start=(j == 0), stop=(j == i))
                last.then_inc(s["av_done"], 1)

            pe.wait_ge(s["qk_ready"], 2 * H)
            pe.wait_ge(s["AT_ready"], 2 * T)
            for i in range(2):
                pe.wait_ge(acc_free[i], (N_SA - 2) // 2)
            logits(0)

            def gate_pass(p):
                if p < GATE_PASSES:
                    feature_pass(N_SA + p // 3, p % 3)
                if p == 2:
                    for i in range(2):
                        pe.wait_ge(acc_free[i], N_SA // 2)

            for u in range(UNITS + 2):
                gate_pass(2 * u)
                if u + 1 < UNITS:
                    logits(u + 1)
                if 1 <= u <= UNITS:
                    prob_transposes(u - 1)
                gate_pass(2 * u + 1)
                if u >= 2:
                    attend(u - 2)

            with pe.Fori(0, K, 2) as f:
                for j in range(2):
                    pe.wait_ge(s["f_free"], f + (j + 1))
                    for i, (src_hi, src_lo, which) in enumerate(((AT_hi, AT_lo, "AT"), (BT_hi, BT_lo, "BT"))):
                        q = Q_P + 2 * j + i
                        pe.wait_ge(s[which + "_hi_ready"], K)
                        pe.wait_ge(s["whi_ready"], f * 2 + (q + 1))
                        hi, lo = quarter(w_hi, q), quarter(w_lo, q)
                        for w, h in ((hi, src_hi), (hi, src_lo), (lo, src_hi)):
                            if h is src_lo:
                                pe.wait_ge(s[which + "_lo_ready"], K)
                            if w is lo:
                                pe.wait_ge(s["wlo_ready"], f * 2 + (q + 1))
                            for k in range(K):
                                last = mm(bank[2 * j + i][:, :], w[:, k, :], h[:, k, :],
                                          start=(w is hi and h is src_hi and k == 0), stop=(w is lo and k == K - 1))
                    last.then_inc(s["f_ready"], 1)

            def h2_transposes(t):
                pe.wait_ge(s["h2_ready"], t + 1)
                if t >= 1:
                    pe.wait_ge(s["lgT_ready"], t)
                for hf in range(2):
                    if t >= 1:
                        pe.wait_ge(s["h2T_ready"], 2 * (t - 1) + hf + 1)
                    for k in range(4):
                        last = tr(bank[hf][:, k * P:(k + 1) * P], h2s[t % 2][:, (4 * hf + k) * P:(4 * hf + k + 1) * P],
                                  ident[:, :])
                    last.then_inc(s["h2T_ps"], 1)

            def router_logits(t):
                pe.wait_ge(s["h2T_ready"], 2 * t + 2)
                for k in range(K):
                    last = mm(bank[0][0:G + NE, 0:P], wr[:, k, :], h2T[:, k, t * P:(t + 1) * P],
                              start=(k == 0), stop=(k == K - 1))
                last.then_inc(s["lgT_ps"], 1)

            def token_major_logits(t):
                pe.wait_ge(s["lgT_ready"], t + 1)
                if t >= 1:
                    pe.wait_ge(s["maskb_ready"], t)
                tr(bank[3][:, 0:G + NE], lgT[0:G + NE, t * P:(t + 1) * P],
                   ident[0:G + NE, 0:G + NE]).then_inc(s["lg_ps"], 1)

            def ranks(t):
                pe.wait_ge(s["maskb_ready"], t + 1)
                if t >= 1:
                    pe.wait_ge(s["tab_ready"], t)
                for j in range(t + 1):
                    last = mm(bank[2][:, t * NE:(t + 1) * NE], (before if j == t else ones_b)[:, :],
                              mask_b[:, j, :], start=(j == 0), stop=(j == t))
                last.then_inc(s["rank_ready"], 1)

            pe.wait_ge(s["wr_loaded"], 16)
            for n in range(2 * T):
                hf, t = divmod(n, T)
                if n >= 4:
                    pe.wait_ge(s["x2_ready"], n - 3)
                for i, (m, w) in enumerate(((mix_hi, wout_hi[hf]), (mix_lo, wout_hi[hf]), (mix_hi, wout_lo[hf]))):
                    if i == 1 and n == 0:
                        pe.wait_ge(s["mix_lo_ready"], K)
                    for k in range(K):
                        if t == 0 and i == 0:
                            pe.wait_ge(s["wout_hi_ready"], K * hf + k + 1)
                            if hf == 0:
                                pe.wait_ge(s["mix_hi_ready"], k + 1)
                        if t == 0 and i == 2:
                            pe.wait_ge(wout_lo_ready[hf], k + 1)
                        last = mm(bank[4 + n % 4][:, :], m[:, k, t * P:(t + 1) * P], w[:, k, :],
                                  start=(i == 0 and k == 0), stop=(i == 2 and k == K - 1))
                    if i == 2:
                        last.then_inc(s["x_out_ready"], 1)
                    if hf == 1 and i == 0 and t >= 2:
                        router_logits(t - 2)
                    if hf == 1 and i == 1 and t >= 1:
                        h2_transposes(t - 1)
                    if hf == 1 and i == 2 and t >= 2:
                        token_major_logits(t - 2)
            router_logits(T - 2)
            h2_transposes(T - 1)
            for t in range(T - 3):
                ranks(t)
            token_major_logits(T - 2)
            router_logits(T - 1)
            ranks(T - 3)
            token_major_logits(T - 1)
            ranks(T - 2)
            ranks(T - 1)
            for j in range(T):
                last = mm(bank[3][:, 0:NE], ones_b[:, :], mask_b[:, j, :],
                          start=(j == 0), stop=(j == T - 1))
            last.then_inc(s["counts_ready"], 1)

            def gather_transposes(b, done):
                for k in range(K):
                    last = tr(bank[4][:, k * WIDE:(k + 1) * WIDE], xg[b][0:WIDE, k * P:(k + 1) * P],
                              ident[0:WIDE, 0:WIDE])
                last.then_inc(done, 1)

            def gate_up(sl, done):
                for k in range(K):
                    for hf in range(2):
                        last = mm(bank[0][hf * WIDE:(hf + 1) * WIDE, :], hTe[sl][:, k, :],
                                  wgu[sl][2][:, :, k, hf * HALF:(hf + 1) * HALF], start=(k == 0), stop=(k == K - 1))
                last.then_inc(done, 1)

            def hidden_transposes(done):
                for c in range(2):
                    last = tr(bank[5][:, c * P:(c + 1) * P], hid[:, c * P:(c + 1) * P], ident[:, :])
                last.then_inc(done, 1)

            def down(sl, done):
                for k in range(F // P):
                    for hf in range(2):
                        last = mm(bank[1][hf * WIDE:(hf + 1) * WIDE, :], hidT[:, k % 2, k // 2, :],
                                  wdn[sl][:, k, hf * 512:(hf + 1) * 512], start=(k == 0), stop=(k == F // P - 1))
                last.then_inc(done, 1)

            def run_expert(e, sl, up_round, has_next=True):
                pe.wait_ge(wgu_loaded[sl], up_round * 2)
                nx = (sl + 1) % 3
                if has_next:
                    pe.wait_ge(xg_loaded[nx], up_round + (16 if nx == 0 else 0))
                pe.wait_ge(s["he_ready"], e + 1)
                gate_up(sl, s["gu_ready"])
                if has_next:
                    gather_transposes(nx, s["xg_T"])
                pe.wait_ge(s["hid_ready"], e + 1)
                hidden_transposes(s["hidT_ps"])
                pe.wait_ge(s["hidT_ready"], e + 1)
                pe.wait_ge(wdn_loaded[sl], up_round)
                down(sl, s["y_ready"])

            pe.wait_ge(xg_loaded[0], 16)
            gather_transposes(0, s["xg_T"])
            with pe.Fori(0, E3 // 3) as r:
                for sl in range(3):
                    run_expert(r * 3 + sl, sl, r * 16 + 16)
            for sl in range(2):
                run_expert(E3 + sl, sl, 16 * (E3 // 3 + 1), has_next=(sl == 0))

            n_more = pe.value_load(own_i[0:1, MORE:MORE + 1], min_val=0, max_val=MORE)
            with pe.If(n_more > 0):
                with pe.Fori(0, n_more) as t:
                    pe.wait_ge(s["m_xg"], t * 16 + 16)
                    for k in range(K):
                        last = tr(bank[3 + k // 4][:, (k % 4) * P:(k % 4 + 1) * P], xg[0][:, k * P:(k + 1) * P],
                                  ident[:, :])
                    last.then_inc(s["m_T"], 1)
                    pe.wait_ge(s["m_w"], t * 48 + 48)
                    pe.wait_ge(s["m_he"], t + 1)
                    gate_up(2, s["m_gu"])
                    pe.wait_ge(s["m_hid"], t + 1)
                    hidden_transposes(s["m_hT"])
                    pe.wait_ge(s["m_hTs"], t + 1)
                    down(2, s["m_y"])

        @block.scalar
        def _(act):
            A = nc.scalar.activation
            act.wait_ge(s["eps_ready"], 1)
            for t in range(T):
                act.wait_ge(x_loaded[t], 16)
                A(xn[:, t, :], x_sb[:, t, :], ACT.Square, scale=float(D) ** -0.5,
                  accum_out=ms[:, t:t + 1]).then_inc(s["ms_ready"], 1)
                act.wait_ge(s["ms_ready"], t + 1)
                A(ms[:, t:t + 1], ms[:, t:t + 1], ACT.Sqrt, bias=eps[:, 0:1]).then_inc(s["rs_ready"], 1)
            act.wait_ge(s["consts_done"], 1)
            act.wait_ge(s["small_loaded"], 16 * SMALL_DMAS)
            A(wsm_hi, wsm, ACT.Copy).then_inc(s["wsm_hi_ready"], 1)

            done = [0]

            def split_hi(upto):
                while done[0] <= min(upto, Q_END - 1):
                    q = done[0]
                    act.wait_ge(w_loaded[q % 4], 16 * (q // 4 + 1))
                    A(quarter(w_hi, q), quarter(w_raw, q), ACT.Copy).then_inc(s["whi_ready"], 1)
                    done[0] += 1

            def before_tile(n):
                split_hi(n + 3 if (n - 1) // 4 not in TOKEN_BLOCKS else n + 2)

            split_hi(0)
            for k in range(K):
                act.wait_ge(s["xT_ready"], k + 1)
                A(hT_hi[:, k, :], bank[2 + k % 4][:, :], ACT.Copy, scale=g1c[:, k:k + 1]).then_inc(s["hT_hi_ready"], 1)
            split_hi(2)

            for c in range(4):
                n = N_IQ + c
                before_tile(n)
                if c == 1:
                    act.wait_ge(s["ki_cen_ready"], 1)
                    A(ki_sq[0:ID, :], ki_cen[0:ID, :], ACT.Square).then_inc(s["ki_sq_ready"], 1)
                act.wait_ge(s["acc_ready"], n + 1)
                A(qiT[0:ID, 2 * c, :], bank[n % 2][0:ID, :], ACT.Copy)
                A(qiT[0:ID, 2 * c + 1, :], bank[n % 2][ID:2 * ID, :], ACT.Copy).then_inc(acc_free[n % 2], 1)
                if c == 1:
                    act.wait_ge(s["ki_var_ready"], 1)
                    A(ki_raw[0:ID, :], bank[6][0:ID, :], ACT.Sqrt, bias=eps[0:ID, 0:1]).then_inc(s["ki_std_ready"], 1)

            def evict_tokens(n, first, dst, func=ACT.Copy):
                half, c = divmod(n - first, 2)
                act.wait_ge(s["acc_ready"], n + 1)
                A(dst[:, 2 * c:2 * c + 2, half * 2 * P:(half + 1) * 2 * P],
                  bank[n % 2][:, :].rearrange("p (i n) -> p i n", i=2), func).then_inc(acc_free[n % 2], 1)

            for n in range(N_GQ, N_GV):
                before_tile(n)
                if n < N_GK:
                    act.wait_ge(s["acc_ready"], n + 1)
                    A(gqT[:, n - N_GQ, :], bank[n % 2][:, :], ACT.Copy, scale=float(DK) ** -0.5)\
                        .then_inc(acc_free[n % 2], 1)
                else:
                    evict_tokens(n, N_GK, gk)
                for u in range(3 * (n - N_GQ), 3 * (n - N_GQ) + 3):
                    w = (u // IH + 2) * P
                    act.wait_ge(s["idx_logit_ready"], u + 1)
                    if u >= 2:
                        act.wait_ge(s["relu_used"], u - 1)
                    A(relu[u % 2][:, 0:w], bank[2 + u % 4][:, 0:w], ACT.Relu).then_inc(s["relu_ready"], 1)

            def gate_log(t):
                act.wait_ge(s["a_abs"], t + 1)
                A(g_log, g_abs, ACT.Exp).then_inc(s["act_s"], 1)
                act.wait_ge(s["act_s"], t + 1)
                A(g_abs, g_log, ACT.Ln, bias=one[:, 0:1]).then_inc(s["a_exp"], 1)

            for n in range(N_GV, N_GR):
                before_tile(n)
                evict_tokens(n, N_GV, gv)
                t = n - N_GV - 1
                if t == -1:
                    gate_log(0)
                elif t < T:
                    act.wait_ge(s["suf_ready"], t + 1)
                    A(g_kd, bank[3][:, :], ACT.Exp).then_inc(s["kd_ready"], 1)
                    act.wait_ge(s["ind_ready"], t + 1)
                    A(decay[:, :, 2 * t:2 * t + 2], bank[4][:, 0:2 * GH].rearrange("p (h c) -> p h c", h=GH),
                      ACT.Exp).then_inc(s["decay_ready"], 1)
                    if t + 1 < T:
                        gate_log(t + 1)
            for n in range(N_GR, N_Q):
                before_tile(n)
                evict_tokens(n, N_GR, gr, ACT.Silu)

            def root(j):
                act.wait_ge(s["qk_ms_ready"], j + 1)
                if j >= 2:
                    act.wait_ge(s["qk_ready"], j - 1)
                A(rms[j % 2], bank[2][:, :], ACT.Sqrt, bias=eps[:, 0:1]).then_inc(s["qk_rms_ready"], 1)

            def evict_out(t, hf):
                act.wait_ge(s["oT_ready"], 2 * t + hf + 1)
                A(AT[:, 4 * hf:4 * hf + 4, t * P:(t + 1) * P],
                  bank[7][:, :].rearrange("p (k t) -> p k t", k=4), ACT.Copy).then_inc(s["AT_ready"], 1)

            for j in range(2 * H):
                n = N_Q + j
                before_tile(n)
                act.wait_ge(s["acc_ready"], n + 1)
                if j >= 2:
                    act.wait_ge(s["qk_ms_ready"], j - 1)
                A(sq[j % 2], bank[n % 2][:, :], ACT.Square).then_inc(s["qk_sq_ready"], 1)
                if j > 0:
                    root(j - 1)
                t, r = divmod(j, 4)
                if r in (1, 2) and t >= 1:
                    evict_out(t - 1, r - 1)
                if r == 2:
                    act.wait_ge(s["o_ready"], 2 * t + 2)
                    for h in range(GH):
                        last = A(oscr[h], bank[3 + h // 2][:, (h % 2) * DV:(h % 2 + 1) * DV], ACT.Square,
                                 scale=float(DV) ** -0.5, accum_out=oms[:, t, h:h + 1])
                    last.then_inc(s["oms_ready"], 1)
                    act.wait_ge(s["oms_ready"], t + 1)
                    A(ors[:, t, :], oms[:, t, :], ACT.Sqrt, bias=eps[:, 0:1]).then_inc(s["ors_ready"], 1)

            for n in range(N_DV, N_SA):
                before_tile(n)
                if n == N_DV:
                    act.wait_ge(s["kv_ready"], NCH)
                evict_tokens(n, N_DV, dv)
                if n == N_DV:
                    root(2 * H - 1)
                if n in (N_DV + 1, N_DV + 2):
                    evict_out(T - 1, n - N_DV - 1)

            def gate_tile(n):
                before_tile(N_SA + n)
                act.wait_ge(s["acc_ready"], N_SA + n + 1)
                A(gates[n // K][:, n % K, :], bank[n % 2][:, :], ACT.Exp, scale=-1.0)\
                    .then_inc(acc_free[n % 2], 1)

            def hi_of(dst, src, k, done_):
                A(dst[:, k, :], src[:, k, :], ACT.Copy).then_inc(s[done_], 1)

            first_free = max(u for u in range(UNITS) if gate_tiles(u)) + 1
            for u in range(UNITS + 2):
                if u < UNITS:
                    n = (u % T + 1) * P
                    act.wait_ge(s["lmax_ready"], u + 1)
                    A(prob[u % 3][:, 0:n], prob[u % 3][:, 0:n], ACT.Exp, bias=nmx[:, u:u + 1],
                      scale=float(HD) ** -0.5, accum_out=psm[:, u:u + 1]).then_inc(s["prob_ready"], 1)
                if u >= 2:
                    v = u - 2
                    n = (v % T + 1) * P
                    act.wait_ge(s["pT_ready"], v + 1)
                    if v >= 3:
                        act.wait_ge(s["av_done"], v - 2)
                    A(probT[v % 3][:, 0:n], bank[4 + v % 2][:, 0:n], ACT.Copy).then_inc(s["pT_evicted"], 1)
                    if v % T == 0 and v >= T:
                        act.wait_ge(s["av_done"], v)
                        h = v // T - 1
                        A(BT[:, h, :], bank[6 + h % 2][:, :], ACT.Copy).then_inc(s["BT_ready"], 1)
                for n in gate_tiles(u):
                    gate_tile(n)
                if u >= first_free and u - first_free < K:
                    act.wait_ge(s["acc_ready"], N_END)
                    split_hi(Q_P + 3)
                    hi_of(AT_hi, AT, u - first_free, "AT_hi_ready")
                if u >= first_free and u - first_free < H - 2:
                    act.wait_ge(s["BT_ready"], u - first_free + 1)
                    hi_of(BT_hi, BT, u - first_free, "BT_hi_ready")
            act.wait_ge(s["av_done"], UNITS)
            A(BT[:, H - 1, :], bank[6 + (H - 1) % 2][:, :], ACT.Copy).then_inc(s["BT_ready"], 1)
            act.wait_ge(s["BT_ready"], H)
            for h in range(H - 2, H):
                hi_of(BT_hi, BT, h, "BT_hi_ready")

            for f in range(K):
                split_hi(Q_P + 2 * f + 5)
                if f >= 1:
                    act.wait_ge(s["mix_ready"], f)
                    hi_of(mix_hi, mixT, f - 1, "mix_hi_ready")
            act.wait_ge(s["f_ready"], K)
            for hf in range(2):
                act.wait_ge(s["wout_loaded"], 16 * (hf + 1))
                for k in range(K):
                    hi_of(wout_hi[hf], wout_sb[hf], k, "wout_hi_ready")
                    if hf == 0 and k == 3:
                        act.wait_ge(s["mix_ready"], K)
                        hi_of(mix_hi, mixT, K - 1, "mix_hi_ready")

            act.wait_ge(s["rows_zeroed"], 16)

            def mean_square_of_x2(t):
                act.wait_ge(s["x2_ready"], T + t + 1)
                if t >= 2:
                    act.wait_ge(h2s_stored[t % 2], 16 * (t // 2))
                    act.wait_ge(s["h2T_ps"], 2 * (t - 2) + 2)
                A(h2s[t % 2], x2[:, t, :], ACT.Square, scale=float(D) ** -0.5,
                  accum_out=ms[:, t:t + 1]).then_inc(s["h2_ms"], 1)
                act.wait_ge(s["h2_ms"], t + 1)
                A(ms[:, t:t + 1], ms[:, t:t + 1], ACT.Sqrt, bias=eps[:, 0:1]).then_inc(s["h2_rs"], 1)

            def evict_h2T(t):
                act.wait_ge(s["h2_ready"], t + 1)
                act.dma_start(h2_rows[t * P:(t + 1) * P, :], h2s[t % 2]).then_inc(h2s_stored[t % 2], 16)
                for hf in range(2):
                    act.wait_ge(s["h2T_ps"], 2 * t + hf + 1)
                    A(h2T[:, 4 * hf:4 * hf + 4, t * P:(t + 1) * P],
                      bank[hf][:, :].rearrange("p (k t) -> p k t", k=4), ACT.Copy).then_inc(s["h2T_ready"], 1)

            def add_router_bias(t):
                act.wait_ge(s["lgT_ps"], t + 1)
                A(lgT[0:G + NE, t * P:(t + 1) * P], bank[0][0:G + NE, 0:P], ACT.Identity,
                  bias=brt[:, 0:1]).then_inc(s["lgT_ready"], 1)

            for t in range(T):
                mean_square_of_x2(t)
                if t >= 1:
                    add_router_bias(t - 1)
                evict_h2T(t)
            add_router_bias(T - 1)
            act.wait_ge(s["gexp_in"], 1)
            A(tg[:, :, :], tg[:, :, :], ACT.Exp).then_inc(s["gexp_out"], 1)
            act.wait_ge(s["eexp_in"], 1)
            A(wt[:, 1, :], wt[:, 1, :], ACT.Exp).then_inc(s["eexp_out"], 1)

            def store_y(row, sl, done):
                for hf in range(2):
                    act.dma_start(y_rows[bass.ds(row, SLOTS), hf * 512:(hf + 1) * 512],
                                  y_sb[sl][hf * WIDE:hf * WIDE + SLOTS, :]).then_inc(done, 16)

            def run_expert(e, sl, rounds):
                act.wait_ge(s["gu_ready"], e + 1)
                A(silu_g, bank[0][:, 0:HALF], ACT.Silu).then_inc(s["silu_ready"], 1)
                act.wait_ge(s["hidT_ps"], e + 1)
                A(hidT, bank[5][:, 0:HALF].rearrange("p (c h s) -> p c h s", c=2, h=2), ACT.Copy)\
                    .then_inc(s["hidT_ready"], 1)
                act.wait_ge(s["y_ready"], e + 1)
                act.wait_ge(y_stored[sl], rounds * 32 + 32)
                A(y_sb[sl], bank[1][:, :], ACT.Copy).then_inc(s["act_s"], 1)
                act.wait_ge(s["act_s"], e + (T + 1))
                store_y(e * SLOTS, sl, y_stored[sl])

            with act.Fori(0, E3 // 3) as r:
                for sl in range(3):
                    run_expert(r * 3 + sl, sl, r)
            for sl in range(2):
                run_expert(E3 + sl, sl, E3 // 3)

            n_more = act.value_load(own_i[0:1, MORE:MORE + 1], min_val=0, max_val=MORE)
            with act.If(n_more > 0):
                with act.Fori(0, n_more) as t:
                    act.wait_ge(s["m_gu"], t + 1)
                    A(silu_g, bank[0][:, 0:HALF], ACT.Silu).then_inc(s["m_silu"], 1)
                    act.wait_ge(s["m_hT"], t + 1)
                    A(hidT, bank[5][:, 0:HALF].rearrange("p (c h s) -> p c h s", c=2, h=2), ACT.Copy)\
                        .then_inc(s["m_hTs"], 1)
                    act.wait_ge(s["m_y"], t + 2)
                    act.wait_ge(y_stored[2], 32 * (E3 // 3 + 1))
                    act.wait_ge(s["m_st"], t * 32 + 32)
                    A(y_sb[2], bank[1][:, :], ACT.Copy).then_inc(s["act_s"], 1)
                    act.wait_ge(s["act_s"], t + (NE + T + 1))
                    store_y(t * SLOTS + FIRST_MORE, 2, s["m_st"])

            for t in range(T):
                act.wait_ge(s["out_ready"], t + 1)
                act.dma_start(outd[:, t, :], x2[:, t, :]).then_inc(s["out_stored"], 16)
            act.wait_ge(s["out_stored"], 16 * T)

        @block.vector
        def _(dve):
            V = nc.vector
            st = Steps(dve, s["dve_s"])
            V.engine_nop().then_inc(s["m_y"], 1)
            for counted in y_stored + [s["m_st"]]:
                V.engine_nop().then_inc(counted, 32)
            for t in range(T):
                dve.wait_ge(s["rs_ready"], t + 1)
                st.did(V.reciprocal(rs[:, t:t + 1], ms[:, t:t + 1]))
                st.settle()
                V.tensor_scalar(xn[:, t, :], x_sb[:, t, :], rs[:, t:t + 1], None, ALU.mult).then_inc(s["xn_ready"], 1)
            dve.wait_ge(s["small_loaded"], 16 * SMALL_DMAS)
            dve.wait_ge(s["wsm_hi_ready"], 1)
            V.tensor_tensor(wsm_lo, wsm, wsm_hi.bitcast(F32), ALU.subtract).then_inc(s["wsm_lo_ready"], 1)
            for k in range(K):
                dve.wait_ge(s["hT_hi_ready"], k + 1)
                V.scalar_tensor_tensor(hT_lo[:, k, :], bank[2 + k % 4][:, :], g1c[:, k:k + 1],
                                       hT_hi[:, k, :].bitcast(F32), ALU.mult, ALU.subtract)\
                    .then_inc(s["hT_lo_ready"], 1)

            dve.wait_ge(s["small_ready"], 1)
            V.tensor_copy(ki_raw[0:ID, :], bank[6][0:ID, :]).then_inc(s["ki_evicted"], 1)
            V.tensor_copy(gaT[0:RANK, :], bank[6][ID:ID + RANK, :])
            V.tensor_scalar(wiT[0:IH, :], bank[6][ID + 32:ID + 32 + IH, :], float(ID) ** -0.5 * float(IH) ** -0.5,
                            None, ALU.mult).then_inc(s["small_evicted"], 1)
            dve.wait_ge(s["ki_evicted"], 1)
            dve.wait_ge(s["ki_mean_ready"], 1)
            V.tensor_tensor(ki_cen[0:ID, :], ki_raw[0:ID, :], bank[7][0:ID, :], ALU.subtract)\
                .then_inc(s["ki_cen_ready"], 1)
            dve.wait_ge(s["ki_std_ready"], 1)
            st.did(V.reciprocal(ki_raw[0:ID, :], ki_raw[0:ID, :]))
            st.settle()
            dve.wait_ge(s["ki_cen_ready"], 1)
            st.did(V.scalar_tensor_tensor(kiT[0:ID, :], ki_cen[0:ID, :], lngb[:, 0:1], ki_raw[0:ID, :],
                                          ALU.mult, ALU.mult))
            st.settle()
            V.tensor_scalar(kiT[0:ID, :], kiT[0:ID, :], lngb[:, 1:2], None, ALU.add).then_inc(s["kiT_ready"], 1)
            dve.wait_ge(s["wi_ps"], 1)
            V.tensor_copy(wi[:, :, :], bank[7][:, 0:T * IH].rearrange("p (t h) -> p t h", t=T))\
                .then_inc(s["wi_ready"], 1)
            dve.wait_ge(s["wi_ready"], 1)
            u = 0
            for i in range(1, T):
                n = (i + 1) * P
                for h in range(IH):
                    dve.wait_ge(s["relu_ready"], u + 1)
                    if h == 0:
                        V.tensor_scalar(bias[i][:, :], relu[u % 2][:, 0:n], wi[:, i, 0:1], None, ALU.mult)\
                            .then_inc(s["relu_used"], 1)
                    else:
                        dve.wait_ge(s["relu_used"], u)
                        V.scalar_tensor_tensor(bias[i][:, :], relu[u % 2][:, 0:n], wi[:, i, h:h + 1],
                                               bias[i][:, :], ALU.mult, ALU.add).then_inc(s["relu_used"], 1)
                    u += 1
                dve.wait_ge(s["relu_used"], u)
                st.did(V.memset(bias[i][0:CHUNK, n - CHUNK:n], NEG))
            st.settle()

            ROUNDS = TOPK // 8
            rounds = [0]

            def topk_round():
                if rounds[0] < ROUNDS:
                    rounds[0] += 1
                    st.settle()
                    for i in range(1, T):
                        st.did(V.max(mx8[:, i, :], bias[i][:, :]))
                    st.settle()
                    for i in range(1, T):
                        st.did(V.match_replace(bias[i][:, :], mx8[:, i, :], bias[i][:, :], TAKEN))

            dve.wait_ge(s["gla_loaded"], 48)

            def gate_pre(t):
                dve.wait_ge(s["a_ready"], t + 1)
                st.did(V.tensor_scalar(g_min, bank[2][:, :], 0.0, None, ALU.min))
                st.settle()
                V.scalar_tensor_tensor(g_abs, g_min, 2.0, bank[2][:, :], ALU.mult, ALU.subtract)\
                    .then_inc(s["a_abs"], 1)

            gate_pre(0)
            for i in range(2):
                dve.wait_ge(acc_free[i], N_GV // 2)
            for t in range(T):
                dve.wait_ge(s["a_exp"], t + 1)
                st.settle()
                V.tensor_tensor(g_log, g_min, g_abs, ALU.subtract).then_inc(s["la_ready"], 1)
                topk_round()
                dve.wait_ge(s["kd_ready"], t + 1)
                V.tensor_tensor(gk[:, t, :], gk[:, t, :], g_kd, ALU.mult).then_inc(s["kdec_ready"], 1)
                if t + 1 < T:
                    dve.wait_ge(s["la_ready"], t + 1)
                    dve.wait_ge(s["ind_ready"], t + 1)
                    gate_pre(t + 1)
            while rounds[0] < ROUNDS:
                topk_round()
            st.settle()
            for i in range(1, T):
                V.tensor_scalar(bias[i][:, :], bias[i][:, :], TAKEN * 0.5, NEG, ALU.is_ge, ALU.mult)\
                    .then_inc(s["bias_ready"], 1)

            def finish_norm(j):
                dve.wait_ge(s["qk_rms_ready"], j + 1)
                st.did(V.reciprocal(rms[j % 2], rms[j % 2]))
                st.settle()
                V.tensor_tensor(qk[:, j, :], qk[:, j, :], rms[j % 2], ALU.mult).then_inc(s["qk_ready"], 1)

            def next_state(ch):
                t, c = divmod(ch, 2)
                dve.wait_ge(s["kv_ready"], ch + 1)
                dve.wait_ge(s["decay_ready"], t + 1)
                if ch >= 1:
                    dve.wait_ge(s["state_ready"], ch)
                if ch >= 2:
                    dve.wait_ge(s["o_ready"], ch - 1)
                for h in range(GH):
                    kv = bank[5 + h // 2][:, (h % 2) * DV:(h % 2 + 1) * DV]
                    if ch == 0:
                        last = V.tensor_copy(state[c][:, h, :], kv)
                    else:
                        last = V.scalar_tensor_tensor(state[c][:, h, :], state[1 - c][:, h, :],
                                                      decay[:, h, ch:ch + 1], kv, ALU.mult, ALU.add)
                last.then_inc(s["state_ready"], 1)

            for i in range(2):
                dve.wait_ge(acc_free[i], N_Q // 2)
            for j in range(2 * H):
                n = N_Q + j
                t, r = divmod(j, 4)
                dve.wait_ge(s["qk_sq_ready"], j + 1)
                V.tensor_scalar(qk[:, j, :], bank[n % 2][:, :], gqk[:, j // H:j // H + 1], None, ALU.mult)\
                    .then_inc(acc_free[n % 2], 1)
                if j > 0:
                    dve.wait_ge(acc_free[(n - 1) % 2], (n - 1) // 2 + 1)
                    finish_norm(j - 1)
                if r < 2:
                    next_state(2 * t + r)
                if r == 1:
                    for h in range(GH):
                        st.did(V.tensor_tensor(gr[:, t, h * DV:(h + 1) * DV], gr[:, t, h * DV:(h + 1) * DV],
                                               gnorm[:, :], ALU.mult))
                if r == 3:
                    dve.wait_ge(s["ors_ready"], t + 1)
                    st.did(V.reciprocal(ors[:, t, :], ors[:, t, :]))
                    st.settle()
                    for h in range(GH):
                        last = V.scalar_tensor_tensor(gr[:, t, h * DV:(h + 1) * DV],
                                                      bank[3 + h // 2][:, (h % 2) * DV:(h % 2 + 1) * DV],
                                                      ors[:, t, h:h + 1], gr[:, t, h * DV:(h + 1) * DV],
                                                      ALU.mult, ALU.mult)
                    last.then_inc(s["o_normed"], 1)
            dve.wait_ge(acc_free[(N_Q + 2 * H - 1) % 2], (N_Q + 2 * H - 1) // 2 + 1)
            finish_norm(2 * H - 1)

            dve.wait_ge(s["bias_ready"], T)
            for u in range(UNITS + 1):
                if u < UNITS:
                    i = u % T
                    n = (i + 1) * P
                    dve.wait_ge(s["logit_ready"], u + 1)
                    if u >= 3:
                        dve.wait_ge(s["pT_ready"], u - 2)
                    st.did(V.tensor_tensor_reduce(out=prob[u % 3][:, 0:n], in0=bank[2 + u % 2][:, 0:n],
                                                  in1=bias[i][:, :], scale=1.0, scalar=2.0 * NEG, op0=ALU.add,
                                                  op1=ALU.max, accum_out=mxl[:, u:u + 1]))
                    st.settle()
                    V.tensor_scalar(nmx[:, u:u + 1], mxl[:, u:u + 1], -float(HD) ** -0.5, None, ALU.mult)\
                        .then_inc(s["lmax_ready"], 1)
                if u >= 1:
                    v = u - 1
                    n = (v % T + 1) * P
                    dve.wait_ge(s["prob_ready"], v + 1)
                    st.did(V.reciprocal(prc[:, v:v + 1], psm[:, v:v + 1]))
                    st.settle()
                    V.tensor_scalar(prob[v % 3][:, 0:n], prob[v % 3][:, 0:n], prc[:, v:v + 1], None, ALU.mult)\
                        .then_inc(s["probn_ready"], 1)

            def sigmoid(f):
                for g in range(2):
                    st.did(V.tensor_scalar(gates[g][:, f, :], gates[g][:, f, :], 1.0, None, ALU.add))
                    st.settle()
                    st.did(V.reciprocal(gates[g][:, f, :], gates[g][:, f, :]))

            def mix_lo_of(f):
                dve.wait_ge(s["mix_hi_ready"], f + 1)
                V.tensor_tensor(mix_lo[:, f, :], mixT[:, f, :], mix_hi[:, f, :].bitcast(F32), ALU.subtract)\
                    .then_inc(s["mix_lo_ready"], 1)

            for i in range(2):
                dve.wait_ge(acc_free[i], N_END // 2)
                dve.wait_ge(s["av_done"], UNITS)
                V.engine_nop().then_inc(s["f_free"], 1)
            sigmoid(0)
            for f in range(K):
                b0 = 2 * (f % 2)
                dve.wait_ge(s["f_ready"], f + 1)
                st.settle()
                st.did(V.tensor_tensor(gates[0][:, f, :], bank[b0][:, :], gates[0][:, f, :], ALU.mult))
                V.tensor_tensor(mtmp[f % 2], bank[b0 + 1][:, :], gates[1][:, f, :], ALU.mult)\
                    .then_inc(s["f_free"], 1)
                st.settle()
                dve.wait_ge(s["f_free"], f + 3)
                V.tensor_tensor(mixT[:, f, :], mixT[:, f, :], mtmp[f % 2], ALU.add).then_inc(s["mix_ready"], 1)
                if f + 1 < K:
                    sigmoid(f + 1)
                if f >= 1:
                    mix_lo_of(f - 1)
            mix_lo_of(K - 1)
            for k in range(K):
                dve.wait_ge(s["wout_hi_ready"], k + 1)
                V.tensor_tensor(wout_lo[0][:, k, :], wout_sb[0][:, k, :], wout_hi[0][:, k, :].bitcast(F32),
                                ALU.subtract).then_inc(wout_lo_ready[0], 1)

            dve.wait_ge(s["x_again"], 16)
            dve.wait_ge(s["g2_loaded"], 16)
            dve.wait_ge(s["rows_zeroed"], 16)

            def add(n):
                hf, t = divmod(n, T)
                dve.wait_ge(s["x_out_ready"], n + 1)
                V.tensor_tensor(x2[:, t, hf * BLK:(hf + 1) * BLK], bank[4 + n % 4][:, :],
                                x2[:, t, hf * BLK:(hf + 1) * BLK], ALU.add).then_inc(s["x2_ready"], 1)

            def normalise(t):
                dve.wait_ge(s["h2_rs"], t + 1)
                st.did(V.reciprocal(rs[:, t:t + 1], ms[:, t:t + 1]))
                st.settle()
                dve.wait_ge(s["x2_ready"], T + t + 1)
                V.scalar_tensor_tensor(h2s[t % 2], x2[:, t, :], rs[:, t:t + 1], g2b, ALU.mult, ALU.mult)\
                    .then_inc(s["h2_ready"], 1)

            def choose(t):
                logits_ = bank[3][:, 0:G + NE]
                dve.wait_ge(s["lg_ps"], t + 1)
                st.did(V.tensor_copy(lg[:, t, 0:G], logits_[:, 0:G]))
                st.did(V.tensor_copy(le[:, t, :], logits_[:, G:G + NE]))
                st.settle()
                st.did(V.max(v8[:, t, :], lg[:, t, :]))
                st.settle()
                st.did(V.max_index(i8[:, t, :], v8[:, t, :], lg[:, t, :]))
                st.did(V.tensor_scalar(tg[:, t, :], lg[:, t, 0:G], v8[:, t, 0:1], None, ALU.subtract))
                st.settle()
                st.did(V.tensor_copy(gid[:, t:t + 1], i8[:, t, 0:1]))
                st.settle()
                st.did(V.tensor_scalar(pen[:, 0, :], gio[:, :], gid[:, t:t + 1], NEG, ALU.not_equal, ALU.mult))
                st.settle()
                st.did(V.tensor_tensor(le[:, t, :], le[:, t, :], pen[:, 0, :], ALU.add))
                st.settle()
                st.did(V.max(v8[:, t, :], le[:, t, :]))
                st.settle()
                st.did(V.max_index(i8[:, t, :], v8[:, t, :], le[:, t, :]))
                st.settle()
                st.did(V.tensor_copy(eid[:, :, t], i8[:, t, 0:TOP_E]))
                st.settle()
                for k in range(TOP_E):
                    st.did(V.tensor_scalar(oh[:, k, t, :], eio[:, :], eid[:, k, t:t + 1], None, ALU.is_equal))
                st.settle()
                V.tensor_tensor(mask_b[:, t, :], oh[:, 0, t, :], oh[:, 1, t, :], ALU.add)\
                    .then_inc(s["maskb_ready"], 1)
                st.did(V.tensor_tensor(wt[:, 1, t:t + 1], v8[:, t, 1:2], v8[:, t, 0:1], ALU.subtract))

            def place(t):
                dve.wait_ge(s["rank_ready"], t + 1)
                for k in range(TOP_E):
                    st.did(V.tensor_tensor_reduce(out=pen[:, k, :], in0=bank[2][:, t * NE:(t + 1) * NE],
                                                  in1=oh[:, k, t, :], scale=1.0, scalar=0.0, op0=ALU.mult, op1=ALU.add,
                                                  accum_out=rk[:, k, t:t + 1]))
                st.settle()
                st.did(V.scalar_tensor_tensor(tabf[:, :, t], rk[:, :, t], float(NE), eid[:, :, t], ALU.mult, ALU.add))
                st.settle()
                V.tensor_copy(tab_i[:, :, t], tabf[:, :, t]).then_inc(s["tab_ready"], 1)

            st.did(V.memset(lg[:, :, :], NEG))
            for n in range(T):
                add(n)
            for t in range(T):
                add(T + t)
                normalise(t)
                if t >= 2:
                    choose(t - 2)
                if t >= 3:
                    place(t - 3)
            choose(T - 2)
            place(T - 3)
            choose(T - 1)
            place(T - 2)
            place(T - 1)

            st.settle()
            V.engine_nop().then_inc(s["gexp_in"], 1)
            V.engine_nop().then_inc(s["eexp_in"], 1)
            dve.wait_ge(s["counts_ready"], 1)
            st.did(V.tensor_copy(cnt, bank[3][:, 0:NE]))
            st.settle()
            st.did(V.tensor_scalar(more, cnt, float(SLOTS), None, ALU.is_gt))
            for m in range(2, MAX_TILES):
                st.settle()
                st.did(V.scalar_tensor_tensor(more, cnt, float(SLOTS * m), more, ALU.is_gt, ALU.add))
            st.did(V.memset(mbase, 1.0))
            st.settle()
            st.did(V.tensor_tensor_scan(xinc, mbase, more, 0.0, ALU.mult, ALU.add))
            st.settle()
            st.did(V.tensor_tensor(more, xinc, more, ALU.subtract))
            st.did(V.tensor_tensor(own[:, :, :], xinc.unsqueeze(1).to_broadcast([P, MORE, NE]),
                                   tio[:, :].unsqueeze(2).to_broadcast([P, MORE, NE]), ALU.is_le))
            st.did(V.tensor_copy(ownf[:, MORE:MORE + 1], xinc[:, NE - 1:NE]))
            st.settle()
            st.did(V.tensor_scalar(mbase, more, float(SLOTS), float(FIRST_MORE - SLOTS), ALU.mult, ALU.add))
            st.did(V.reduce_sum(ownf[:, 0:MORE], own[:, :, :], AX))
            st.settle()
            st.did(V.tensor_scalar(ownf[:, 0:MORE], ownf[:, 0:MORE], float(NE - 1), None, ALU.min))
            st.settle()
            V.tensor_copy(own_i[:, :], ownf[:, :]).then_inc(s["own_ready"], 1)
            for k in range(TOP_E):
                st.did(V.tensor_tensor(base_of[:, :, :], oh[:, k], mbase.unsqueeze(1).to_broadcast([P, T, NE]),
                                       ALU.mult))
                st.settle()
                st.did(V.reduce_sum(rtmp[:, k, :], base_of[:, :, :], AX))
                st.settle()
            st.did(V.tensor_scalar(isov[:, :, :], rk[:, :, :], float(SLOTS), None, ALU.is_ge))
            st.did(V.scalar_tensor_tensor(rowf[:, :, :], eid[:, :, :], float(SLOTS), rk[:, :, :], ALU.mult, ALU.add))
            st.did(V.tensor_tensor(rtmp[:, :, :], rtmp[:, :, :], rk[:, :, :], ALU.add))
            st.settle()
            st.did(V.tensor_tensor(oh[:, :, :, 0], rtmp[:, :, :], rowf[:, :, :], ALU.subtract))
            st.did(V.scalar_tensor_tensor(tabf[:, :, :], rtmp[:, :, :], -float(ROWS), isov[:, :, :], ALU.add, ALU.mult))
            st.settle()
            st.did(V.tensor_tensor(oh[:, :, :, 0], oh[:, :, :, 0], isov[:, :, :], ALU.mult))
            st.did(V.tensor_scalar(tabf[:, :, :], tabf[:, :, :], float(ROWS), None, ALU.add))
            st.settle()
            st.did(V.tensor_tensor(rowf[:, :, :], rowf[:, :, :], oh[:, :, :, 0], ALU.add))
            st.did(V.tensor_copy(tab_more[:, :, :], tabf[:, :, :]))
            st.settle()
            V.tensor_copy(row_i[:, :, :], rowf[:, :, :]).then_inc(s["rows_ready"], 1)
            dve.wait_ge(s["gexp_out"], 1)
            st.did(V.reduce_sum(gw[:, :], tg[:, :, :], AX))
            dve.wait_ge(s["eexp_out"], 1)
            st.did(V.tensor_scalar(wt[:, 0, :], wt[:, 1, :], 1.0, None, ALU.add))
            st.settle()
            st.did(V.tensor_tensor(gw[:, :], gw[:, :], wt[:, 0, :], ALU.mult))
            st.settle()
            st.did(V.reciprocal(wt[:, 0, :], gw[:, :]))
            st.settle()
            st.did(V.tensor_tensor(wt[:, 1, :], wt[:, 1, :], wt[:, 0, :], ALU.mult))
            st.settle()

            def evict_gathered(sl, done):
                V.tensor_copy(hTe[sl], bank[4][:, :].rearrange("p (k s) -> p k s", k=K)).then_inc(done, 1)

            def run_expert(e, sl, has_next=True):
                dve.wait_ge(s["silu_ready"], e + 1)
                V.tensor_tensor(hid, silu_g, bank[0][:, HALF:F], ALU.mult).then_inc(s["hid_ready"], 1)
                if has_next:
                    dve.wait_ge(s["xg_T"], e + 2)
                    evict_gathered((sl + 1) % 3, s["he_ready"])

            dve.wait_ge(s["xg_T"], 1)
            evict_gathered(0, s["he_ready"])
            with dve.Fori(0, E3 // 3) as r:
                for sl in range(3):
                    run_expert(r * 3 + sl, sl)
            for sl in range(2):
                run_expert(E3 + sl, sl, has_next=(sl == 0))
            dve.wait_ge(s["own_ready"], 1)
            n_more = dve.value_load(own_i[0:1, MORE:MORE + 1], min_val=0, max_val=MORE)
            with dve.If(n_more > 0):
                with dve.Fori(0, n_more) as t:
                    dve.wait_ge(s["m_T"], t + 1)
                    for hf in range(2):
                        last = V.tensor_copy(hTe[2][:, 4 * hf:4 * hf + 4, :],
                                             bank[3 + hf][:, :].rearrange("p (k s) -> p k s", k=4)[:, :, 0:WIDE])
                    last.then_inc(s["m_he"], 1)
                    dve.wait_ge(s["m_silu"], t + 1)
                    V.tensor_tensor(hid, silu_g, bank[0][:, HALF:F], ALU.mult).then_inc(s["m_hid"], 1)

            for t in range(T):
                dve.wait_ge(yg_loaded[t], 16 * TOP_E)
                for k in range(TOP_E):
                    last = V.scalar_tensor_tensor(x2[:, t, :], yg[TOP_E * t + k], wt[:, k, t:t + 1], x2[:, t, :],
                                                  ALU.mult, ALU.add)
                    if k < TOP_E - 1:
                        st.did(last)
                        st.settle()
                last.then_inc(s["out_ready"], 1)

        @block.gpsimd
        def _(pool):
            Q = nc.gpsimd
            st = Steps(pool, s["pool_s"])

            def step(instruction):
                st.did(instruction)
                st.settle()

            Q.memset(eps[:, :], EPS).then_inc(s["eps_ready"], 1)
            step(Q.memset(gaT[:, :], 1.0))
            Q.memset(wsm[:, :, :], 0.0).then_inc(s["wsm_zeroed"], 1)
            pool.wait_ge(s["wsm_zeroed"], 1)
            def ones_where(tile, value, *selects):
                step(Q.memset(tile, value))
                for base, cm, pattern in selects:
                    step(Q.affine_select(out=tile, in_=tile, compare_op=ALU.is_ge, fill=0.0, base=base,
                                           pattern=pattern, channel_multiplier=cm))

            ones_where(ident[:, :], 1.0, (0, 1, [[-1, P]]), (0, -1, [[1, P]]))
            ones_where(mean_m[:, :], 1.0 / HD)
            ones_where(mean_i[:, :], 1.0 / ID)
            ones_where(one[:, :], 1.0)
            ones_where(ones_b[:, :], 1.0)
            ones_where(before[:, :], 1.0, (-1, -1, [[1, P]]))
            inv = 1.0 / GATE_TEMP
            ones_where(suffix[:, :], inv, (-1, 1, [[-1, P]]))
            step(Q.memset(suffix[CHUNK:P, 0:CHUNK], 0.0))
            ones_where(chunk_of[:, 0:1], inv, (CHUNK - 1, -1, [[0, 1]]))
            ones_where(chunk_of[:, 1:2], inv, (-CHUNK, 1, [[0, 1]]))
            step(Q.memset(no_token[:, :], S))
            step(Q.memset(bias0[:, :], 0.0))
            Q.memset(bias0[0:CHUNK, CHUNK:P], NEG).then_inc(s["bias_ready"], 1)
            step(Q.iota(tokid[:, :], pattern=[[P, T]], base=0, channel_multiplier=1))
            step(Q.iota(eio[:, :], pattern=[[1, NE]], base=0, channel_multiplier=0,
                          allow_small_or_imprecise_dtypes=True))
            step(Q.iota(gio[:, :].rearrange("p (g e) -> p g e", g=G), pattern=[[1, G], [0, EPG]], base=0,
                          channel_multiplier=0, allow_small_or_imprecise_dtypes=True))
            step(Q.iota(tio[:, :], pattern=[[1, MORE]], base=0, channel_multiplier=0,
                          allow_small_or_imprecise_dtypes=True))
            pool.engine_nop().then_inc(s["consts_done"], 1)

            def split_lo(first, end):
                for q in range(first, end):
                    pool.wait_ge(s["whi_ready"], q + 1)
                    Q.tensor_tensor(quarter(w_lo, q), quarter(w_raw, q), quarter(w_hi, q).bitcast(F32),
                                    ALU.subtract).then_inc(s["wlo_ready"], 1)

            tab = row_token.rearrange("(p n) a -> p (n a)", p=SLOTS)
            pool.dma_start(tab, no_token[0:SLOTS, :]).then_inc(s["table_zero"], 16)
            with nc.allow_non_contiguous_dma(reason="the routers' columns"):
                pool.dma_start(wr[:, :, G:G + NE], w_router_expert[0].rearrange("(k p) n -> p k n", p=P))\
                    .then_inc(s["wr_loaded"], 16)
            pool.wait_ge(s["xn_ready"], T)
            pool.dma_start(wa2[0:RANK, :], gla_w_a2[0]).then_inc(s["gla_loaded"], 16)
            pool.dma_start(wa2[RANK:RANK + 1, :], gla_b_a).then_inc(s["gla_loaded"], 16)
            pool.dma_start(gnorm[:, :], gla_norm_g[0].partition_broadcast(P)).then_inc(s["gla_loaded"], 16)
            split_lo(0, N_SA)
            pool.wait_ge(s["o_normed"], T)
            step(Q.memset(zrow, 0.0))
            zp = (ROWS - FIRST_MORE) // 8
            pool.dma_start(y_rows[FIRST_MORE:ROWS].rearrange("(p r) d -> p r d", r=8),
                           zrow[0:zp].unsqueeze(1).to_broadcast([zp, 8, D])).then_inc(s["rows_zeroed"], 16)
            split_lo(N_SA, Q_P + 4)
            for src, lo, hi, which in ((AT, AT_lo, AT_hi, "AT"), (BT, BT_lo, BT_hi, "BT")):
                for k in range(K):
                    pool.wait_ge(s[which + "_hi_ready"], k + 1)
                    Q.tensor_tensor(lo[:, k, :], src[:, k, :], hi[:, k, :].bitcast(F32), ALU.subtract)\
                        .then_inc(s[which + "_lo_ready"], 1)
            pool.wait_ge(s["av_done"], UNITS)
            pool.dma_start(g2b, norm2_g[0].partition_broadcast(P)).then_inc(s["g2_loaded"], 16)
            split_lo(Q_P + 4, Q_END)
            for k in range(K):
                pool.wait_ge(s["wout_hi_ready"], K + k + 1)
                Q.tensor_tensor(wout_lo[1][:, k, :], wout_sb[1][:, k, :], wout_hi[1][:, k, :].bitcast(F32),
                                ALU.subtract).then_inc(wout_lo_ready[1], 1)

            pool.wait_ge(s["table_zero"], 16)

            def scatter(entries, k, t, end, done):
                pool.indirect_dma_start(
                    out=row_token, out_offset=bass.IndirectOffsetOnAxis(ap=entries[:, k, t:t + 1], axis=0),
                    in_=tokid[:, t:t + 1], in_offset=None, bounds_check=end - 1, oob_is_err=False)\
                    .then_inc(done, 16)

            for t in range(T):
                pool.wait_ge(s["tab_ready"], t + 1)
                for k in range(TOP_E):
                    scatter(tab_i, k, t, FIRST_MORE, s["scattered"])
            pool.wait_ge(s["scattered"], 16 * TOP_E * T)
            pool.dma_start(idx_all[:, :], row_token[0:FIRST_MORE].rearrange("(r e) a -> r (e a)", e=NE))\
                .then_inc(s["idx_loaded"], 16)
            pool.wait_ge(s["idx_loaded"], 16)
            for i in range(2):
                pool.wait_ge(h2s_stored[i], 16 * (T // 2))

            def gather(sl, tokens, done):
                pool.indirect_dma_start(
                    out=xg[sl][0:SLOTS, :], out_offset=None, in_=h2_rows,
                    in_offset=bass.IndirectOffsetOnAxis(ap=tokens, axis=0),
                    bounds_check=S - 1, oob_is_err=False).then_inc(done, 16)

            pool.wait_ge(s["lgT_ready"], T)
            for e in range(NE):
                if e >= 3:
                    pool.wait_ge(s["xg_T"], e - 2)
                gather(e % 3, idx_all[:, e:e + 1], xg_loaded[e % 3])
            pool.wait_ge(s["own_ready"], 1)
            n_more = pool.value_load(own_i[0:1, MORE:MORE + 1], min_val=0, max_val=MORE)
            with pool.If(n_more > 0):
                pool.wait_ge(s["xg_T"], NE)
                pool.wait_ge(s["rows_ready"], 1)
                for t in range(T):
                    for k in range(TOP_E):
                        scatter(tab_more, k, t, ROWS, s["scattered_more"])
                pool.wait_ge(s["scattered_more"], 16 * TOP_E * T)
                for t in range(MORE):
                    with pool.If(n_more > t):
                        if t >= 1:
                            pool.wait_ge(s["m_T"], t)
                        pool.dma_start(idx_more[:, :], row_token[FIRST_MORE + t * SLOTS:FIRST_MORE + (t + 1) * SLOTS, :])\
                            .then_inc(s["m_idx"], 16)
                        pool.wait_ge(s["m_idx"], 16 * (t + 1))
                        gather(0, idx_more[:, :], s["m_xg"])
                pool.wait_ge(s["m_st"], n_more * 32 + 32)
            for sl in range(3):
                pool.wait_ge(y_stored[sl], 32 * (1 + E3 // 3 + (1 if sl < NE % 3 else 0)))
            pool.wait_ge(s["rows_ready"], 1)
            for t in range(T):
                for k in range(TOP_E):
                    pool.indirect_dma_start(
                        out=yg[TOP_E * t + k], out_offset=None, in_=y_rows,
                        in_offset=bass.IndirectOffsetOnAxis(ap=row_i[:, k, t:t + 1], axis=0),
                        bounds_check=ROWS - 1, oob_is_err=False).then_inc(yg_loaded[t], 16)


_NAMES = ['x', 'norm1_g', 'w_in', 'gla_w_a2', 'gla_b_a', 'gla_norm_g', 'dsa_q_norm_g', 'dsa_k_norm_g',
          'idx_k_ln_g', 'idx_k_ln_b', 'w_branch_gla', 'w_branch_dsa', 'w_out', 'norm2_g',
          'w_router_group', 'b_router_group', 'w_router_expert', 'b_router_expert',
          'w_exp_gate', 'w_exp_up', 'w_exp_down']


def kernel(**inputs):
    import concourse.bacc as bacc
    from concourse.bass_utils import run_bass_kernel_spmd

    nc = bacc.Bacc("TRN2", target_bir_lowering=False, num_devices=1)
    arrays, args = {}, []
    for name in _NAMES:
        a = np.ascontiguousarray(inputs[name])
        arrays[name + "_in"] = a
        args.append(nc.dram_tensor(name + "_in", a.shape, mybir.dt.from_np(a.dtype), kind="ExternalInput").ap())
    shape = arrays["x_in"].shape
    args.append(nc.dram_tensor("out_rows", shape, F32, kind="ExternalOutput").ap())
    encoder_block(nc, *args)
    r = run_bass_kernel_spmd(nc, [arrays], core_ids=[0])
    return r.results[0]["out_rows"]
```
